# Optimizing a Trainium2 kernel written in Bass

```python
import jax, jax.numpy as jnp
from jax import lax
import numpy as np

D_MODEL = 1024
BATCH = 1
SEQ = 512
DEPTH = 1
DEC_BATCH = 8
DEC_SEQ = 4
PAST_LEN = 2048
PAGE_SIZE = 128

N_META = 16
MIX_WIDTH = D_MODEL
ATT_DIM = 64
ATT_WIDTH = MIX_WIDTH // 2
ATT_HEADS = ATT_WIDTH // ATT_DIM
IDX_HEADS = 8
IDX_DIM = 64
TOPK_MAX = 256
RET_DK = 128
RET_DV = 128
RET_WIDTH = MIX_WIDTH - ATT_WIDTH
RET_HEADS = RET_WIDTH // RET_DV
CHUNK = 128
Q_BLOCK = 128
D_FF = 2816
ROPE_BASE = 10000.0
LN_EPS = 1e-5
GN_EPS = 1e-5
ALPHA = (2.0 * DEPTH) ** 0.25
BETA = (8.0 * DEPTH) ** -0.25
IN_SPLITS = (ATT_WIDTH, ATT_WIDTH, ATT_WIDTH, IDX_HEADS * IDX_DIM, IDX_DIM, IDX_HEADS,
             RET_HEADS * RET_DK, RET_HEADS * RET_DK, RET_WIDTH, RET_WIDTH)
IN_COLS = sum(IN_SPLITS)

kernel_name = "hymba_dsa_retention_macaron_step"

def _layernorm(x, g, b):
    xf = x.astype(jnp.float32)
    mu = jnp.mean(xf, axis=-1, keepdims=True)
    var = jnp.mean(jnp.square(xf - mu), axis=-1, keepdims=True)
    return ((xf - mu) * lax.rsqrt(var + LN_EPS) * g.astype(jnp.float32) + b.astype(jnp.float32)).astype(x.dtype)

def _swiglu(x, wg, wu, wd):
    return (jax.nn.silu(x @ wg) * (x @ wu)) @ wd

def _rope(x, pos):
    half = x.shape[-1] // 2
    inv = ROPE_BASE ** (-jnp.arange(half, dtype=jnp.float32) / half)
    ang = pos.astype(jnp.float32)[:, None] * inv[None, :]
    cos = jnp.cos(ang)[None, :, None, :]
    sin = jnp.sin(ang)[None, :, None, :]
    xf = x.astype(jnp.float32)
    x1, x2 = xf[..., :half], xf[..., half:]
    return jnp.concatenate([x1 * cos - x2 * sin, x1 * sin + x2 * cos], axis=-1)

def _log_gamma():
    return jnp.log(1.0 - 2.0 ** (-5.0 - jnp.arange(RET_HEADS, dtype=jnp.float32)))

def _project(h, w_in, pos):
    B, T, _ = h.shape
    z = h @ w_in
    offs = np.cumsum(IN_SPLITS)[:-1].tolist()
    q, k, v, qi, ki, wi, rq, rk, rv, g = jnp.split(z, offs, axis=-1)
    q = q.reshape(B, T, ATT_HEADS, ATT_DIM)
    k = k.reshape(B, T, ATT_HEADS, ATT_DIM)
    v = v.reshape(B, T, ATT_HEADS, ATT_DIM)
    qi = qi.reshape(B, T, IDX_HEADS, IDX_DIM)
    rq = _rope(rq.reshape(B, T, RET_HEADS, RET_DK), pos)
    rk = _rope(rk.reshape(B, T, RET_HEADS, RET_DK), pos) * (RET_DK ** -0.5)
    rv = rv.reshape(B, T, RET_HEADS, RET_DV).astype(jnp.float32)
    return q, k, v, qi, ki, wi, rq, rk, rv, g

def _indexer_topk(qi, wi, q_pos, ki, topk):
    L = ki.shape[1]
    s = jnp.einsum('bqhd,bld->bqhl', qi, ki).astype(jnp.float32) * (IDX_DIM ** -0.5)
    score = jnp.einsum('bqhl,bqh->bql', jax.nn.relu(s), wi.astype(jnp.float32)) * (IDX_HEADS ** -0.5)
    visible = jnp.arange(L, dtype=jnp.int32)[None, None, :] <= q_pos[None, :, None]
    score = jnp.where(visible, score, -jnp.inf)
    _, idx = lax.top_k(score, topk)
    valid = idx <= q_pos[None, :, None]
    return idx, valid

def _sparse_attend(q, ks, vs, valid):
    logits = jnp.einsum('bqhd,bqkhd->bqhk', q, ks).astype(jnp.float32) * (ATT_DIM ** -0.5)
    logits = jnp.where(valid[:, :, None, :], logits, -jnp.inf)
    p = jax.nn.softmax(logits, axis=-1).astype(vs.dtype)
    return jnp.einsum('bqhk,bqkhd->bqhd', p, vs)

def _retention_chunk(q, k, v, s_prev, lg):
    L = q.shape[1]
    n = jnp.arange(L, dtype=jnp.float32)
    diff = n[:, None] - n[None, :]
    decay = jnp.where(diff[None] >= 0, jnp.exp(jnp.maximum(diff, 0.0)[None] * lg[:, None, None]), 0.0)
    inner = jnp.einsum('bnhd,bmhd->bhnm', q, k) * decay[None]
    intra = jnp.einsum('bhnm,bmhe->bnhe', inner, v)
    xi = jnp.exp((n[:, None] + 1.0) * lg[None, :])
    sp = s_prev.astype(jnp.float32)
    cross = jnp.einsum('bnhd,bhde->bnhe', q, sp) * xi[None, :, :, None]
    zeta = jnp.exp((L - 1.0 - n)[:, None] * lg[None, :])
    s_new = jnp.exp(L * lg)[None, :, None, None] * sp + jnp.einsum('bmhd,bmhe->bhde', k * zeta[None, :, :, None], v)
    return intra + cross, s_new

def _mixer_out(att, ret, g, w_out):
    B, T = att.shape[:2]
    mu = jnp.mean(ret, axis=-1, keepdims=True)
    var = jnp.mean(jnp.square(ret - mu), axis=-1, keepdims=True)
    retn = ((ret - mu) * lax.rsqrt(var + GN_EPS)).reshape(B, T, RET_WIDTH).astype(g.dtype)
    y = jnp.concatenate([att.reshape(B, T, ATT_WIDTH), jax.nn.silu(g) * retn], axis=-1)
    return y @ w_out

def _prompt_mixer(h, w_in, w_out):
    B, T, _ = h.shape
    pos = jnp.arange(T, dtype=jnp.int32)
    q, k, v, qi, ki, wi, rq, rk, rv, g = _project(h, w_in, pos)
    topk = min(TOPK_MAX, SEQ // 4)
    bidx = jnp.arange(B)[:, None, None]

    def attend(qb, qib, wb, posb):
        idx, valid = _indexer_topk(qib, wb, posb, ki, topk)
        return _sparse_attend(qb, k[bidx, idx], v[bidx, idx], valid)

    att_meta = attend(q[:, :N_META], qi[:, :N_META], wi[:, :N_META], pos[:N_META])
    nb = SEQ // Q_BLOCK
    blk = lambda a: jnp.moveaxis(a[:, N_META:].reshape((B, nb, Q_BLOCK) + a.shape[2:]), 1, 0)
    att_real = lax.map(lambda xs: attend(*xs), (blk(q), blk(qi), blk(wi), pos[N_META:].reshape(nb, Q_BLOCK)))
    att_real = jnp.moveaxis(att_real, 0, 1).reshape(B, SEQ, ATT_HEADS, ATT_DIM)
    att = jnp.concatenate([att_meta, att_real], axis=1)

    lg = _log_gamma()
    s0 = jnp.zeros((B, RET_HEADS, RET_DK, RET_DV), jnp.float32)
    ret_meta, s = _retention_chunk(rq[:, :N_META], rk[:, :N_META], rv[:, :N_META], s0, lg)
    nc = SEQ // CHUNK
    chk = lambda a: jnp.moveaxis(a[:, N_META:].reshape((B, nc, CHUNK) + a.shape[2:]), 1, 0)

    def step(carry, xs):
        qc, kc, vc = xs
        o, carry = _retention_chunk(qc, kc, vc, carry, lg)
        return carry, o

    s_fin, ret_real = lax.scan(step, s, (chk(rq), chk(rk), chk(rv)))
    ret_real = jnp.moveaxis(ret_real, 0, 1).reshape(B, SEQ, RET_HEADS, RET_DV)
    ret = jnp.concatenate([ret_meta, ret_real], axis=1)
    out = _mixer_out(att, ret, g, w_out)
    return out, (k, v, ki, s_fin.astype(h.dtype))

def _sample_mixer(h, cache_k, cache_v, cache_idx_k, state_ret, page_table, layer, w_in, w_out):
    B = h.shape[0]
    n_pages = PAST_LEN // PAGE_SIZE
    pos = PAST_LEN + jnp.arange(DEC_SEQ, dtype=jnp.int32)
    q, k, v, qi, ki, wi, rq, rk, rv, g = _project(h, w_in, pos)
    ki_past = cache_idx_k[layer, page_table].reshape(B, PAST_LEN, IDX_DIM).astype(ki.dtype)
    ki_all = jnp.concatenate([ki_past, ki], axis=1)
    topk = min(TOPK_MAX, (PAST_LEN + DEC_SEQ) // 4)
    idx, valid = _indexer_topk(qi, wi, pos, ki_all, topk)
    bidx = jnp.arange(B)[:, None, None]
    in_past = idx < PAST_LEN
    phys = page_table[bidx, jnp.minimum(idx // PAGE_SIZE, n_pages - 1)]
    off = idx % PAGE_SIZE
    new_i = jnp.clip(idx - PAST_LEN, 0, DEC_SEQ - 1)

    def sel(cache, new):
        return jnp.where(in_past[..., None, None], cache[layer, phys, off].astype(new.dtype), new[bidx, new_i])

    att = _sparse_attend(q, sel(cache_k, k), sel(cache_v, v), valid)
    ret, s_new = _retention_chunk(rq, rk, rv, state_ret[layer], _log_gamma())
    out = _mixer_out(att, ret, g, w_out)
    return out, (k, v, ki, s_new.astype(state_ret.dtype))

def _macaron_layer(x, mixer, f1g, f1u, f1d, ln1g, ln1b, ln2g, ln2b, f2g, f2u, f2d, ln3g, ln3b):
    x = _layernorm(ALPHA * x + 0.5 * _swiglu(x, f1g, f1u, f1d), ln1g, ln1b)
    m, st = mixer(x)
    x = _layernorm(ALPHA * x + m, ln2g, ln2b)
    x = _layernorm(ALPHA * x + 0.5 * _swiglu(x, f2g, f2u, f2d), ln3g, ln3b)
    return x, st

def setup_inputs(seed: int = 0) -> dict:
    key = jax.random.key(seed)
    ks = jax.random.split(key, 24)
    f32 = jnp.float32
    n_pages = PAST_LEN // PAGE_SIZE
    n_used = DEC_BATCH * n_pages
    n_pool = n_used + max(1, n_used // 4)

    def nrm(k, shape, scale):
        return jax.random.normal(k, shape, f32) * scale

    page_table = jax.random.permutation(ks[6], n_pool)[:n_used].reshape(DEC_BATCH, n_pages).astype(jnp.int32)
    return {
        "x_prompt": nrm(ks[0], (BATCH, SEQ, D_MODEL), 1.0),
        "x_sample": nrm(ks[1], (DEC_BATCH, DEC_SEQ, D_MODEL), 1.0),
        "cache_k": nrm(ks[2], (DEPTH, n_pool, PAGE_SIZE, ATT_HEADS, ATT_DIM), 1.0),
        "cache_v": nrm(ks[3], (DEPTH, n_pool, PAGE_SIZE, ATT_HEADS, ATT_DIM), 1.0),
        "cache_idx_k": nrm(ks[4], (DEPTH, n_pool, PAGE_SIZE, IDX_DIM), 1.0),
        "state_ret": nrm(ks[5], (DEPTH, DEC_BATCH, RET_HEADS, RET_DK, RET_DV), 0.5),
        "page_table": page_table,
        "meta_tokens": nrm(ks[7], (N_META, D_MODEL), 1.0),
        "ffn1_w_gate": nrm(ks[8], (DEPTH, D_MODEL, D_FF), D_MODEL ** -0.5),
        "ffn1_w_up": nrm(ks[9], (DEPTH, D_MODEL, D_FF), D_MODEL ** -0.5),
        "ffn1_w_down": nrm(ks[10], (DEPTH, D_FF, D_MODEL), BETA * D_FF ** -0.5),
        "ln1_g": 1.0 + nrm(ks[11], (DEPTH, D_MODEL), 0.02),
        "ln1_b": nrm(ks[12], (DEPTH, D_MODEL), 0.02),
        "w_in": nrm(ks[13], (DEPTH, D_MODEL, IN_COLS), D_MODEL ** -0.5),
        "w_out": nrm(ks[14], (DEPTH, MIX_WIDTH, D_MODEL), BETA * MIX_WIDTH ** -0.5),
        "ln2_g": 1.0 + nrm(ks[15], (DEPTH, D_MODEL), 0.02),
        "ln2_b": nrm(ks[16], (DEPTH, D_MODEL), 0.02),
        "ffn2_w_gate": nrm(ks[17], (DEPTH, D_MODEL, D_FF), D_MODEL ** -0.5),
        "ffn2_w_up": nrm(ks[18], (DEPTH, D_MODEL, D_FF), D_MODEL ** -0.5),
        "ffn2_w_down": nrm(ks[19], (DEPTH, D_FF, D_MODEL), BETA * D_FF ** -0.5),
        "ln3_g": 1.0 + nrm(ks[20], (DEPTH, D_MODEL), 0.02),
        "ln3_b": nrm(ks[21], (DEPTH, D_MODEL), 0.02),
    }

def reference(x_prompt, x_sample, cache_k, cache_v, cache_idx_k, state_ret, page_table, meta_tokens,
              ffn1_w_gate, ffn1_w_up, ffn1_w_down, ln1_g, ln1_b, w_in, w_out, ln2_g, ln2_b,
              ffn2_w_gate, ffn2_w_up, ffn2_w_down, ln3_g, ln3_b):
    meta = jnp.broadcast_to(meta_tokens[None].astype(x_prompt.dtype), (x_prompt.shape[0], N_META, D_MODEL))
    xp = jnp.concatenate([meta, x_prompt], axis=1)
    xs = x_sample
    new_p, new_s = [], []
    for l in range(DEPTH):
        lw = (ffn1_w_gate[l], ffn1_w_up[l], ffn1_w_down[l], ln1_g[l], ln1_b[l], ln2_g[l], ln2_b[l],
              ffn2_w_gate[l], ffn2_w_up[l], ffn2_w_down[l], ln3_g[l], ln3_b[l])
        xp, stp = _macaron_layer(xp, lambda h: _prompt_mixer(h, w_in[l], w_out[l]), *lw)
        xs, sts = _macaron_layer(xs, lambda h: _sample_mixer(h, cache_k, cache_v, cache_idx_k, state_ret,
                                                             page_table, l, w_in[l], w_out[l]), *lw)
        new_p.append(stp)
        new_s.append(sts)
    k_prompt = jnp.stack([s[0] for s in new_p])
    v_prompt = jnp.stack([s[1] for s in new_p])
    idxk_prompt = jnp.stack([s[2] for s in new_p])
    ret_prompt = jnp.stack([s[3] for s in new_p])
    k_sample = jnp.stack([s[0] for s in new_s])
    v_sample = jnp.stack([s[1] for s in new_s])
    idxk_sample = jnp.stack([s[2] for s in new_s])
    ret_sample = jnp.stack([s[3] for s in new_s])
    y_prompt = xp[:, N_META:]
    return (y_prompt, xs, k_prompt, v_prompt, idxk_prompt, ret_prompt, k_sample, v_sample, idxk_sample, ret_sample)


_drawn_inputs = setup_inputs


def setup_inputs(seed=0):
    import zlib

    import numpy as np

    out = dict(_drawn_inputs(seed))
    spreads = {}
    factors = {'ln2_g': 2.83, 'ln2_b': 2.817, 'ln3_g': 2.952, 'ln3_b': 2.748}
    for name, (base, spread) in spreads.items():
        noise = np.random.default_rng([zlib.crc32(name.encode()), seed]).standard_normal(out[name].shape)
        drawn = base * np.exp(spread * noise) if base else spread * noise
        out[name] = __import__('jax').numpy.asarray(drawn.astype(out[name].dtype))
    for name, factor in factors.items():
        out[name] = (out[name] * factor).astype(out[name].dtype)
    return out
```

```python
from contextlib import ExitStack, contextmanager

import numpy as np
import concourse.bass as bass
from concourse import mybir

ALU = mybir.AluOpType
ACT = mybir.ActivationFunctionType
AX = mybir.AxisListType
F32 = mybir.dt.float32
I32 = mybir.dt.int32

P = 128
D, SEQ, META, DFF = 1024, 512, 16, 2816
NB, NQ, PAST, PAGE = 8, 4, 2048, 128
NPAGE = PAST // PAGE
NS = NB * NQ
TAIL = SEQ + META - 512
T = 512 + NS + TAIL
HALF = T // 2
SMP, TL = 512, 512 + NS
KT, FT = D // P, DFF // P
AH, AD, RH = 8, 64, 4
TOPK_P, TOPK_S = 128, 256
ALPHA = 2.0 ** 0.25
EPS = 1e-5
QI, KW, Q, K, V, RQ, RK, RV, G, ZT = 0, 4, 5, 9, 13, 17, 21, 25, 29, 33
FIRST = 9
NEVER, TAKEN = -1e30, -3e38
KEYS = PAST + NQ
CH, NCH = KEYS // 6, 6
LGW = (NPAGE + 1) * 32
ACC_AT = [None, 0, 256, 640, 1152]
ACC_W = 1680

CONSTS = {}
_at = 0
for _n, _w in (("ident", 128), ("mean", 128), ("ones", 128), ("rot", 128), ("tri", 128), ("sel", 128),
               ("maskg", 64), ("blkrow", 256), ("decs", 128), ("xis", 128), ("own", 32), ("tri4", 4),
               ("zeta", 4), ("zetat", 4), ("zetas", 4), ("gam", 12), ("blkcol", 8), ("ln", 48), ("eps", 1)):
    CONSTS[_n] = (_at, _w)
    _at += _w
CONST_W = _at


@contextmanager
def loop(eng, count, steps):
    start = [(t, t.n, k) for t, k in steps]
    with eng.Fori(0, count) as i:
        for t, n, k in start:
            t.n = i * k + n
        yield i
    for t, n, k in start:
        t.n = n + count * k


class Tally:

    def __init__(self, sem, n=0):
        self.sem, self.n = sem, n

    def up(self, k=1):
        self.n = self.n + k
        return self.n


def build(nc, x_t, wg1, wu1, wd1, wg2, wu2, wd2, w_in, w_out, k_pool, v_pool, i_pool, state, pages,
          consts, rope_tab, ret_tab, acc_tab, y_o, k_o, v_o, i_o, rp_o, rs_o):
    wgs, wus, wds = [wg1, wg2], [wu1, wu2], [wd1, wd2]
    with ExitStack() as ctx:
        def sb(name, cols, dt=F32):
            return ctx.enter_context(nc.sbuf_tensor(name, [P, cols], dt))

        sems = {}

        def sem(name):
            if name not in sems:
                sems[name] = ctx.enter_context(nc.semaphore(name))
            return sems[name]

        xbuf, rbuf, big = sb("xbuf", KT * T), sb("rbuf", KT * T), sb("big", ZT * T)
        wring, dring = sb("wring", 4 * 1024), sb("dring", 2 * FT * P)
        lg, sc, acc, scr = sb("lg", NB * LGW), sb("sc", KEYS), sb("acc", ACC_W), sb("scr", 4144)
        cst = sb("cst", CONST_W)
        wi_t, wsel, qibd, qbd = sb("wi_t", 40), sb("wsel", 64), sb("qibd", 256), sb("qbd", 256)
        mask_t, mxb, small = sb("mask_t", LGW), sb("mxb", 512), sb("small", 160)
        pt = ctx.enter_context(nc.sbuf_tensor("pt", [1, NB * NPAGE], I32))
        ps = ctx.enter_context(nc.psum_tensor("ps", [P, 8, 512], F32))

        def c(name):
            a, w = CONSTS[name]
            return cst[:, a:a + w]

        def tiles(buf, n, at=0):
            return buf[:, at:at + n * T].rearrange("p (k t) -> p k t", t=T)

        x, r0, z = tiles(xbuf, KT), tiles(rbuf, KT), tiles(big, ZT)
        h, rbig, mix = tiles(big, FT), tiles(big, KT), r0
        rs = [r0, rbig, r0]

        def halves(ap):
            return ap.rearrange("p (a n) -> p a n", a=2)

        def pair(p):
            return ps[:, 2 * p:2 * p + 2, 0:HALF]

        ident, ones = c("ident"), c("ones")
        lng = c("ln").rearrange("p (n k) -> p n k", n=6)
        w4 = wring[:, :].rearrange("p (s n) -> p s n", s=4)
        d2 = dring[:, :].rearrange("p (s n) -> p s n", s=2)
        kv = dring[:, 0:4096].rearrange("p (s n) -> p s n", s=8)
        st = dring[:, 4096:5632].rearrange("p (s n) -> p s n", s=3)
        s_buf = tiles(scr, 2)
        y_buf = tiles(scr, 2, 2 * T)
        sq = tiles(scr, 2, 4 * T)
        rstd = scr[:, 6 * T:7 * T]
        kid = scr[:, 0:T]
        rel = scr[:, T:T + 1056].rearrange("p (s n) -> p s n", s=2)
        rl = scr[:, T + 1056:T + 1056 + KEYS]
        ki = lg[:, 0:2 * KEYS].rearrange("p (s n) -> p s n", s=2)
        qib = qibd[:, :].rearrange("p (r n) -> p r n", r=4)
        qb = qbd[:, :].rearrange("p (a b n) -> p a b n", a=4, b=NB)
        wi = wi_t[:, :].rearrange("p (t h) -> p t h", h=8)
        ws = wsel[:, :].rearrange("p (g n) -> p g n", g=2)
        lgt = lg[:, :].rearrange("p (b n) -> p b n", b=NB)
        cos_t, sin_t = scr[:, 0:T], scr[:, T:2 * T]
        zc = tiles(scr, 2, 2 * T)
        zs = scr[:, 4 * T:5 * T]
        diag = scr[:, 5 * T:5 * T + 256]
        it_b, kz_b, qx_b, rn_b = (scr[:, 512 * j:512 * (j + 1)] for j in range(4))
        l_b = scr[:, 2048:2048 + 1056].rearrange("p (s n) -> p s n", s=2)
        pt_b = scr[:, 3104:3104 + 1024].rearrange("p (s n) -> p s n", s=2)
        dec, xi, sr = (sc[:, 512 * j:512 * (j + 1)] for j in range(3))
        vt = big[:, 0:2048].rearrange("p (t n) -> p t n", t=4)
        vr = wring[:, 0:2048].rearrange("p (t n) -> p t n", t=4)
        vrs, vrt, vs, vtl = (wring[:, 2048 + 512 * j:2048 + 512 * (j + 1)] for j in range(4))
        mx, rsum = mxb[:, 0:256], mxb[:, 256:512]
        smx, ssum, nmx, rcp = small[:, 0:2], small[:, 2:4], small[:, 4:6], small[:, 6:8]
        m8, mx2, bn, bag, rsd, cmp16 = (small[:, 8:40], small[:, 40:42], small[:, 42:66], small[:, 66:74],
                                        small[:, 74:78], small[:, 80:112])

        def acc_ap(t):
            w = 128 * (t + 1) if t < 4 else 528
            return acc[0:(P if t < 4 else TAIL), ACC_AT[t]:ACC_AT[t] + w]

        block = ctx.enter_context(nc.Block())

        @block.sync
        def _(sp):
            free = [Tally(sem(f"w_free{s}")) for s in range(4)]
            sp.dma_start(pt[:, :], pages).then_inc(sem("pages_in"), 16)

            def weight(s, src, first=False):
                if not first:
                    sp.wait_ge(free[s].sem, free[s].up())
                sp.dma_start(w4[:, s, :], src).then_inc(sem(f"w_in{s}"), 16)

            def ffn_loads(m):
                for s in range(4):
                    f, up = divmod(s, 2)
                    weight(s, (wus if up else wgs)[m][f], first=(m == 0))
                with loop(sp, FT // 2 - 1, [(f, 1) for f in free]) as i:
                    for s in range(4):
                        f, up = divmod(s, 2)
                        weight(s, (wus if up else wgs)[m][bass.ds(i * 2 + 2 + f, 1)].rearrange("a p n -> (a p) n"))
                dfree = [Tally(sem(f"d_free{s}"), 4 * m) for s in range(2)]
                if m == 1:
                    for s in range(8):
                        sp.wait_ge(sem(f"kv_free{s}"), 4 * NB)
                    sp.wait_ge(sem("st_out0"), 48)
                    sp.wait_ge(sem("st_out1"), 48)
                    sp.wait_ge(sem("st_out2"), 32)
                for s in range(2):
                    sp.dma_start(d2[:, s, :], wds[m][s]).then_inc(sem(f"d_in{s}"), 16)
                with loop(sp, KT // 2 - 1, [(d, 1) for d in dfree]) as i:
                    for s in range(2):
                        sp.wait_ge(dfree[s].sem, dfree[s].up())
                        sp.dma_start(d2[:, s, :], wds[m][bass.ds(i * 2 + 2 + s, 1)].rearrange("a p n -> (a p) n")) \
                            .then_inc(sem(f"d_in{s}"), 16)

            def page_reg(at):
                return sp.value_load(pt[0:1, bass.ds(at, 1)], min_val=0, max_val=k_pool.shape[0] - 1)

            def index_pages(pr):
                for b2 in range(2):
                    with sp.Fori(0, NPAGE) as i:
                        pg = page_reg(i + (2 * pr + b2) * NPAGE)
                        sp.dma_start(ki[64 * b2:64 * b2 + 64, pr % 2, bass.ds(i * PAGE, PAGE)],
                                     i_pool[bass.ds(pg, 1)].rearrange("a p n -> (a p) n")) \
                            .then_inc(sem(f"ki_in{pr}"), 16)

            ffn_loads(0)
            sp.wait_ge(sem("pages_in"), 16)
            for t in range(FIRST):
                weight(t % 4, w_in[t])
            for pr in range(2):
                index_pages(pr)
            sp.wait_ge(sem("ki_used"), 1)
            for pr in range(2, 4):
                index_pages(pr)
            for s in range(2):
                sp.wait_ge(sem(f"d_free{s}"), 4)
            kvf = [Tally(sem(f"kv_free{s}")) for s in range(8)]

            def kv_page(s, at, pool, first=False):
                if not first:
                    sp.wait_ge(kvf[s].sem, kvf[s].up())
                pg = page_reg(at)
                sp.dma_start(kv[:, s, :], pool[bass.ds(pg, 1)].rearrange("a p n -> (a p) n")) \
                    .then_inc(sem(f"kv_in{s}"), 16)

            for s in range(8):
                kv_page(s, s, k_pool, first=True)
            for s in range(3):
                weight(s, w_in[FIRST + s])
            for s in range(8):
                kv_page(s, s + 8, k_pool)
            with loop(sp, NB - 1, [(f, 1) for f in free[:3]] + [(f, 2) for f in kvf]) as i:
                for s in range(3):
                    weight(s, w_in[bass.ds(i * 3 + FIRST + 3 + s, 1)].rearrange("a p n -> (a p) n"))
                for s in range(16):
                    kv_page(s % 8, i * NPAGE + NPAGE + s, k_pool)
            sp.wait_ge(sem("index_done"), 1)
            sp.dma_start(scr[:, 0:2 * T], rope_tab).then_inc(sem("rope_in"), 16)
            sp.wait_ge(sem("z_done"), ZT)
            sp.dma_start(k_o, z[:, K:K + 4, :]).then_inc(sem("kvi_out"), 16)
            sp.dma_start(v_o, z[:, V:V + 4, :]).then_inc(sem("kvi_out"), 16)
            sp.dma_start(i_o, z[0:64, KW, :]).then_inc(sem("kvi_out"), 16)
            with loop(sp, NB * 2, [(f, 1) for f in kvf]) as i:
                for s in range(8):
                    kv_page(s, i * 8 + s, v_pool)
            sp.wait_ge(sem("mix_read"), 1)
            for s in range(4):
                weight(s, w_out[s])
            for s in range(4):
                weight(s, w_out[s + 4])
            ffn_loads(1)
            with sp.Fori(0, KT) as i:
                sp.wait_ge(sem("x_done"), i + 2 * KT + 1)
                sp.dma_start(y_o[bass.ds(i, 1)].rearrange("a p n -> (a p) n"),
                             x[:, bass.ds(i, 1), :].rearrange("p a n -> p (a n)")).then_inc(sem("y_out"), 16)
            sp.wait_ge(sem("y_out"), 16 * KT)
            sp.wait_ge(sem("kvi_out"), 48)
            sp.wait_ge(sem("rp_out"), 16)
            for s in range(3):
                sp.wait_ge(sem(f"st_out{s}"), 16 * ((NB - s + 2) // 3))

        @block.tensor
        def _(pe):
            w_in_t = [Tally(sem(f"w_in{s}")) for s in range(4)]
            d_in_t = [Tally(sem(f"d_in{s}")) for s in range(2)]
            kv_in_t = [Tally(sem(f"kv_in{s}")) for s in range(8)]
            hdone, rdone = Tally(sem("h_done")), Tally(sem("r_done"))
            zdone = Tally(sem("z_done"))
            pe.sem_inc(sem("sq_free"), 2)

            def mm(out, lhs, rhs, start=True, stop=True, **kw):
                return nc.tensor.matmul(out, lhs, rhs, start=start, stop=stop, **kw)

            def tr(out, in_, k0, k1):
                return nc.tensor.transpose(out, in_, ident[k0:k1, k0:k1])

            def wide(p, wt, kn, src, free_sem, full_sem=None):
                for a in range(2):
                    for k in range(kn):
                        last = mm(ps[:, 2 * p + a, 0:HALF], wt[:, k * P:(k + 1) * P],
                                  src[:, k, a * HALF:(a + 1) * HALF], k == 0, k == kn - 1)
                return last

            def weight(s):
                pe.wait_ge(w_in_t[s].sem, w_in_t[s].up(16))

            def ffn(m):
                hdone.n = FT * m
                with loop(pe, FT // 2, [(w, 16) for w in w_in_t] + [(hdone, 2)]):
                    for j in range(2):
                        pe.wait_ge(sem("h_done"), hdone.up())
                        weight(2 * j)
                        wide(j, w4[:, 2 * j, :], KT, x, None).then_inc(sem(f"w_free{2 * j}"), 1)
                        weight(2 * j + 1)
                        wide(2 + j, w4[:, 2 * j + 1, :], KT, x, None).then_inc(sem(f"w_free{2 * j + 1}"), 1)
                pe.wait_ge(sem("h_done"), 2 + FT * (m + 1))
                rdone.n = KT * 2 * m
                with loop(pe, KT // 2, [(w, 16) for w in d_in_t] + [(rdone, 2)]):
                    for j in range(2):
                        pe.wait_ge(sem("r_done"), rdone.up())
                        pe.wait_ge(d_in_t[j].sem, d_in_t[j].up(16))
                        wide(j, d2[:, j, :], FT, h, None).then_inc(sem(f"d_free{j}"), 1)
                norm(2 * m)

            def norm(n):
                r = rs[n]
                for d in range(KT):
                    pe.wait_ge(sem("r_done"), 2 + KT * n + d + 1)
                    for a in range(2):
                        last = mm(ps[:, 4 + a, 0:HALF], c("mean"), r[:, d, a * HALF:(a + 1) * HALF],
                                  d == 0, d == KT - 1)
                last.then_inc(sem("mean_full"), 1)
                for d in range(KT):
                    pe.wait_ge(sem("sq_done"), KT * n + d + 1)
                    for a in range(2):
                        last = mm(ps[:, 6 + a, 0:HALF], c("mean"), sq[:, d % 2, a * HALF:(a + 1) * HALF],
                                  d == 0, d == KT - 1)
                    last.then_inc(sem("sq_free"), 1)
                pe.wait_ge(sem("x_done"), KT * (n + 1))

            pe.wait_ge(sem("x_in"), 16)
            pe.wait_ge(sem("cst_in"), 16)
            ffn(0)

            for t in range(FIRST):
                weight(t % 4)
                if t >= 3:
                    pe.wait_ge(sem("z_done"), t - 2)
                wide(t % 3, w4[:, t % 4, :], KT, x, None).then_inc(sem(f"w_free{t % 4}"), 1)
            pe.wait_ge(sem("z_done"), FIRST)
            for t in (1, 2, 3):
                tr(ps[:, 6, 64 * t:64 * t + 64], z[64:128, KW, 128 * t:128 * t + 128], 64, 128)
            tr(ps[0:TAIL, 6, 0:64], z[64:128, KW, TL:T], 64, 128)
            mm(ps[:, 7, 0:NS], c("sel")[64:128, :], z[64:128, KW, SMP:TL]).then_inc(sem("prep_full"), 1)
            pe.wait_ge(sem("kid_done"), 2)
            u = 0
            for t in (1, 2, 3, 4):
                for hd in range(AH):
                    lo = 64 * (hd % 2)
                    p = u % 2
                    if u >= 2:
                        pe.wait_ge(sem("rel_done"), u - 1)
                    q0, n, nk = (128 * t, P, 128 * (t + 1)) if t < 4 else (TL, TAIL, 512)
                    last = mm(ps[0:n, 2 * p, 0:nk], z[lo:lo + 64, QI + hd // 2, q0:q0 + n], kid[lo:lo + 64, 0:nk])
                    if t == 4:
                        last = mm(ps[0:n, 2 * p + 1, 0:TAIL], z[lo:lo + 64, QI + hd // 2, q0:q0 + n],
                                  kid[lo:lo + 64, TL:T])
                    last.then_inc(sem("s_full"), 1)
                    u += 1
            pe.wait_ge(sem("qib_done"), 1)
            pe.wait_ge(sem("rel_done"), u)
            pe.wait_ge(sem("wsel_done"), 1)
            pe.wait_ge(sem("wi_done"), 1)
            for g in range(2):
                for j in range(2):
                    pe.wait_ge(sem(f"ki_in{2 * g + j}"), 16 * 2 * NPAGE)
                    pe.wait_ge(sem("kin_done"), 2 * g + j + 1)
                for ch in range(NCH):
                    if g:
                        pe.wait_ge(sem("rl_done"), ch + 1)
                    for j in range(2):
                        last = mm(ps[64 * j:64 * j + 64, ch, 0:CH], qib[:, 2 * g + j, :],
                                  ki[:, j, ch * CH:(ch + 1) * CH])
                    last.then_inc(sem("ss_full"), 1)
                if g == 0:
                    pe.wait_ge(sem("ss_full"), NCH)
                    pe.sem_inc(sem("ki_used"), 1)
                for ch in range(NCH):
                    pe.wait_ge(sem("rl_done"), NCH * g + ch + 1)
                    k = NCH * g + ch
                    if k >= 2:
                        s_, v_ = ("sw_g0", k - 1) if k - 2 < NCH else ("sw_g1", k - 1 - NCH)
                        pe.wait_ge(sem(s_), v_)
                    mm(ps[0:NS, 6 + ch % 2, 0:CH], ws[:, g, :], rl[:, ch * CH:(ch + 1) * CH]) \
                        .then_inc(sem("sw_full"), 1)
            pe.wait_ge(sem("sw_g1"), NCH)
            pe.wait_ge(sem("qb_done"), 1)
            zdone.n = FIRST - 2 - 1
            lgd = Tally(sem("lg_done"))
            with loop(pe, NB, [(w, 16) for w in w_in_t[:3]] + [(k_, 32) for k_ in kv_in_t] + [(zdone, 3), (lgd, 1)]) as i:
                for j in range(3):
                    weight(j)
                    pe.wait_ge(sem("z_done"), zdone.up())
                    wide(j, w4[:, j, :], KT, x, None).then_inc(sem(f"w_free{j}"), 1)
                pe.wait_ge(sem("lg_done"), lgd.up())
                for pg in range(NPAGE):
                    s = pg % 8
                    pe.wait_ge(kv_in_t[s].sem, kv_in_t[s].up(16))
                    for hp in range(4):
                        last = mm(ps[:, 6, pg * 32 + hp * 8:pg * 32 + hp * 8 + 8], kv[:, s, hp * P:(hp + 1) * P],
                                  qb[:, hp, bass.ds(i, 1), :].rearrange("p a n -> p (a n)"))
                    last.then_inc(sem(f"kv_free{s}"), 1)
            pe.wait_ge(sem("z_done"), ZT)
            for hp in range(4):
                last = mm(ps[0:NS, 7, hp * 64:hp * 64 + 64], z[:, K + hp, SMP:TL],
                          qb[:, hp, :, :].rearrange("p b n -> p (b n)"))
            last.then_inc(sem("p16_full"), 1)
            k = 0
            for src in (V, RV):
                for t0, n in [(128 * t, P) for t in range(4)] + [(SMP, NS), (TL, TAIL)]:
                    if k >= 4:
                        pe.wait_ge(sem("tr_done"), k - 3)
                    for j in range(4):
                        last = tr(ps[0:n, k % 4, j * P:(j + 1) * P], z[:, src + j, t0:t0 + n], 0, P)
                    last.then_inc(sem("tr_full"), 1)
                    k += 1
            pe.wait_ge(sem("tr_done"), 12)
            pe.wait_ge(sem("lg_done"), NB + 1)
            pe.wait_ge(sem("smask_done"), 1)
            for pg in range(NPAGE):
                tr(ps[:, 4, pg * NS:(pg + 1) * NS], sc[0:NS, pg * PAGE:(pg + 1) * PAGE], 0, NS)
            tr(ps[0:NS, 5, 0:NS], cmp16[0:NS, :], 0, NS).then_inc(sem("masks_full"), 1)
            for u in range(8):
                if u >= 2:
                    pe.wait_ge(sem("zs_done"), u - 1)
                for a in range(2):
                    last = mm(ps[:, 2 * (u % 2) + a, 0:HALF], c("rot"), z[:, RQ + u, a * HALF:(a + 1) * HALF])
                last.then_inc(sem("rot_full"), 1)
            pe.wait_ge(sem("mask_used"), 1)
            pe.wait_ge(sem("mx_done"), 1)
            for g in range(2):
                last = tr(ps[:, 5, g * P:(g + 1) * P], mx[:, g * P:(g + 1) * P], 0, P)
            last.then_inc(sem("mxt_full"), 1)
            pe.wait_ge(sem("diag_done"), 1)
            mm(ps[:, 4, 0:256], ones, diag).then_inc(sem("mxb_full"), 1)
            pe.wait_ge(sem("psum_done"), 1)
            mm(ps[:, 5, 0:256], ones, mx).then_inc(sem("sum_full"), 1)
            pe.wait_ge(sem("rsum_done"), 1)
            pe.wait_ge(sem("rope_done"), 8)

            def ret_in(cn, t0, n):
                for hd in range(RH):
                    last = mm(ps[0:n, 0, hd * P:hd * P + n], z[:, RK + hd, t0:t0 + n], z[:, RQ + hd, t0:t0 + n])
                last.then_inc(sem("inner_full"), 1)
                for hd in range(RH):
                    last = tr(ps[0:n, 1, hd * P:(hd + 1) * P], z[:, RK + hd, t0:t0 + n], 0, P)
                last.then_inc(sem("kt_full"), 1)

            def ret_out(cn, n):
                pe.wait_ge(sem("rn_done"), cn + 1)
                for hd in range(RH):
                    last = tr(ps[:, 4, hd * P:hd * P + n], rn_b[0:n, hd * P:(hd + 1) * P], 0, n)
                last.then_inc(sem("rt_full"), 1)

            for cn in range(5):
                t0, n = (128 * cn, P) if cn < 4 else (TL, TAIL)
                vv = vr[:, cn, :] if cn < 4 else vrt
                ret_in(cn, t0, n)
                pe.wait_ge(sem("it_done"), cn + 1)
                pe.wait_ge(sem("qx_done"), cn + 1)
                if cn:
                    pe.wait_ge(sem("sr_done"), cn)
                for hd in range(RH):
                    o = ps[0:n, 2, hd * P:(hd + 1) * P]
                    last = mm(o, it_b[0:n, hd * P:hd * P + n], vv[0:n, hd * P:(hd + 1) * P], True, cn == 0)
                    if cn:
                        last = mm(o, qx_b[:, hd * P:hd * P + n], sr[:, hd * P:(hd + 1) * P], False, True)
                last.then_inc(sem("ro_full"), 1)
                pe.wait_ge(sem("kz_done"), cn + 1)
                for hd in range(RH):
                    last = mm(ps[:, 3, hd * P:(hd + 1) * P], kz_b[0:n, hd * P:(hd + 1) * P],
                              vv[0:n, hd * P:(hd + 1) * P])
                last.then_inc(sem("rst_full"), 1)
                ret_out(cn, n)
                pe.wait_ge(sem("mixr_done"), cn + 1)
            ret_in(5, SMP, NS)
            pe.wait_ge(sem("it_done"), 6)
            for hd in range(RH):
                mm(ps[0:NS, 4 + hd, 0:P], it_b[0:NS, hd * P:hd * P + NS], vrs[0:NS, hd * P:(hd + 1) * P], True, False)
            for b in range(NB):
                pe.wait_ge(sem("qxb_done"), b + 1)
                pe.wait_ge(sem(f"st_in{b % 3}"), 16 * (b // 3 + 1))
                for hd in range(RH):
                    last = mm(ps[0:NS, 4 + hd, 0:P], qx_b[:, 128 * (b % 2) + hd * NS + 256:128 * (b % 2) + (hd + 1) * NS + 256],
                              st[:, b % 3, hd * P:(hd + 1) * P], False, b == NB - 1)
                last.then_inc(sem("cross_full"), 1)
                pe.wait_ge(sem("kzb_done"), b + 1)
                if b >= 2:
                    pe.wait_ge(sem("st_new"), b - 1)
                for hd in range(RH):
                    last = mm(ps[:, 2 + b % 2, hd * P:(hd + 1) * P],
                              rn_b[0:NS, hd * P:(hd + 1) * P] if b % 2 else l_b[0:NS, 0, hd * P:(hd + 1) * P],
                              vrs[0:NS, hd * P:(hd + 1) * P])
                last.then_inc(sem("dst_full"), 1)
            pe.wait_ge(sem("rn_done"), 6)
            for hd in range(RH):
                last = tr(ps[:, 0, hd * P:hd * P + NS], rn_b[0:NS, hd * P:(hd + 1) * P], 0, NS)
            last.then_inc(sem("rt_full"), 1)
            pe.wait_ge(sem("mixr_done"), 6)
            pe.wait_ge(sem("st_new"), NB)

            units = [(hd, t) for hd in range(AH) for t in range(5)]

            def scores(u, hd, t):
                lo, p = 64 * (hd % 2), u % 2
                q0, n, nk = (128 * t, P, 128 * (t + 1)) if t < 4 else (TL, TAIL, 512)
                if u >= 2:
                    pe.wait_ge(sem("al_done"), u - 1)
                last = mm(ps[0:n, p, 0:nk], z[lo:lo + 64, Q + hd // 2, q0:q0 + n], z[lo:lo + 64, K + hd // 2, 0:nk])
                if t == 4:
                    last = mm(ps[0:n, 2, 0:TAIL], z[lo:lo + 64, Q + hd // 2, q0:q0 + n],
                              z[lo:lo + 64, K + hd // 2, TL:T])
                last.then_inc(sem("as_full"), 1)

            def turn(u, hd, t):
                p, n = u % 2, (P if t < 4 else TAIL)
                pe.wait_ge(sem("ap_done"), u + 1)
                if u >= 2:
                    pe.wait_ge(sem("apt_done"), u - 1)
                for j in range(t + 1 if t < 4 else 4):
                    last = tr(ps[:, 4 + p, j * n:(j + 1) * n], l_b[0:n, p, j * P:(j + 1) * P], 0, n)
                if t == 4:
                    last = tr(ps[0:TAIL, 4 + p, 4 * n:5 * n], l_b[0:n, p, 512:512 + TAIL], 0, n)
                last.then_inc(sem("at_full"), 1)

            def values(u, hd, t):
                p, n, lo = u % 2, (P if t < 4 else TAIL), 64 * (hd % 2)
                pe.wait_ge(sem("apt_done"), u + 1)
                if u >= 2:
                    pe.wait_ge(sem("ao_done"), u - 1)
                nj = t + 1 if t < 4 else 5
                for j in range(nj):
                    lhs = vt[:, j, hd * AD:(hd + 1) * AD] if j < 4 else vtl[0:TAIL, hd * AD:(hd + 1) * AD]
                    rhs = pt_b[:, p, j * n:(j + 1) * n] if j < 4 else pt_b[0:TAIL, p, 4 * n:5 * n]
                    last = mm(ps[lo:lo + 64, 6 + p, 0:n], lhs, rhs, j == 0, j == nj - 1)
                last.then_inc(sem("ao_full"), 1)

            def sample_values(b):
                pe.wait_ge(sem("sp_done"), NB)
                if b >= 1:
                    pe.wait_ge(sem("so_done"), 4 * b)
                for hf in range(2):
                    for s in range(8):
                        pe.wait_ge(kv_in_t[s].sem, kv_in_t[s].up(16))
                    for hp in range(4):
                        o = ps[:, 3, hf * 32 + hp * 8:hf * 32 + hp * 8 + 8]
                        for s in range(8):
                            last = mm(o, kv[:, s, hp * P:(hp + 1) * P],
                                      lgt[:, b, (hf * 8 + s) * 32 + hp * 8:(hf * 8 + s) * 32 + hp * 8 + 8],
                                      s == 0, s == 7 and hf == 0)
                            if hp == 3:
                                last.then_inc(sem(f"kv_free{s}"), 1)
                        if hf:
                            last = mm(o, vs[0:NS, hp * P:(hp + 1) * P],
                                      lgt[0:NS, b, 512 + hp * 8:512 + hp * 8 + 8], False, True)
                last.then_inc(sem("so_full"), 1)

            for u in range(len(units) + 2):
                if u < len(units):
                    scores(u, *units[u])
                if 1 <= u <= len(units):
                    turn(u - 1, *units[u - 1])
                if u >= 2:
                    values(u - 2, *units[u - 2])
                if u % 5 == 4 and u // 5 < NB:
                    sample_values(u // 5)
            pe.wait_ge(sem("ao_done"), len(units))
            pe.wait_ge(sem("so_done"), 4 * NB)
            pe.sem_inc(sem("mix_read"), 1)

            for d in range(KT):
                weight(d % 4)
                pe.wait_ge(sem("r_done"), KT + d + 1)
                wide(d % 2, w4[:, d % 4, :], KT, mix, None).then_inc(sem(f"w_free{d % 4}"), 1)
            norm(1)
            ffn(1)

        @block.scalar
        def _(act):
            act.sem_inc(sem("lg_done"), 1)
            act.dma_start(xbuf[:, :], x_t).then_inc(sem("x_in"), 16)
            act.dma_start(cst[:, :], consts).then_inc(sem("cst_in"), 16)
            act.dma_start(acc[:, :], acc_tab).then_inc(sem("acc_in"), 16)
            act.wait_ge(sem("cst_in"), 16)

            def ev(out, in_, func=ACT.Copy, **kw):
                return nc.scalar.activation(out, in_, func, **kw)

            def ffn(m):
                ups = [Tally(sem("w_free1"), up_seen[0]), Tally(sem("w_free3"), up_seen[1])]
                with loop(act, FT // 2, [(u_, 1) for u_ in ups]):
                    for j in range(2):
                        act.wait_ge(ups[j].sem, ups[j].up())
                        ev(halves(s_buf[:, j, :]), pair(j), ACT.Silu).then_inc(sem("s_done"), 1)
                dn = [Tally(sem(f"d_free{j}"), 4 * m) for j in range(2)]
                with loop(act, KT // 2, [(d_, 1) for d_ in dn]):
                    for j in range(2):
                        act.wait_ge(dn[j].sem, dn[j].up())
                        ev(halves(y_buf[:, j, :]), pair(j), scale=0.5).then_inc(sem("y_done"), 1)
                norm(2 * m)

            def norm(n):
                r = rs[n]
                cd, sf = Tally(sem("c_done"), KT * n), Tally(sem("sq_free"), KT * n)
                with loop(act, KT // 2, [(cd, 2), (sf, 2)]) as i:
                    for j in range(2):
                        act.wait_ge(cd.sem, cd.up())
                        act.wait_ge(sf.sem, sf.up())
                        ev(sq[:, j, :], r[:, bass.ds(i * 2 + j, 1), :].rearrange("p a n -> p (a n)"), ACT.Square) \
                            .then_inc(sem("sq_done"), 1)
                act.wait_ge(sem("sq_free"), 2 + KT * (n + 1))
                ev(halves(rstd), pair(3), ACT.Sqrt, bias=c("eps")).then_inc(sem("std_done"), 1)
                nd = Tally(sem("n_done"), KT * n)
                with loop(act, KT, [(nd, 1)]) as i:
                    act.wait_ge(nd.sem, nd.up())
                    ev(x[:, bass.ds(i, 1), :].rearrange("p a n -> p (a n)"),
                       r[:, bass.ds(i, 1), :].rearrange("p a n -> p (a n)"), ACT.Identity,
                       scale=lng[:, 2 * n, bass.ds(i, 1)], bias=lng[:, 2 * n + 1, bass.ds(i, 1)]) \
                        .then_inc(sem("x_done"), 1)

            up_seen = [0, 0]
            ffn(0)
            for t in range(FIRST):
                act.wait_ge(sem(f"w_free{t % 4}"), 11 + t // 4 + 1)
                if t == KW:
                    for lo in (0, 64):
                        ev(kid[lo:lo + 64, :].rearrange("p (a n) -> p a n", a=2), ps[0:64, 2 * (t % 3):2 * (t % 3) + 2, 0:HALF]) \
                            .then_inc(sem("kid_done"), 1)
                ev(halves(z[:, t, :]), pair(t % 3)).then_inc(sem("z_done"), 1)
            act.wait_ge(sem("prep_full"), 1)
            for t in (1, 2, 3):
                ev(wi[:, t, :], ps[:, 6, 64 * t:64 * t + 8], scale=AH ** -0.5)
            ev(wi[0:TAIL, 4, :], ps[0:TAIL, 6, 0:8], scale=AH ** -0.5).then_inc(sem("wi_done"), 1)
            u = 0
            for t in (1, 2, 3, 4):
                for hd in range(AH):
                    n, nk = (P, 128 * (t + 1)) if t < 4 else (TAIL, 512)
                    act.wait_ge(sem("s_full"), u + 1)
                    if u >= 2:
                        act.wait_ge(sem("acc_done"), u - 1)
                    last = ev(rel[0:n, u % 2, 0:nk], ps[0:n, 2 * (u % 2), 0:nk], ACT.Relu, scale=AD ** -0.5)
                    if t == 4:
                        last = ev(rel[0:n, u % 2, 512:512 + TAIL], ps[0:n, 2 * (u % 2) + 1, 0:TAIL], ACT.Relu,
                                  scale=AD ** -0.5)
                    last.then_inc(sem("rel_done"), 1)
                    u += 1
            for g in range(2):
                for ch in range(NCH):
                    act.wait_ge(sem("ss_full"), NCH * g + ch + 1)
                    if g:
                        act.wait_ge(sem("sw_full"), ch + 1)
                    ev(rl[:, ch * CH:(ch + 1) * CH], ps[:, ch, 0:CH], ACT.Relu, scale=AD ** -0.5) \
                        .then_inc(sem("rl_done"), 1)
                if g == 0:
                    for ch in range(NCH):
                        act.wait_ge(sem("sw_full"), ch + 1)
                        ev(sc[0:NS, ch * CH:(ch + 1) * CH], ps[0:NS, 6 + ch % 2, 0:CH]).then_inc(sem("sw_g0"), 1)
            wf = [Tally(sem("w_free0"), 14), Tally(sem("w_free1"), 13), Tally(sem("w_free2"), 13)]
            kf = Tally(sem("kv_free7"))
            with loop(act, NB, [(w, 1) for w in wf] + [(kf, 2)]) as i:
                for j in range(3):
                    act.wait_ge(wf[j].sem, wf[j].up())
                    ev(halves(z[:, bass.ds(i * 3 + FIRST + j, 1), :].rearrange("p a n -> p (a n)")), pair(j)) \
                        .then_inc(sem("z_done"), 1)
                act.wait_ge(kf.sem, kf.up(2))
                ev(lgt[:, bass.ds(i, 1), 0:512].rearrange("p a n -> p (a n)"), ps[:, 6, :], scale=AD ** -0.5) \
                    .then_inc(sem("lg_done"), 1)
            act.wait_ge(sem("p16_full"), 1)
            act.wait_ge(sem("lg_init"), 1)
            for hp in range(4):
                last = ev(lgt[0:NS, :, 512 + hp * 8:512 + hp * 8 + 8],
                          ps[0:NS, 7, hp * 64:hp * 64 + 64].rearrange("p (b n) -> p b n", b=NB), scale=AD ** -0.5)
            last.then_inc(sem("p16_done"), 1)
            k = 0
            for src in (V, RV):
                for t in range(6):
                    n = P if t < 4 else (NS, TAIL)[t - 4]
                    dst = ((vt, vs, vtl) if src == V else (vr, vrs, vrt))
                    o = dst[0][:, t, :] if t < 4 else dst[t - 3][0:n, :]
                    act.wait_ge(sem("tr_full"), k + 1)
                    ev(o, ps[0:n, k % 4, :]).then_inc(sem("tr_done"), 1)
                    k += 1
            for j in range(4):
                act.wait_ge(sem("z_done"), ZT)
                last = ev(z[:, G + j, :], z[:, G + j, :], ACT.Silu)
            last.then_inc(sem("sg_done"), 1)
            for b in range(NB):
                act.wait_ge(sem("sub_done"), b + 1)
                ev(lgt[:, b, :], lgt[:, b, :], ACT.Exp).then_inc(sem("sp_done"), 1)
            for cn in range(6):
                n = P if cn < 4 else (TAIL, NS)[cn - 4]
                act.wait_ge(sem("bag_done"), cn + 1)
                ev(rsd[0:n, :], bag[0:n, 1::2], ACT.Sqrt, bias=c("eps")[0:n, :]).then_inc(sem("rsd_done"), 1)
            units = [(hd, t) for hd in range(AH) for t in range(5)]

            def probs(u, hd, t):
                p, n, w = u % 2, (P if t < 4 else TAIL), (128 * (t + 1) if t < 4 else 528)
                act.wait_ge(sem("nmx_done"), u + 1)
                ev(l_b[0:n, p, 0:w], l_b[0:n, p, 0:w], ACT.Exp, bias=nmx[0:n, p:p + 1],
                   accum_out=ssum[0:n, p:p + 1]).then_inc(sem("ae_done"), 1)

            def turned(u, hd, t):
                p, n = u % 2, (P if t < 4 else TAIL)
                act.wait_ge(sem("at_full"), u + 1)
                if u >= 2:
                    act.wait_ge(sem("ao_full"), u - 1)
                w = (t + 1 if t < 4 else 4) * n
                last = ev(pt_b[:, p, 0:w], ps[:, 4 + p, 0:w])
                if t == 4:
                    last = ev(pt_b[0:TAIL, p, 4 * n:5 * n], ps[0:TAIL, 4 + p, 4 * n:5 * n])
                last.then_inc(sem("apt_done"), 1)

            def out(u, hd, t):
                p, n, lo, q0 = u % 2, (P if t < 4 else TAIL), 64 * (hd % 2), (128 * t if t < 4 else TL)
                act.wait_ge(sem("ao_full"), u + 1)
                ev(mix[lo:lo + 64, hd // 2, q0:q0 + n], ps[lo:lo + 64, 6 + p, 0:n]).then_inc(sem("ao_done"), 1)

            for u in range(len(units) + 2):
                if u < len(units):
                    probs(u, *units[u])
                if 1 <= u <= len(units):
                    turned(u - 1, *units[u - 1])
                if u >= 2:
                    out(u - 2, *units[u - 2])
            norm(1)
            up_seen = [11 + 2 + 8 + 2, 11 + 2 + 2]
            ffn(1)

        @block.vector
        def _(dve):
            v = nc.vector
            own = Tally(sem("dve_own"))

            def seq(ins):
                ins.then_inc(own.sem, 1)
                dve.wait_ge(own.sem, own.up())

            dve.sem_inc(sem("h_done"), 2)
            dve.sem_inc(sem("r_done"), 2)
            seq(v.memset(qibd[:, :], 0.0))
            seq(v.memset(qbd[:, :], 0.0))
            dve.wait_ge(sem("cst_in"), 16)

            def row(ap, i):
                return ap[:, bass.ds(i, 1), :].rearrange("p a n -> p (a n)")

            def ffn(m):
                sd = Tally(sem("s_done"), FT * m)
                with loop(dve, FT // 2, [(sd, 2)]) as i:
                    for j in range(2):
                        dve.wait_ge(sd.sem, sd.up())
                        v.tensor_tensor(halves(row(h, i * 2 + j)), halves(s_buf[:, j, :]), pair(2 + j), ALU.mult) \
                            .then_inc(sem("h_done"), 1)
                yd = Tally(sem("y_done"), KT * m)
                with loop(dve, KT // 2, [(yd, 2)]) as i:
                    for j in range(2):
                        dve.wait_ge(yd.sem, yd.up())
                        v.scalar_tensor_tensor(row(rs[2 * m], i * 2 + j), row(x, i * 2 + j), ALPHA, y_buf[:, j, :],
                                               ALU.mult, ALU.add).then_inc(sem("r_done"), 1)
                norm(2 * m)

            def norm(n):
                r = rs[n]
                dve.wait_ge(sem("mean_full"), n + 1)
                dve.wait_ge(sem("r_done"), 2 + KT * (n + 1))
                with dve.Fori(0, KT) as i:
                    v.tensor_tensor(halves(row(r, i)), halves(row(r, i)), pair(2), ALU.subtract) \
                        .then_inc(sem("c_done"), 1)
                dve.wait_ge(sem("std_done"), n + 1)
                dve.wait_ge(sem("c_done"), KT * (n + 1))
                seq(v.reciprocal(rstd, rstd))
                with dve.Fori(0, KT) as i:
                    v.tensor_tensor(row(r, i), row(r, i), rstd, ALU.mult).then_inc(sem("n_done"), 1)

            ffn(0)
            dve.wait_ge(sem("z_done"), 4)
            for b2 in range(2):
                for par in range(2):
                    o = qib[64 * b2:64 * b2 + 64, :, 32 * b2:32 * b2 + 32] \
                        .rearrange("p r (a two q) -> p r a two q", two=2, q=NQ)
                    s_ = z[64 * par:64 * par + 64, QI:QI + 4, SMP:TL].rearrange("p a (r two q) -> p r a two q", two=2, q=NQ)
                    for a in range(4):
                        last = v.tensor_copy(o[:, :, a, par, :], s_[:, :, a, b2, :])
            last.then_inc(sem("qib_done"), 1)
            def new_keys(pr):
                for b2 in range(2):
                    lo = 64 * b2
                    c0 = SMP + (2 * pr + b2) * NQ
                    last = v.tensor_copy(ki[lo:lo + 64, pr % 2, PAST:KEYS], kid[lo:lo + 64, c0:c0 + NQ])
                last.then_inc(sem("kin_done"), 1)

            dve.wait_ge(sem("kid_done"), 2)
            new_keys(0)
            new_keys(1)
            dve.wait_ge(sem("z_done"), FIRST)
            for h2 in range(2):
                lo = 64 * h2
                last = v.tensor_copy(qb[lo:lo + 64, :, :, 4 * h2:4 * h2 + 4],
                                     z[lo:lo + 64, Q:Q + 4, SMP:TL].rearrange("p a (b q) -> p a b q", q=NQ))
            last.then_inc(sem("qb_done"), 1)
            dve.wait_ge(sem("prep_full"), 1)
            for g in range(2):
                last = v.tensor_tensor(ws[:, g, :], ps[:, 7, 0:NS], c("maskg")[:, g * NS:(g + 1) * NS], ALU.mult)
            last.then_inc(sem("wsel_done"), 1)
            dve.wait_ge(sem("wi_done"), 1)
            dve.wait_ge(sem("acc_in"), 16)
            u = 0
            for t in (1, 2, 3, 4):
                n, w = (P, 128 * (t + 1)) if t < 4 else (TAIL, 528)
                for hd in range(AH):
                    dve.wait_ge(sem("rel_done"), u + 1)
                    if hd:
                        dve.wait_ge(sem("acc_done"), u)
                    v.scalar_tensor_tensor(acc_ap(t), rel[0:n, u % 2, 0:w], wi[0:n, t, hd:hd + 1], acc_ap(t),
                                           ALU.mult, ALU.add).then_inc(sem("acc_done"), 1)
                    u += 1
            dve.wait_ge(sem("ki_used"), 1)
            new_keys(2)
            new_keys(3)
            for ch in range(NCH):
                dve.wait_ge(sem("sw_full"), NCH + ch + 1)
                dve.wait_ge(sem("sw_g0"), ch + 1)
                o = sc[0:NS, ch * CH:(ch + 1) * CH]
                v.tensor_tensor(o, o, ps[0:NS, 6 + ch % 2, 0:CH], ALU.add).then_inc(sem("sw_g1"), 1)
            dve.wait_ge(sem("sw_g1"), NCH)
            o = sc[0:NS, PAST:KEYS]
            seq(v.tensor_tensor(o, o, c("tri4")[0:NS, :], ALU.add))
            dve.wait_ge(sem("acc_done"), u)
            with loop(dve, TOPK_P // 8, [(own, 8)]):
                for t in (1, 2, 3, 4):
                    n = P if t < 4 else TAIL
                    v.max(m8[0:n, 8 * (t - 1):8 * t], acc_ap(t)).then_inc(own.sem, 1)
                dve.wait_ge(own.sem, own.up(4))
                dve.sem_inc(sem("rounds"), 1)
                for t in (1, 2, 3, 4):
                    n = P if t < 4 else TAIL
                    v.match_replace(acc_ap(t), m8[0:n, 8 * (t - 1):8 * t], acc_ap(t), TAKEN).then_inc(own.sem, 1)
                dve.wait_ge(own.sem, own.up(4))
                dve.sem_inc(sem("rounds"), 1)
            for t in (1, 2, 3, 4):
                v.tensor_scalar(acc_ap(t), acc_ap(t), TAKEN / 2, NEVER, ALU.is_gt, ALU.mult).then_inc(own.sem, 1)
            dve.wait_ge(own.sem, own.up(4))
            with loop(dve, TOPK_S // 8, [(own, 2)]):
                seq(v.max(m8[0:NS, 0:8], sc[0:NS, :]))
                dve.sem_inc(sem("rounds"), 1)
                seq(v.match_replace(sc[0:NS, :], m8[0:NS, 0:8], sc[0:NS, :], TAKEN))
                dve.sem_inc(sem("rounds"), 1)
            seq(v.tensor_scalar(sc[0:NS, :], sc[0:NS, :], TAKEN / 2, NEVER, ALU.is_gt, ALU.mult))
            v.tensor_tensor(cmp16[0:NS, :].rearrange("p (b j) -> p b j", j=NQ),
                            sc[0:NS, PAST:KEYS].unsqueeze(1).broadcast_to([NS, NB, NQ]),
                            c("own")[0:NS, :].rearrange("p (b j) -> p b j", j=NQ), ALU.add) \
                .then_inc(sem("smask_done"), 1)
            dve.wait_ge(sem("masks_full"), 1)
            seq(v.tensor_copy(mask_t[:, 0:512], ps[:, 4, :]))
            v.tensor_copy(mask_t[0:NS, 512:544], ps[0:NS, 5, 0:NS]).then_inc(sem("masks_read"), 1)
            dve.wait_ge(sem("masks_read"), 1)
            dve.wait_ge(sem("rope_in"), 16)
            for u in range(8):
                dve.wait_ge(sem("rot_full"), u + 1)
                if u:
                    dve.wait_ge(sem("rope_done"), u)
                v.tensor_tensor(halves(zs), pair(u % 2), halves(sin_t), ALU.mult).then_inc(sem("zs_done"), 1)
                dve.wait_ge(sem("zs_done"), u + 1)
                dve.wait_ge(sem("zc_done"), u + 1)
                v.tensor_tensor(z[:, RQ + u, :], zc[:, u % 2, :], zs, ALU.add).then_inc(sem("rope_done"), 1)
            dve.wait_ge(sem("lg_done"), NB + 1)
            dve.wait_ge(sem("p16_done"), 1)
            for b in range(NB):
                o = lgt[:, b, 0:512].rearrange("p (g h q) -> p g h q", g=NPAGE, q=NQ)
                m = mask_t[:, 0:512].rearrange("p (g n) -> p g n", g=NPAGE)[:, :, b * NQ:(b + 1) * NQ]
                v.tensor_tensor(o, o, m.unsqueeze(2).broadcast_to([P, NPAGE, AH, NQ]), ALU.add)
            o = lgt[0:NS, :, 512:544].rearrange("p b (h q) -> p b h q", q=NQ)
            m = mask_t[0:NS, 512:544].rearrange("p (b q) -> p b q", q=NQ)
            v.tensor_tensor(o, o, m.unsqueeze(2).broadcast_to([NS, NB, AH, NQ]), ALU.add).then_inc(sem("mask_used"), 1)
            dve.wait_ge(sem("mask_used"), 1)

            def over_pages(func, b):
                return func(mx[:, b * 32:(b + 1) * 32], lgt[:, b, :].rearrange("p (g n) -> p n g", n=32), axis=AX.X)

            for b in range(NB):
                last = over_pages(v.reduce_max, b)
            last.then_inc(sem("mx_done"), 1)
            dve.wait_ge(sem("mxt_full"), 1)
            seq(v.reduce_max(mx2[:, :], ps[:, 5, 0:256].rearrange("p (g n) -> p g n", g=2), axis=AX.X))
            for g in range(2):
                last = v.tensor_scalar(diag[:, g * P:(g + 1) * P], ident, mx2[:, g:g + 1], None, ALU.mult)
            last.then_inc(sem("diag_done"), 1)
            dve.wait_ge(sem("mxb_full"), 1)
            for b in range(NB):
                o = lgt[:, b, :].rearrange("p (g n) -> p g n", n=32)
                m = ps[:, 4, b * 32:(b + 1) * 32].unsqueeze(1).broadcast_to([P, NPAGE + 1, 32])
                v.tensor_tensor(o, o, m, ALU.subtract).then_inc(sem("sub_done"), 1)
            for b in range(NB):
                dve.wait_ge(sem("sp_done"), b + 1)
                last = over_pages(v.reduce_sum, b)
            last.then_inc(sem("psum_done"), 1)
            dve.wait_ge(sem("sum_full"), 1)
            v.reciprocal(rsum, ps[:, 5, 0:256]).then_inc(sem("rsum_done"), 1)

            def h4(ap, n):
                return ap.rearrange("p (h m) -> p h m", h=RH)[:, :, 0:n]

            def ret_scale(cn, t0, n, dec_, xi_, zeta_):
                dve.wait_ge(sem("inner_full"), cn + 1)
                v.tensor_tensor(h4(it_b[0:n, :], n), h4(ps[0:n, 0, :], n), dec_, ALU.mult).then_inc(sem("it_done"), 1)
                v.tensor_tensor(xi_[0], z[:, RQ:RQ + 4, t0:t0 + n], xi_[1], ALU.mult).then_inc(sem("qx_done"), 1)
                dve.wait_ge(sem("kt_full"), cn + 1)
                v.tensor_tensor(h4(kz_b[0:n, :], P), h4(ps[0:n, 1, :], P), zeta_.unsqueeze(2).broadcast_to([n, RH, P]),
                                ALU.mult).then_inc(sem("kz_done"), 1)

            def group_norm(cn, n, o_ps):
                for hd in range(RH):
                    v.bn_stats(bn[0:n, 6 * hd:6 * hd + 6], o_ps(hd)).then_inc(own.sem, 1)
                dve.wait_ge(own.sem, own.up(4))
                for hd in range(RH):
                    last = v.bn_aggr(bag[0:n, 2 * hd:2 * hd + 2], bn[0:n, 6 * hd:6 * hd + 6])
                last.then_inc(sem("bag_done"), 1)
                dve.wait_ge(sem("bag_done"), cn + 1)
                dve.wait_ge(sem("rsd_done"), cn + 1)
                seq(v.reciprocal(rsd[0:n, :], rsd[0:n, :]))
                for hd in range(RH):
                    last = v.tensor_scalar(rn_b[0:n, hd * P:(hd + 1) * P], o_ps(hd), bag[0:n, 2 * hd:2 * hd + 1],
                                           rsd[0:n, hd:hd + 1], ALU.subtract, ALU.mult)
                last.then_inc(sem("rn_done"), 1)

            def gated(cn, t0, n, bank):
                dve.wait_ge(sem("rt_full"), cn + 1)
                v.tensor_tensor(mix[:, 4:8, t0:t0 + n], h4(ps[:, bank, :], n), z[:, G:G + 4, t0:t0 + n], ALU.mult) \
                    .then_inc(sem("mixr_done"), 1)

            dve.wait_ge(sem("ret_in"), 16)
            dve.wait_ge(sem("sg_done"), 1)
            dve.wait_ge(sem("rope_done"), 8)
            gam = c("gam")
            for cn in range(5):
                t0, n = (128 * cn, P) if cn < 4 else (TL, TAIL)
                ret_scale(cn, t0, n, h4(dec[0:n, :], n), (h4(qx_b, n), h4(xi, n)),
                          c("zeta") if cn < 4 else c("zetat")[0:n, :])
                dve.wait_ge(sem("rst_full"), cn + 1)
                if cn == 0:
                    v.tensor_copy(sr, ps[:, 3, :]).then_inc(sem("sr_done"), 1)
                else:
                    gg = gam[:, 0:4] if cn < 4 else gam[:, 4:8]
                    dve.wait_ge(sem("sr_done"), cn)
                    dve.wait_ge(sem("ro_full"), cn + 1)
                    seq(v.tensor_tensor(h4(sr, P), h4(sr, P), gg.unsqueeze(2).broadcast_to([P, RH, P]), ALU.mult))
                    v.tensor_tensor(sr, sr, ps[:, 3, :], ALU.add).then_inc(sem("sr_done"), 1)
                dve.wait_ge(sem("ro_full"), cn + 1)
                group_norm(cn, n, lambda hd: ps[0:n, 2, hd * P:(hd + 1) * P])
                gated(cn, t0, n, 4)
            qs = qx_b[:, 0:128].rearrange("p (h m) -> p h m", h=RH)
            ret_scale(5, SMP, NS, c("decs")[0:NS, :].rearrange("p (h m) -> p h m", h=RH),
                      (qs, c("xis").rearrange("p (h m) -> p h m", h=RH)), c("zetas")[0:NS, :])
            dve.wait_ge(sem("qx_done"), 6)
            dve.wait_ge(sem("kz_done"), 6)
            blk = c("blkrow").rearrange("p (b m) -> p b m", b=NB)

            def batch_parts(b):
                if b >= 2:
                    dve.wait_ge(sem("cross_full"), b - 1)
                v.tensor_tensor(qx_b[:, 256 + 128 * (b % 2):384 + 128 * (b % 2)].rearrange("p (h m) -> p h m", h=RH), qs,
                                blk[:, b, :].unsqueeze(1).broadcast_to([P, RH, NS]), ALU.mult).then_inc(sem("qxb_done"), 1)
                if b >= 2:
                    dve.wait_ge(sem("dst_full"), b - 1)
                o = rn_b[0:NS, :] if b % 2 else l_b[0:NS, 0, 0:512]
                v.tensor_scalar(o, kz_b[0:NS, :], c("blkcol")[0:NS, b:b + 1], None, ALU.mult).then_inc(sem("kzb_done"), 1)

            batch_parts(0)
            for b in range(NB):
                if b + 1 < NB:
                    batch_parts(b + 1)
                dve.wait_ge(sem("cross_full"), b + 1)
                o = st[:, b % 3, :]
                seq(v.tensor_tensor(h4(o, P), h4(o, P), gam[:, 8:12].unsqueeze(2).broadcast_to([P, RH, P]), ALU.mult))
                dve.wait_ge(sem("dst_full"), b + 1)
                v.tensor_tensor(o, o, ps[:, 2 + b % 2, :], ALU.add).then_inc(sem("st_new"), 1)
            group_norm(5, NS, lambda hd: ps[0:NS, 4 + hd, 0:P])
            gated(5, SMP, NS, 0)

            units = [(hd, t) for hd in range(AH) for t in range(5)]

            def logits(u, hd, t):
                p, n, w = u % 2, (P if t < 4 else TAIL), (128 * (t + 1) if t < 4 else 528)
                dve.wait_ge(sem("as_full"), u + 1)
                if u >= 2:
                    dve.wait_ge(sem("at_full"), u - 1)
                m = c("tri") if t == 0 else acc_ap(t)
                w0 = min(w, 512)
                last = v.scalar_tensor_tensor(l_b[0:n, p, 0:w0], ps[0:n, p, 0:w0], AD ** -0.5, m[:, 0:w0],
                                              ALU.mult, ALU.add)
                if t == 4:
                    last = v.scalar_tensor_tensor(l_b[0:n, p, 512:528], ps[0:n, 2, 0:TAIL], AD ** -0.5,
                                                  m[:, 512:528], ALU.mult, ALU.add)
                last.then_inc(sem("al_done"), 1)
                dve.wait_ge(sem("al_done"), u + 1)
                seq(v.reduce_max(smx[0:n, p:p + 1], l_b[0:n, p, 0:w], axis=AX.X))
                v.tensor_scalar(nmx[0:n, p:p + 1], smx[0:n, p:p + 1], -1.0, None, ALU.mult).then_inc(sem("nmx_done"), 1)

            def scaled(u, hd, t):
                p, n, w = u % 2, (P if t < 4 else TAIL), (128 * (t + 1) if t < 4 else 528)
                dve.wait_ge(sem("ae_done"), u + 1)
                seq(v.reciprocal(rcp[0:n, p:p + 1], ssum[0:n, p:p + 1]))
                v.tensor_scalar(l_b[0:n, p, 0:w], l_b[0:n, p, 0:w], rcp[0:n, p:p + 1], None, ALU.mult) \
                    .then_inc(sem("ap_done"), 1)

            def sample_out(b):
                dve.wait_ge(sem("so_full"), b + 1)
                a0 = small[:, 112:144]
                seq(v.tensor_copy(a0, ps[:, 3, 0:32]))
                seq(v.tensor_tensor(a0, a0, ps[:, 3, 32:64], ALU.add))
                seq(v.tensor_tensor(a0, a0, rsum[:, b * 32:(b + 1) * 32], ALU.mult))
                a1 = a0.rearrange("p (a n) -> p a n", a=4)
                for h2 in range(2):
                    lo = 64 * h2
                    v.tensor_copy(mix[lo:lo + 64, 0:4, SMP + b * NQ:SMP + (b + 1) * NQ],
                                  a1[lo:lo + 64, :, 4 * h2:4 * h2 + 4]).then_inc(sem("so_done"), 2)
                dve.wait_ge(sem("so_done"), 4 * (b + 1))

            dve.wait_ge(sem("rsum_done"), 1)
            for u in range(len(units) + 1):
                if u < len(units):
                    logits(u, *units[u])
                if u >= 1:
                    scaled(u - 1, *units[u - 1])
                if u % 5 == 0 and u >= 5:
                    sample_out(u // 5 - 1)
            for d in range(KT):
                dve.wait_ge(sem(f"w_free{d % 4}"), OUT_W[d % 4] + d // 4 + 1)
                v.scalar_tensor_tensor(halves(rs[1][:, d, :]), halves(x[:, d, :]), ALPHA, pair(d % 2), ALU.mult, ALU.add) \
                    .then_inc(sem("r_done"), 1)
            norm(1)
            ffn(1)

        @block.gpsimd
        def _(pool):
            pool.wait_ge(sem("sw_g1"), NCH)
            pool.memset(lgt[:, :, 512:544], NEVER).then_inc(sem("lg_init"), 1)
            pool.sem_inc(sem("index_done"), 1)
            for s in range(2):
                pool.wait_ge(sem(f"d_free{s}"), 4)
            for s in range(3):
                pool.dma_start(st[:, s, :], state[s]).then_inc(sem(f"st_in{s}"), 16)
            pool.wait_ge(sem("rope_in"), 16)
            pool.wait_ge(sem("z_done"), ZT)
            for u in range(8):
                if u >= 2:
                    pool.wait_ge(sem("rope_done"), u - 1)
                pool.tensor_tensor(zc[:, u % 2, :], z[:, RQ + u, :], cos_t, ALU.mult).then_inc(sem("zc_done"), 1)
            pool.wait_ge(sem("masks_read"), 1)
            pool.dma_start(sc[:, 0:1024], ret_tab).then_inc(sem("ret_in"), 16)
            pool.wait_ge(sem("sr_done"), 5)
            pool.dma_start(rp_o, sr).then_inc(sem("rp_out"), 16)
            for b in range(NB):
                pool.wait_ge(sem("st_new"), b + 1)
                pool.dma_start(rs_o[b], st[:, b % 3, :]).then_inc(sem(f"st_out{b % 3}"), 16)
                if b + 3 < NB:
                    pool.wait_ge(sem(f"st_out{b % 3}"), 16 * (b // 3 + 1))
                    pool.dma_start(st[:, b % 3, :], state[b + 3]).then_inc(sem(f"st_in{b % 3}"), 16)


OUT_W = [11 + 3 + 8, 11 + 2 + 8, 11 + 2 + 8, 11 + 2]


def _tables():
    f = np.float32
    cs = np.zeros((P, CONST_W), f)

    def put(name, a, rows=slice(None)):
        at, w = CONSTS[name]
        cs[rows, at:at + w] = a

    put("ident", np.eye(P))
    put("mean", 1.0 / D)
    put("ones", 1.0)
    rot = np.zeros((P, P), f)
    for m in range(64):
        rot[m + 64, m] = -1.0
        rot[m, m + 64] = 1.0
    put("rot", rot)
    n = np.arange(P)
    put("tri", np.where(n[None, :] <= n[:, None], 0.0, NEVER))
    sel = np.zeros((P, P), f)
    row = np.arange(P)
    sel[64 + (row // NQ) % AH, row] = 1.0
    put("sel", sel)
    mg = np.zeros((P, 2, NS), f)
    for g in range(2):
        mg[row, g, (4 * g + row // 32) * NQ + row % NQ] = AH ** -0.5
    put("maskg", mg.reshape(P, -1))
    own = np.arange(NS) // NQ
    put("blkrow", np.broadcast_to((own[None, :] == np.arange(NB)[:, None]).astype(f)[None], (P, NB, NS)).reshape(P, -1))
    lg = np.log(f(1.0) - f(2.0) ** (f(-5.0) - np.arange(RH, dtype=f))).astype(f).astype(np.float64)
    sc = P ** -0.5
    j = np.arange(NS) % NQ
    dj = j[None, :] - j[:, None]
    same = (own[:, None] == own[None, :]) & (dj >= 0)
    put("decs", np.stack([np.where(same, np.exp(dj * l) * sc, 0) for l in lg], 1).reshape(NS, -1), slice(0, NS))
    put("xis", np.broadcast_to(np.stack([np.exp((j + 1) * l) for l in lg]).reshape(1, -1), (P, RH * NS)))
    put("own", np.where(own[:, None] == own[None, :], 0.0, NEVER), slice(0, NS))
    put("tri4", np.where(np.arange(NQ)[None, :] <= j[:, None], 0.0, NEVER), slice(0, NS))
    put("zeta", np.exp((P - 1 - n)[:, None] * lg[None]) * sc)
    put("zetat", np.exp((TAIL - 1 - np.arange(TAIL))[:, None] * lg[None]) * sc, slice(0, TAIL))
    put("zetas", np.exp((NQ - 1 - j)[:, None] * lg[None]) * sc, slice(0, NS))
    put("gam", np.concatenate([np.exp(L * lg) for L in (P, TAIL, NQ)])[None])
    put("blkcol", (own[:, None] == np.arange(NB)[None]).astype(f), slice(0, NS))
    put("eps", EPS)
    pos = np.concatenate([np.arange(512), PAST + np.arange(NS) % NQ, 512 + np.arange(TAIL)]).astype(f)
    inv = (f(10000.0) ** (-np.arange(64, dtype=f) / f(64))).astype(f)
    ang = (pos[None, :] * inv[:, None]).astype(f)
    ang = np.concatenate([ang, ang])
    rope = np.concatenate([np.cos(ang), np.sin(ang)], 1).astype(f)
    d = n[None, :] - n[:, None]
    dec = np.stack([np.where(d >= 0, np.exp(np.maximum(d, 0) * l) * sc, 0) for l in lg], 1).reshape(P, -1)
    xi = np.broadcast_to(np.stack([np.exp((n + 1) * l) for l in lg]).reshape(1, -1), (P, RH * P))
    ret = np.concatenate([dec, xi], 1).astype(f)
    a0 = np.zeros((P, ACC_W), f)
    for t in (1, 2, 3):
        a0[:, ACC_AT[t] + 128 * t:ACC_AT[t] + 128 * (t + 1)] = np.where(n[None, :] <= n[:, None], 0.0, NEVER)
    a0[0:TAIL, ACC_AT[4] + 512:ACC_AT[4] + 528] = np.where(n[None, :TAIL] <= n[:TAIL, None], 0.0, NEVER)
    return cs, rope, ret, a0


def kernel(**inputs):
    import concourse.bacc as _bacc
    from concourse.bass_utils import run_bass_kernel_spmd as _run

    a = {k: np.asarray(v) for k, v in inputs.items()}

    def cols(xp, xs):
        return np.concatenate([xp[0:512], xs.reshape(NS, -1), xp[512:]], 0)

    def tiled(w):
        kk, nn = w.shape
        return w.reshape(kk // P, P, nn // P, P).transpose(2, 1, 0, 3).reshape(nn // P, P, kk)

    xt = cols(np.concatenate([a["meta_tokens"], a["x_prompt"][0]], 0), a["x_sample"])
    xt = xt.T.reshape(KT, P, T).transpose(1, 0, 2).reshape(P, KT * T)
    w = a["w_in"][0]
    o = np.cumsum([0, 512, 512, 512, 512, 64, 8, 512, 512, 512, 512])
    part = [w[:, o[i]:o[i + 1]] for i in range(10)]
    wp = np.concatenate([part[3], part[4], part[5], np.zeros((D, 56), w.dtype), part[0], part[1], part[2],
                         part[6], part[7], part[8], part[9]], 1)
    pool = a["cache_k"].shape[1]
    cs, rope, ret, a0 = _tables()
    at = CONSTS["ln"][0]
    ln = np.stack([a[f"ln{i}_{s}"][0].reshape(KT, P).T for i in (1, 2, 3) for s in "gb"], 1).reshape(P, 48)
    cs = np.concatenate([cs[:, :at], ln, cs[:, at + 48:]], 1)
    ins = dict(
        x_t=xt, wg1=tiled(a["ffn1_w_gate"][0]), wu1=tiled(a["ffn1_w_up"][0]), wd1=tiled(a["ffn1_w_down"][0]),
        wg2=tiled(a["ffn2_w_gate"][0]), wu2=tiled(a["ffn2_w_up"][0]), wd2=tiled(a["ffn2_w_down"][0]),
        w_in=tiled(wp), w_out=tiled(a["w_out"][0]),
        k_pool=a["cache_k"][0].reshape(pool, PAGE, 4, P).transpose(0, 3, 2, 1).reshape(pool, P, 512),
        v_pool=a["cache_v"][0].reshape(pool, PAGE, 512), i_pool=a["cache_idx_k"][0].transpose(0, 2, 1),
        state=a["state_ret"][0].transpose(0, 2, 1, 3).reshape(NB, P, 512),
        pages=a["page_table"].reshape(1, -1), consts=cs, rope_tab=rope, ret_tab=ret, acc_tab=a0)
    outs = dict(y_o=(KT, P, T), k_o=(P, 4, T), v_o=(P, 4, T), i_o=(64, T), rp_o=(P, 512), rs_o=(NB, P, 512))
    nc = _bacc.Bacc("TRN2", target_bir_lowering=False, num_devices=1)
    arrays, args = {}, {}
    for name, v in ins.items():
        v = np.ascontiguousarray(v)
        arrays["in_" + name] = v
        args[name] = nc.dram_tensor("in_" + name, v.shape, mybir.dt.from_np(v.dtype), kind="ExternalInput").ap()
    for name, shape in outs.items():
        args[name] = nc.dram_tensor("out_" + name, shape, F32, kind="ExternalOutput").ap()
    build(nc, **args)
    r = _run(nc, [arrays], core_ids=[0]).results[0]
    r = {k: r["out_" + k] for k in outs}

    def split(t):
        return np.concatenate([t[0:512], t[TL:T]], 0), t[SMP:TL]

    yp, ys = split(r["y_o"].reshape(D, T).T)
    kp, ks = split(r["k_o"].transpose(1, 0, 2).reshape(512, T).T)
    vp, vs_ = split(r["v_o"].transpose(1, 0, 2).reshape(512, T).T)
    ip, is_ = split(r["i_o"].T)
    L = SEQ + META
    res = (yp[META:].reshape(1, SEQ, D), ys.reshape(NB, NQ, D),
           kp.reshape(1, 1, L, AH, AD), vp.reshape(1, 1, L, AH, AD), ip.reshape(1, 1, L, AD),
           r["rp_o"].reshape(P, RH, P).transpose(1, 0, 2).reshape(1, 1, RH, P, P),
           ks.reshape(1, NB, NQ, AH, AD), vs_.reshape(1, NB, NQ, AH, AD), is_.reshape(1, NB, NQ, AD),
           r["rs_o"].reshape(NB, P, RH, P).transpose(0, 2, 1, 3).reshape(1, NB, RH, P, P))
    return tuple(np.ascontiguousarray(t) for t in res)
```

```python
from contextlib import ExitStack, contextmanager

import numpy as np
import concourse.bass as bass
from concourse import mybir

ALU = mybir.AluOpType
ACT = mybir.ActivationFunctionType
AX = mybir.AxisListType
F32 = mybir.dt.float32
F32R = mybir.dt.float32r
I32 = mybir.dt.int32

P = 128
D, SEQ, META, DFF = 1024, 512, 16, 2816
NB, NQ, PAST, PAGE = 8, 4, 2048, 128
NPAGE = PAST // PAGE
NS = NB * NQ
TAIL = SEQ + META - 512
T = 512 + NS + TAIL
HALF = T // 2
SMP, TL = 512, 512 + NS
KT, FT = D // P, DFF // P
AH, AD, RH = 8, 64, 4
TOPK_P, TOPK_S = 128, 256
ALPHA = 2.0 ** 0.25
EPS = 1e-5
QI, KW, Q, K, V, RQ, RK, RV, G, ZT = 0, 4, 5, 9, 13, 17, 21, 25, 29, 33
FIRST = 9
NEVER, TAKEN = -1e30, -3e38
KEYS = PAST + NQ
CUT = [0, 5, 10, NPAGE]
DOWN = [1024, 1024, 768]
FF_W = [FT // 2 + KT] * 3 + [FT // 2]
CH, NCH = KEYS // 6, 6
LGW = (NPAGE + 1) * 32
ACC_AT = [None, 0, 256, 640, 1152]
ACC_W = 1680

CONSTS = {}
_at = 0
for _n, _w in (("ident", 128), ("mean", 128), ("ones", 128), ("rot", 128), ("tri", 128), ("sel", 128),
               ("maskg", 64), ("blkrow", 256), ("decs", 128), ("xis", 128), ("own", 32), ("tri4", 4),
               ("zeta", 4), ("zetat", 4), ("zetas", 4), ("gam", 12), ("blkcol", 8), ("hsel", 8), ("ln", 48), ("eps", 1)):
    CONSTS[_n] = (_at, _w)
    _at += _w
CONST_W = _at


@contextmanager
def loop(eng, count, steps):
    start = [(t, t.n, k) for t, k in steps]
    with eng.Fori(0, count) as i:
        for t, n, k in start:
            t.n = i * k + n
        yield i
    for t, n, k in start:
        t.n = n + count * k


class Tally:

    def __init__(self, sem, n=0):
        self.sem, self.n = sem, n

    def up(self, k=1):
        self.n = self.n + k
        return self.n


def build(nc, x_t, wg1, wu1, wd1, wg2, wu2, wd2, w_in, w_out, k_pool, v_pool, i_pool, state, pages,
          consts, rope_tab, ret_tab, acc_tab, y_o, k_o, v_o, i_o, rp_o, rs_o):
    wgs, wus, wds = [wg1, wg2], [wu1, wu2], [wd1, wd2]
    with ExitStack() as ctx:
        def sb(name, cols, dt=F32):
            return ctx.enter_context(nc.sbuf_tensor(name, [P, cols], dt))

        sems = {}

        def sem(name):
            if name not in sems:
                sems[name] = ctx.enter_context(nc.semaphore(name))
            return sems[name]

        xbuf = sb("xbuf", KT * T)
        rbuf_at = nc.sbuf_base
        rbuf = sb("rbuf", KT * T)
        h_at = nc.sbuf_base
        big, dring, mask_t = sb("big", ZT * T), sb("dring", 5632), sb("mask_t", LGW)
        assert 2 * FT * T <= ZT * T + 5632 + LGW
        wring = sb("wring", 4 * 1024)
        lg_at = nc.sbuf_base
        lg, sc, mxb = sb("lg", NB * LGW), sb("sc", KEYS), sb("mxb", 512)
        assert KT * T + 2048 <= NB * LGW + KEYS + 512
        acc = sb("acc", ACC_W)
        scr_at = nc.sbuf_base
        scr = sb("scr", 4144)
        cst = sb("cst", CONST_W)
        wi_t, wsel, qibd, qbd = sb("wi_t", 40), sb("wsel", 64), sb("qibd", 256), sb("qbd", 256)
        small = sb("small", 160)

        def over(name, cols, offset):
            return nc.alloc_sbuf_tensor_at(name, [P, cols], F32R, offset=offset)

        h_high, h_low = over("h_high", FT * T, h_at), over("h_low", FT * T, h_at + FT * T * 4)
        x_high, x_low = over("x_high", KT * T, rbuf_at), over("x_low", KT * T, lg_at)
        w_high, w_low = over("w_high", 2048, scr_at + 2 * T * 4), over("w_low", 2048, lg_at + KT * T * 4)

        pt = ctx.enter_context(nc.sbuf_tensor("pt", [1, NB * NPAGE], I32))
        ps = ctx.enter_context(nc.psum_tensor("ps", [P, 8, 512], F32))

        def c(name):
            a, w = CONSTS[name]
            return cst[:, a:a + w]

        def tiles(buf, n, at=0):
            return buf[:, at:at + n * T].rearrange("p (k t) -> p k t", t=T)

        x, r0, z = tiles(xbuf, KT), tiles(rbuf, KT), tiles(big, ZT)
        rbig, mix = tiles(big, KT), r0
        rs = [r0, rbig, r0]

        def halves(ap):
            return ap.rearrange("p (a n) -> p a n", a=2)

        def pair(p):
            return ps[:, 2 * p:2 * p + 2, 0:HALF]

        ident, ones = c("ident"), c("ones")
        lng = c("ln").rearrange("p (n k) -> p n k", n=6)
        xh, xl, hh, hl = tiles(x_high, KT), tiles(x_low, KT), tiles(h_high, FT), tiles(h_low, FT)
        wh, wl = (w[:, :].rearrange("p (s n) -> p s n", s=2) for w in (w_high, w_low))
        w4 = wring[:, :].rearrange("p (s n) -> p s n", s=4)
        kv = dring[:, 0:4096].rearrange("p (s n) -> p s n", s=8)
        st = dring[:, 4096:5632].rearrange("p (s n) -> p s n", s=3)
        s_buf = tiles(scr, 2)
        sq = tiles(scr, 2, 4 * T)
        rstd = scr[:, 6 * T:7 * T]
        kid = scr[:, 0:T]
        rel = scr[:, T:T + 1056].rearrange("p (s n) -> p s n", s=2)
        rl = scr[:, T + 1056:T + 1056 + KEYS]
        kis = [buf[:, 0:2 * KEYS].rearrange("p (s n) -> p s n", s=2) for buf in (lg, rbuf)]
        qib = qibd[:, :].rearrange("p (r n) -> p r n", r=4)
        qb = qbd[:, :].rearrange("p (a b n) -> p a b n", a=4, b=NB)
        wi = wi_t[:, :].rearrange("p (t h) -> p t h", h=8)
        ws = wsel[:, :].rearrange("p (g n) -> p g n", g=2)
        lgt = lg[:, :].rearrange("p (b n) -> p b n", b=NB)
        cos_t, sin_t = scr[:, 0:T], scr[:, T:2 * T]
        zc = tiles(scr, 2, 2 * T)
        zs = scr[:, 4 * T:5 * T]
        diag = scr[:, 5 * T:5 * T + 256]
        it_b, kz_b, qx_b, rn_b = (scr[:, 512 * j:512 * (j + 1)] for j in range(4))
        l_b = scr[:, 2048:2048 + 1056].rearrange("p (s n) -> p s n", s=2)
        pt_b = scr[:, 3104:3104 + 1024].rearrange("p (s n) -> p s n", s=2)
        dec, xi, sr = (sc[:, 512 * j:512 * (j + 1)] for j in range(3))
        vt = big[:, 0:2048].rearrange("p (t n) -> p t n", t=4)
        vr = wring[:, 0:2048].rearrange("p (t n) -> p t n", t=4)
        vrs, vrt, vs, vtl = (wring[:, 2048 + 512 * j:2048 + 512 * (j + 1)] for j in range(4))
        mx, rsum = mxb[:, 0:256], mxb[:, 256:258]
        smx, ssum, nmx, rcp = small[:, 0:2], small[:, 2:4], small[:, 4:6], small[:, 6:8]
        m8, mx2, bn, bag, rsd, cmp16 = (small[:, 8:40], small[:, 40:42], small[:, 42:66], small[:, 66:74],
                                        small[:, 74:78], small[:, 80:112])

        def acc_ap(t):
            w = 128 * (t + 1) if t < 4 else 528
            return acc[0:(P if t < 4 else TAIL), ACC_AT[t]:ACC_AT[t] + w]

        block = ctx.enter_context(nc.Block())

        def page_reg(eng, at):
            return eng.value_load(pt[0:1, bass.ds(at, 1)], min_val=0, max_val=k_pool.shape[0] - 1)

        def index_pages(eng, pr):
            if pr >= 2:
                eng.wait_ge(sem("x_done"), KT)
            for b2 in range(2):
                with eng.Fori(0, NPAGE // 4) as i:
                    for j in range(4):
                        pg = page_reg(eng, i * 4 + (2 * pr + b2) * NPAGE + j)
                        eng.dma_start(kis[pr // 2][64 * b2:64 * b2 + 64, pr % 2, bass.ds(i * (4 * PAGE) + j * PAGE, PAGE)],
                                      i_pool[bass.ds(pg, 1)].rearrange("a p n -> (a p) n")) \
                            .then_inc(sem(f"ki_in{pr}"), 16)

        @block.sync
        def _(sp):
            free = [Tally(sem(f"w_free{s}")) for s in range(4)]
            sp.dma_start(pt[:, :], pages).then_inc(sem("pages_in"), 16)

            def weight(s, src, first=False):
                if not first:
                    sp.wait_ge(free[s].sem, free[s].up())
                sp.dma_start(w4[:, s, :], src).then_inc(sem(f"w_in{s}"), 16)

            def down_chunk(s, src):
                sp.wait_ge(free[s].sem, free[s].up())
                sp.dma_start(w4[:, s, 0:DOWN[s]], src[:, s * 1024:s * 1024 + DOWN[s]]).then_inc(sem(f"w_in{s}"), 16)

            def ffn_loads(m):
                for s in range(4):
                    f, up = divmod(s, 2)
                    weight(s, (wus if up else wgs)[m][f], first=(m == 0))
                with loop(sp, FT // 2 - 1, [(f, 1) for f in free]) as i:
                    for s in range(4):
                        f, up = divmod(s, 2)
                        weight(s, (wus if up else wgs)[m][bass.ds(i * 2 + 2 + f, 1)].rearrange("a p n -> (a p) n"))
                for s in range(3):
                    down_chunk(s, wds[m][0])
                with loop(sp, KT - 1, [(f, 1) for f in free[:3]]) as i:
                    for s in range(3):
                        down_chunk(s, wds[m][bass.ds(i + 1, 1)].rearrange("a p n -> (a p) n"))

            ffn_loads(0)
            sp.wait_ge(sem("pages_in"), 16)
            for t in range(FIRST):
                weight(t % 4, w_in[t])
                if t == 3:
                    index_pages(sp, 3)
            sp.wait_ge(sem("w_free2"), FF_W[2])
            kvf = [Tally(sem(f"kv_free{s}")) for s in range(8)]

            def kv_page(s, at, pool, first=False):
                if not first:
                    sp.wait_ge(kvf[s].sem, kvf[s].up())
                pg = page_reg(sp, at)
                sp.dma_start(kv[:, s, :], pool[bass.ds(pg, 1)].rearrange("a p n -> (a p) n")) \
                    .then_inc(sem(f"kv_in{s}"), 16)

            for j in range(3):
                weight(j, w_in[FIRST + j])
                for s in range(CUT[j], CUT[j + 1]):
                    kv_page(s % 8, s, k_pool, first=(s < 8))
            with loop(sp, NB - 1, [(f, 1) for f in free[:3]] + [(f, 2) for f in kvf]) as i:
                for j in range(3):
                    weight(j, w_in[bass.ds(i * 3 + FIRST + 3 + j, 1)].rearrange("a p n -> (a p) n"))
                    for s in range(CUT[j], CUT[j + 1]):
                        kv_page(s % 8, i * NPAGE + NPAGE + s, k_pool)
            sp.wait_ge(sem("index_done"), 1)
            sp.dma_start(scr[:, 0:2 * T], rope_tab).then_inc(sem("rope_in"), 16)
            sp.wait_ge(sem("z_done"), ZT)
            sp.dma_start(k_o, z[:, K:K + 4, :]).then_inc(sem("kvi_out"), 16)
            sp.dma_start(v_o, z[:, V:V + 4, :]).then_inc(sem("kvi_out"), 16)
            sp.dma_start(i_o, z[0:64, KW, :]).then_inc(sem("kvi_out"), 16)
            with loop(sp, NB * 2, [(f, 1) for f in kvf]) as i:
                for s in range(8):
                    kv_page(s, i * 8 + s, v_pool)
            sp.wait_ge(sem("mix_read"), 1)
            for s in range(4):
                weight(s, w_out[s])
            for s in range(4):
                weight(s, w_out[s + 4])
            ffn_loads(1)
            with sp.Fori(0, KT) as i:
                sp.wait_ge(sem("x_done"), i + 2 * KT + 1)
                sp.dma_start(y_o[bass.ds(i, 1)].rearrange("a p n -> (a p) n"),
                             x[:, bass.ds(i, 1), :].rearrange("p a n -> p (a n)")).then_inc(sem("y_out"), 16)
            sp.wait_ge(sem("y_out"), 16 * KT)
            sp.wait_ge(sem("kvi_out"), 48)
            sp.wait_ge(sem("rp_out"), 16)
            for s in range(3):
                sp.wait_ge(sem(f"st_out{s}"), 16 * ((NB - s + 2) // 3))

        @block.tensor
        def _(pe):
            w_in_t = [Tally(sem(f"w_in{s}")) for s in range(4)]
            kv_in_t = [Tally(sem(f"kv_in{s}")) for s in range(8)]
            hdone, rdone = Tally(sem("h_done")), Tally(sem("r_done"))
            zdone = Tally(sem("z_done"))
            pe.sem_inc(sem("sq_free"), 2)

            def mm(out, lhs, rhs, start=True, stop=True, **kw):
                return nc.tensor.matmul(out, lhs, rhs, start=start, stop=stop, **kw)

            def tr(out, in_, k0, k1):
                return nc.tensor.transpose(out, in_, ident[k0:k1, k0:k1])

            def wide(p, wt, kn, src):
                for a in range(2):
                    for k in range(kn):
                        last = mm(ps[:, 2 * p + a, 0:HALF], wt[:, k * P:(k + 1) * P],
                                  src[:, k, a * HALF:(a + 1) * HALF], k == 0, k == kn - 1)
                return last

            def weight(s):
                pe.wait_ge(w_in_t[s].sem, w_in_t[s].up(16))

            def wide_split(p, s, high, low, k0=0, kn=KT, total=KT):
                for a in range(2):
                    for k in range(kn):
                        for j, (w_, x_) in enumerate(((wh, high), (wh, low), (wl, high))):
                            last = mm(ps[:, 2 * p + a, 0:HALF], w_[:, s, k * P:(k + 1) * P],
                                      x_[:, k0 + k, a * HALF:(a + 1) * HALF], k0 + k + j == 0,
                                      k0 + k == total - 1 and j == 2)
                return last

            def ffn(m):
                hdone.n = FT * m
                pe.wait_ge(sem("xl_done"), KT * (m + 1))
                wl_done = Tally(sem("wl_done"), (2 * FT + 3 * KT) * m)
                for w, n in zip(w_in_t, FF_W):
                    w.up(16 * n)
                with loop(pe, FT // 2, [(wl_done, 4), (hdone, 2)]):
                    for j in range(2):
                        pe.wait_ge(sem("h_done"), hdone.up())
                        for up in range(2):
                            pe.wait_ge(sem("wl_done"), wl_done.up())
                            wide_split(2 * up + j, up, xh, xl).then_inc(sem(f"w_free{2 * j + up}"), 1)
                pe.wait_ge(sem("h_done"), 1 + FT * (m + 1))
                pe.wait_ge(sem("hl_done"), FT * m + 16)
                rdone.n = KT * 2 * m
                with loop(pe, KT // 2, [(wl_done, 6), (rdone, 2)]):
                    for j in range(2):
                        pe.wait_ge(sem("r_done"), rdone.up())
                        for s in range(3):
                            if s == 2:
                                pe.wait_ge(sem("hl_done"), FT * (m + 1))
                            pe.wait_ge(sem("wl_done"), wl_done.up())
                            wide_split(j, (j + s) % 2, hh, hl, 8 * s, DOWN[s] // P, FT).then_inc(sem(f"w_free{s}"), 1)
                norm(2 * m)

            def norm(n):
                r = rs[n]
                for d in range(KT):
                    pe.wait_ge(sem("r_done"), 2 + KT * n + d + 1)
                    for a in range(2):
                        last = mm(ps[:, 4 + a, 0:HALF], c("mean"), r[:, d, a * HALF:(a + 1) * HALF],
                                  d == 0, d == KT - 1)
                last.then_inc(sem("mean_full"), 1)
                for d in range(KT):
                    pe.wait_ge(sem("sq_done"), KT * n + d + 1)
                    for a in range(2):
                        last = mm(ps[:, 6 + a, 0:HALF], c("mean"), sq[:, d % 2, a * HALF:(a + 1) * HALF],
                                  d == 0, d == KT - 1)
                    last.then_inc(sem("sq_free"), 1)
                pe.wait_ge(sem("x_done"), KT * (n + 1))

            pe.wait_ge(sem("x_in"), 16)
            pe.wait_ge(sem("cst_in"), 16)
            ffn(0)

            def first_tile(t):
                weight(t % 4)
                if t >= 2:
                    pe.wait_ge(sem("z_done"), t - 1)
                wide(t % 2, w4[:, t % 4, :], KT, x).then_inc(sem(f"w_free{t % 4}"), 1)

            for t in range(Q):
                first_tile(t)
            pe.wait_ge(sem("z_done"), Q)
            for t in (1, 2, 3):
                tr(ps[:, 6, 64 * t:64 * t + 64], z[64:128, KW, 128 * t:128 * t + 128], 64, 128)
            tr(ps[0:TAIL, 6, 0:64], z[64:128, KW, TL:T], 64, 128)
            mm(ps[:, 7, 0:NS], c("sel")[64:128, :], z[64:128, KW, SMP:TL]).then_inc(sem("prep_full"), 1)
            pe.wait_ge(sem("kid_done"), 2)
            u = 0
            for t in (1, 2, 3, 4):
                first_tile(Q + t - 1)
                if t == 4:
                    pe.wait_ge(sem("wi_done"), 1)
                for hd in range(AH):
                    lo = 64 * (hd % 2)
                    p = u % 2
                    if u >= 2:
                        pe.wait_ge(sem("rel_done"), u - 1)
                    q0, n, nk = (128 * t, P, 128 * (t + 1)) if t < 4 else (TL, TAIL, 512)
                    last = mm(ps[0:n, 4 + p, 0:nk], z[lo:lo + 64, QI + hd // 2, q0:q0 + n], kid[lo:lo + 64, 0:nk])
                    if t == 4:
                        if u >= 1:
                            pe.wait_ge(sem("rel_done"), u)
                        last = mm(ps[0:n, 6, 0:TAIL], z[lo:lo + 64, QI + hd // 2, q0:q0 + n], kid[lo:lo + 64, TL:T])
                    last.then_inc(sem("s_full"), 1)
                    u += 1
            pe.wait_ge(sem("z_done"), FIRST)
            pe.wait_ge(sem("qib_done"), 1)
            pe.wait_ge(sem("rel_done"), u)
            pe.wait_ge(sem("wsel_done"), 1)
            pe.wait_ge(sem("wi_done"), 1)
            for g in range(2):
                for j in range(2):
                    pe.wait_ge(sem(f"ki_in{2 * g + j}"), 16 * 2 * NPAGE)
                    pe.wait_ge(sem("kin_done"), 2 * g + j + 1)
                for ch in range(NCH):
                    if g:
                        pe.wait_ge(sem("rl_done"), ch + 1)
                    for j in range(2):
                        last = mm(ps[64 * j:64 * j + 64, ch, 0:CH], qib[:, 2 * g + j, :],
                                  kis[g][:, j, ch * CH:(ch + 1) * CH])
                    last.then_inc(sem("ss_full"), 1)
                for ch in range(NCH):
                    pe.wait_ge(sem("rl_done"), NCH * g + ch + 1)
                    k = NCH * g + ch
                    if k >= 2:
                        s_, v_ = ("sw_g0", k - 1) if k - 2 < NCH else ("sw_g1", k - 1 - NCH)
                        pe.wait_ge(sem(s_), v_)
                    mm(ps[0:NS, 6 + ch % 2, 0:CH], ws[:, g, :], rl[:, ch * CH:(ch + 1) * CH]) \
                        .then_inc(sem("sw_full"), 1)
            pe.wait_ge(sem("sw_g1"), NCH)
            pe.wait_ge(sem("qb_done"), 1)
            zdone.n = FIRST - 2 - 1
            lgd = Tally(sem("lg_done"))
            with loop(pe, NB, [(w, 16) for w in w_in_t[:3]] + [(k_, 32) for k_ in kv_in_t] + [(zdone, 3), (lgd, 1)]) as i:
                for j in range(3):
                    weight(j)
                    pe.wait_ge(sem("z_done"), zdone.up())
                    wide(j, w4[:, j, :], KT, x).then_inc(sem(f"w_free{j}"), 1)
                    if j == 0:
                        pe.wait_ge(sem("lg_done"), lgd.up())
                    for pg in range(CUT[j], CUT[j + 1]):
                        s = pg % 8
                        pe.wait_ge(kv_in_t[s].sem, kv_in_t[s].up(16))
                        for hp in range(4):
                            last = mm(ps[:, 6, pg * 32 + hp * 8:pg * 32 + hp * 8 + 8], kv[:, s, hp * P:(hp + 1) * P],
                                      qb[:, hp, bass.ds(i, 1), :].rearrange("p a n -> p (a n)"))
                        last.then_inc(sem(f"kv_free{s}"), 1)
            pe.wait_ge(sem("z_done"), ZT)
            for hp in range(4):
                last = mm(ps[0:NS, 7, hp * 64:hp * 64 + 64], z[:, K + hp, SMP:TL],
                          qb[:, hp, :, :].rearrange("p b n -> p (b n)"))
            last.then_inc(sem("p16_full"), 1)
            k = 0
            for src in (V, RV):
                for t0, n in [(128 * t, P) for t in range(4)] + [(SMP, NS), (TL, TAIL)]:
                    if k >= 4:
                        pe.wait_ge(sem("tr_done"), k - 3)
                    for j in range(4):
                        last = tr(ps[0:n, k % 4, j * P:(j + 1) * P], z[:, src + j, t0:t0 + n], 0, P)
                    last.then_inc(sem("tr_full"), 1)
                    k += 1
            pe.wait_ge(sem("tr_done"), 12)
            pe.wait_ge(sem("lg_done"), NB + 1)
            pe.wait_ge(sem("smask_done"), 1)
            for pg in range(NPAGE):
                tr(ps[:, 4, pg * NS:(pg + 1) * NS], sc[0:NS, pg * PAGE:(pg + 1) * PAGE], 0, NS)
            tr(ps[0:NS, 5, 0:NS], cmp16[0:NS, :], 0, NS).then_inc(sem("masks_full"), 1)
            for u in range(8):
                if u >= 2:
                    pe.wait_ge(sem("zs_done"), u - 1)
                for a in range(2):
                    last = mm(ps[:, 2 * (u % 2) + a, 0:HALF], c("rot"), z[:, RQ + u, a * HALF:(a + 1) * HALF])
                last.then_inc(sem("rot_full"), 1)
            pe.wait_ge(sem("mask_used"), 1)
            pe.wait_ge(sem("mx_done"), 1)
            for g in range(2):
                last = tr(ps[:, 5, g * P:(g + 1) * P], mx[:, g * P:(g + 1) * P], 0, P)
            last.then_inc(sem("mxt_full"), 1)
            pe.wait_ge(sem("diag_done"), 1)
            mm(ps[:, 4, 0:256], ones, diag).then_inc(sem("mxb_full"), 1)
            pe.wait_ge(sem("psum_done"), 1)
            for g in range(2):
                last = mm(ps[:, 5, g:g + 1], mx[:, g * P:(g + 1) * P], ones[:, 0:1])
            last.then_inc(sem("sum_full"), 1)
            pe.wait_ge(sem("rsum_done"), 1)
            pe.wait_ge(sem("rope_done"), 8)

            def ret_in(cn, t0, n):
                for hd in range(RH):
                    last = mm(ps[0:n, 0, hd * P:hd * P + n], z[:, RK + hd, t0:t0 + n], z[:, RQ + hd, t0:t0 + n])
                last.then_inc(sem("inner_full"), 1)
                for hd in range(RH):
                    last = tr(ps[0:n, 1, hd * P:(hd + 1) * P], z[:, RK + hd, t0:t0 + n], 0, P)
                last.then_inc(sem("kt_full"), 1)

            def ret_out(cn, n):
                pe.wait_ge(sem("rn_done"), cn + 1)
                for hd in range(RH):
                    last = tr(ps[:, 4, hd * P:hd * P + n], rn_b[0:n, hd * P:(hd + 1) * P], 0, n)
                last.then_inc(sem("rt_full"), 1)

            for cn in range(5):
                t0, n = (128 * cn, P) if cn < 4 else (TL, TAIL)
                vv = vr[:, cn, :] if cn < 4 else vrt
                ret_in(cn, t0, n)
                pe.wait_ge(sem("it_done"), cn + 1)
                pe.wait_ge(sem("qx_done"), cn + 1)
                if cn:
                    pe.wait_ge(sem("sr_done"), cn)
                for hd in range(RH):
                    o = ps[0:n, 2, hd * P:(hd + 1) * P]
                    last = mm(o, it_b[0:n, hd * P:hd * P + n], vv[0:n, hd * P:(hd + 1) * P], True, cn == 0)
                    if cn:
                        last = mm(o, qx_b[:, hd * P:hd * P + n], sr[:, hd * P:(hd + 1) * P], False, True)
                last.then_inc(sem("ro_full"), 1)
                pe.wait_ge(sem("kz_done"), cn + 1)
                for hd in range(RH):
                    last = mm(ps[:, 3, hd * P:(hd + 1) * P], kz_b[0:n, hd * P:(hd + 1) * P],
                              vv[0:n, hd * P:(hd + 1) * P])
                last.then_inc(sem("rst_full"), 1)
                ret_out(cn, n)
                pe.wait_ge(sem("mixr_done"), cn + 1)
            ret_in(5, SMP, NS)
            pe.wait_ge(sem("it_done"), 6)
            for hd in range(RH):
                mm(ps[0:NS, 4 + hd, 0:P], it_b[0:NS, hd * P:hd * P + NS], vrs[0:NS, hd * P:(hd + 1) * P], True, False)
            for b in range(NB):
                pe.wait_ge(sem("qxb_done"), b + 1)
                pe.wait_ge(sem(f"st_in{b % 3}"), 16 * (b // 3 + 1))
                for hd in range(RH):
                    last = mm(ps[0:NS, 4 + hd, 0:P], qx_b[:, 128 * (b % 2) + hd * NS + 256:128 * (b % 2) + (hd + 1) * NS + 256],
                              st[:, b % 3, hd * P:(hd + 1) * P], False, b == NB - 1)
                last.then_inc(sem("cross_full"), 1)
                pe.wait_ge(sem("kzb_done"), b + 1)
                if b >= 2:
                    pe.wait_ge(sem("st_new"), b - 1)
                for hd in range(RH):
                    last = mm(ps[:, 2 + b % 2, hd * P:(hd + 1) * P],
                              rn_b[0:NS, hd * P:(hd + 1) * P] if b % 2 else l_b[0:NS, 0, hd * P:(hd + 1) * P],
                              vrs[0:NS, hd * P:(hd + 1) * P])
                last.then_inc(sem("dst_full"), 1)
            pe.wait_ge(sem("rn_done"), 6)
            for hd in range(RH):
                last = tr(ps[:, 0, hd * P:hd * P + NS], rn_b[0:NS, hd * P:(hd + 1) * P], 0, NS)
            last.then_inc(sem("rt_full"), 1)
            pe.wait_ge(sem("mixr_done"), 6)
            pe.wait_ge(sem("st_new"), NB)

            units = [(hd, t) for hd in range(AH) for t in range(5)]

            def scores(u, hd, t):
                lo, p = 64 * (hd % 2), u % 2
                q0, n, nk = (128 * t, P, 128 * (t + 1)) if t < 4 else (TL, TAIL, 512)
                if u >= 2:
                    pe.wait_ge(sem("al_done"), u - 1)
                last = mm(ps[0:n, p, 0:nk], z[lo:lo + 64, Q + hd // 2, q0:q0 + n], z[lo:lo + 64, K + hd // 2, 0:nk])
                if t == 4:
                    last = mm(ps[0:n, 2, 0:TAIL], z[lo:lo + 64, Q + hd // 2, q0:q0 + n],
                              z[lo:lo + 64, K + hd // 2, TL:T])
                last.then_inc(sem("as_full"), 1)

            def turn(u, hd, t):
                p, n = u % 2, (P if t < 4 else TAIL)
                pe.wait_ge(sem("ap_done"), u + 1)
                if u >= 2:
                    pe.wait_ge(sem("apt_done"), u - 1)
                for j in range(t + 1 if t < 4 else 4):
                    last = tr(ps[:, 4 + p, j * n:(j + 1) * n], l_b[0:n, p, j * P:(j + 1) * P], 0, n)
                if t == 4:
                    last = tr(ps[0:TAIL, 4 + p, 4 * n:5 * n], l_b[0:n, p, 512:512 + TAIL], 0, n)
                last.then_inc(sem("at_full"), 1)

            def values(u, hd, t):
                p, n, lo = u % 2, (P if t < 4 else TAIL), 64 * (hd % 2)
                pe.wait_ge(sem("apt_done"), u + 1)
                if u >= 2:
                    pe.wait_ge(sem("ao_done"), u - 1)
                nj = t + 1 if t < 4 else 5
                for j in range(nj):
                    lhs = vt[:, j, hd * AD:(hd + 1) * AD] if j < 4 else vtl[0:TAIL, hd * AD:(hd + 1) * AD]
                    rhs = pt_b[:, p, j * n:(j + 1) * n] if j < 4 else pt_b[0:TAIL, p, 4 * n:5 * n]
                    last = mm(ps[lo:lo + 64, 6 + p, 0:n], lhs, rhs, j == 0, j == nj - 1)
                last.then_inc(sem("ao_full"), 1)

            def sample_values(n):
                b, pg = divmod(n, NPAGE)
                if n == 0:
                    pe.wait_ge(sem("sp_done"), NB)
                if n == 4 * NPAGE:
                    pe.wait_ge(sem("so_read"), 1)
                o = ps[32 * (b % 4):32 * (b % 4) + 32, 3, :]
                s_ = pg % 8
                pe.wait_ge(kv_in_t[s_].sem, kv_in_t[s_].up(16))
                mm(o, lgt[:, b, pg * 32:(pg + 1) * 32], kv[:, s_, :], pg == 0, False).then_inc(sem(f"kv_free{s_}"), 1)
                if pg == NPAGE - 1:
                    last = mm(o, lgt[0:NS, b, 512:544], vs[0:NS, :], False, True)
                    if b % 4 == 3:
                        last.then_inc(sem("so_full"), 1)

            def sample_turn(g):
                pe.wait_ge(sem("so_att"), g + 1)
                if g:
                    pe.wait_ge(sem("so_done"), 2 * g)
                tr(ps[0:64, 5, 0:P] if g else ps[0:64, 3, 0:P], kz_b[:, 64 * g:64 * g + 64], 0, P) \
                    .then_inc(sem("so_turned"), 1)

            parts = 0
            for u in range(len(units) + 2):
                if u < len(units):
                    scores(u, *units[u])
                if u >= 2:
                    values(u - 2, *units[u - 2])
                half = NPAGE * NB // 2 if u <= len(units) // 2 else NPAGE * NB
                while u < len(units) and parts < half and parts * len(units) < (u + 1) * NPAGE * NB:
                    sample_values(parts)
                    parts += 1
                if 1 <= u <= len(units):
                    turn(u - 1, *units[u - 1])
                if u == len(units) // 2:
                    sample_turn(0)
            sample_turn(1)
            pe.wait_ge(sem("ao_done"), len(units))
            pe.wait_ge(sem("so_done"), 4)
            pe.sem_inc(sem("mix_read"), 1)

            for d in range(KT):
                weight(d % 4)
                pe.wait_ge(sem("r_done"), KT + d + 1)
                wide(d % 2, w4[:, d % 4, :], KT, mix).then_inc(sem(f"w_free{d % 4}"), 1)
            norm(1)
            ffn(1)

        @block.scalar
        def _(act):
            act.sem_inc(sem("lg_done"), 1)
            act.dma_start(xbuf[:, :], x_t).then_inc(sem("x_in"), 16)
            act.dma_start(cst[:, :], consts).then_inc(sem("cst_in"), 16)
            act.dma_start(acc[:, :], acc_tab).then_inc(sem("acc_in"), 16)
            act.wait_ge(sem("cst_in"), 16)

            def ev(out, in_, func=ACT.Copy, **kw):
                return nc.scalar.activation(out, in_, func, **kw)

            def weight_high(s, to, n=1024):
                act.wait_ge(w_in_t[s].sem, w_in_t[s].up(16))
                ev(wh[:, to, 0:n], w4[:, s, 0:n]).then_inc(sem("wh_done"), 1)

            def ffn(m):
                frees = [Tally(sem(f"w_free{s}"), seen[m][s]) for s in range(4)]

                def hidden(f, j, down=False):
                    for up in range(2):
                        w = frees[2 * j + up]
                        act.wait_ge(w.sem, w.up())
                        weight_high(up if down else 2 * (1 - j) + up, up)
                    ev(halves(s_buf[:, j, :]), pair(j), ACT.Silu).then_inc(sem("s_done"), 1)
                    act.wait_ge(hdone.sem, hdone.up())
                    ev(hh[:, bass.ds(f, 1), :].rearrange("p a n -> p (a n)"), s_buf[:, j, :]).then_inc(sem("hh_done"), 1)

                def output(j, more=True):
                    for s in range(3):
                        w = frees[s]
                        act.wait_ge(w.sem, w.up())
                        if more or s == 0:
                            nxt = (s + 2) % 3
                            weight_high(nxt, (j + s) % 2, DOWN[nxt])
                    ev(halves(s_buf[:, j, :]), pair(j), scale=0.5).then_inc(sem("y_done"), 1)

                hdone = Tally(sem("h_done"), 2 + FT * m)
                with loop(act, FT // 2 - 1, [(w, 1) for w in frees] + [(w, 16) for w in w_in_t] + [(hdone, 2)]) as i:
                    hidden(i * 2, 0)
                    hidden(i * 2 + 1, 1)
                hidden(FT - 2, 0)
                hidden(FT - 1, 1, True)
                with loop(act, KT // 2 - 1, [(w, 2) for w in frees[:3]] + [(w, 32) for w in w_in_t[:3]]):
                    output(0)
                    output(1)
                output(0)
                output(1, False)
                norm(2 * m)

            def norm(n):
                r = rs[n]
                cd, sf = Tally(sem("c_done"), KT * n), Tally(sem("sq_free"), KT * n)
                with loop(act, KT // 2, [(cd, 2), (sf, 2)]) as i:
                    for j in range(2):
                        act.wait_ge(cd.sem, cd.up())
                        act.wait_ge(sf.sem, sf.up())
                        ev(sq[:, j, :], r[:, bass.ds(i * 2 + j, 1), :].rearrange("p a n -> p (a n)"), ACT.Square) \
                            .then_inc(sem("sq_done"), 1)
                act.wait_ge(sem("sq_free"), 2 + KT * (n + 1))
                ev(halves(rstd), pair(3), ACT.Sqrt, bias=c("eps")).then_inc(sem("std_done"), 1)
                if n == 1:
                    weight_high(0, 0)
                    weight_high(1, 1)
                nd = Tally(sem("n_done"), KT * n)
                with loop(act, KT, [(nd, 1)]) as i:
                    act.wait_ge(nd.sem, nd.up())
                    if n == 1:
                        ev(xh[:, bass.ds(i, 1), :].rearrange("p a n -> p (a n)"),
                           r[:, bass.ds(i, 1), :].rearrange("p a n -> p (a n)"), ACT.Identity,
                           scale=lng[:, 2, bass.ds(i, 1)], bias=lng[:, 3, bass.ds(i, 1)])
                    ev(x[:, bass.ds(i, 1), :].rearrange("p a n -> p (a n)"),
                       r[:, bass.ds(i, 1), :].rearrange("p a n -> p (a n)"), ACT.Identity,
                       scale=lng[:, 2 * n, bass.ds(i, 1)], bias=lng[:, 2 * n + 1, bass.ds(i, 1)]) \
                        .then_inc(sem("x_done"), 1)

            seen = [[0] * 4, [OUT_W[s] + 2 for s in range(4)]]
            w_in_t = [Tally(sem(f"w_in{s}")) for s in range(4)]
            act.wait_ge(sem("x_in"), 16)
            weight_high(0, 0)
            for k in range(KT):
                ev(xh[:, k, :], x[:, k, :]).then_inc(sem("xh_done"), 1)
            weight_high(1, 1)
            ffn(0)
            def first_tile(t):
                act.wait_ge(sem(f"w_free{t % 4}"), FF_W[t % 4] + t // 4 + 1)
                if t == KW:
                    for lo in (0, 64):
                        ev(halves(kid[lo:lo + 64, :]), ps[0:64, 2 * (t % 2):2 * (t % 2) + 2, 0:HALF]) \
                            .then_inc(sem("kid_done"), 1)
                ev(halves(z[:, t, :]), pair(t % 2)).then_inc(sem("z_done"), 1)

            for t in range(Q):
                first_tile(t)
            act.wait_ge(sem("prep_full"), 1)
            for t in (1, 2, 3):
                ev(wi[:, t, :], ps[:, 6, 64 * t:64 * t + 8], scale=AH ** -0.5)
            ev(wi[0:TAIL, 4, :], ps[0:TAIL, 6, 0:8], scale=AH ** -0.5).then_inc(sem("wi_done"), 1)
            u = 0
            for t in (1, 2, 3, 4):
                first_tile(Q + t - 1)
                for hd in range(AH):
                    n, nk = (P, 128 * (t + 1)) if t < 4 else (TAIL, 512)
                    act.wait_ge(sem("s_full"), u + 1)
                    if u >= 2:
                        act.wait_ge(sem("acc_done"), u - 1)
                    last = ev(rel[0:n, u % 2, 0:nk], ps[0:n, 4 + u % 2, 0:nk], ACT.Relu, scale=AD ** -0.5)
                    if t == 4:
                        last = ev(rel[0:n, u % 2, 512:512 + TAIL], ps[0:n, 6, 0:TAIL], ACT.Relu, scale=AD ** -0.5)
                    last.then_inc(sem("rel_done"), 1)
                    u += 1
            for g in range(2):
                for ch in range(NCH):
                    act.wait_ge(sem("ss_full"), NCH * g + ch + 1)
                    if g:
                        act.wait_ge(sem("sw_full"), ch + 1)
                    ev(rl[:, ch * CH:(ch + 1) * CH], ps[:, ch, 0:CH], ACT.Relu, scale=AD ** -0.5) \
                        .then_inc(sem("rl_done"), 1)
                if g == 0:
                    for ch in range(NCH):
                        act.wait_ge(sem("sw_full"), ch + 1)
                        ev(sc[0:NS, ch * CH:(ch + 1) * CH], ps[0:NS, 6 + ch % 2, 0:CH]).then_inc(sem("sw_g0"), 1)
            wf = [Tally(sem(f"w_free{s}"), FF_W[s] + (3 if s == 0 else 2)) for s in range(3)]
            kf = Tally(sem("kv_free7"))
            with loop(act, NB, [(w, 1) for w in wf] + [(kf, 2)]) as i:
                for j in range(3):
                    act.wait_ge(wf[j].sem, wf[j].up())
                    ev(halves(z[:, bass.ds(i * 3 + FIRST + j, 1), :].rearrange("p a n -> p (a n)")), pair(j)) \
                        .then_inc(sem("z_done"), 1)
                act.wait_ge(kf.sem, kf.up(2))
                ev(lgt[:, bass.ds(i, 1), 0:512].rearrange("p a n -> p (a n)"), ps[:, 6, :], scale=AD ** -0.5) \
                    .then_inc(sem("lg_done"), 1)
            act.wait_ge(sem("p16_full"), 1)
            act.wait_ge(sem("lg_init"), 1)
            for hp in range(4):
                last = ev(lgt[0:NS, :, 512 + hp * 8:512 + hp * 8 + 8],
                          ps[0:NS, 7, hp * 64:hp * 64 + 64].rearrange("p (b n) -> p b n", b=NB), scale=AD ** -0.5)
            last.then_inc(sem("p16_done"), 1)
            k = 0
            for src in (V, RV):
                for t in range(6):
                    n = P if t < 4 else (NS, TAIL)[t - 4]
                    dst = ((vt, vs, vtl) if src == V else (vr, vrs, vrt))
                    o = dst[0][:, t, :] if t < 4 else dst[t - 3][0:n, :]
                    act.wait_ge(sem("tr_full"), k + 1)
                    ev(o, ps[0:n, k % 4, :]).then_inc(sem("tr_done"), 1)
                    k += 1
            for j in range(4):
                act.wait_ge(sem("z_done"), ZT)
                last = ev(z[:, G + j, :], z[:, G + j, :], ACT.Silu)
            last.then_inc(sem("sg_done"), 1)
            for b in range(NB):
                act.wait_ge(sem("sub_done"), b + 1)
                ev(lgt[:, b, :], lgt[:, b, :], ACT.Exp).then_inc(sem("sp_done"), 1)
            for cn in range(6):
                n = P if cn < 4 else (TAIL, NS)[cn - 4]
                act.wait_ge(sem("bag_done"), cn + 1)
                ev(rsd[0:n, :], bag[0:n, 1::2], ACT.Sqrt, bias=c("eps")[0:n, :]).then_inc(sem("rsd_done"), 1)
            units = [(hd, t) for hd in range(AH) for t in range(5)]

            def probs(u, hd, t):
                p, n, w = u % 2, (P if t < 4 else TAIL), (128 * (t + 1) if t < 4 else 528)
                act.wait_ge(sem("nmx_done"), u + 1)
                ev(l_b[0:n, p, 0:w], l_b[0:n, p, 0:w], ACT.Exp, bias=nmx[0:n, p:p + 1],
                   accum_out=ssum[0:n, p:p + 1]).then_inc(sem("ae_done"), 1)

            def turned(u, hd, t):
                p, n = u % 2, (P if t < 4 else TAIL)
                act.wait_ge(sem("at_full"), u + 1)
                if u >= 2:
                    act.wait_ge(sem("ao_full"), u - 1)
                w = (t + 1 if t < 4 else 4) * n
                last = ev(pt_b[:, p, 0:w], ps[:, 4 + p, 0:w])
                if t == 4:
                    last = ev(pt_b[0:TAIL, p, 4 * n:5 * n], ps[0:TAIL, 4 + p, 4 * n:5 * n])
                last.then_inc(sem("apt_done"), 1)

            def out(u, hd, t):
                p, n, lo, q0 = u % 2, (P if t < 4 else TAIL), 64 * (hd % 2), (128 * t if t < 4 else TL)
                act.wait_ge(sem("ao_full"), u + 1)
                ev(mix[lo:lo + 64, hd // 2, q0:q0 + n], ps[lo:lo + 64, 6 + p, 0:n]).then_inc(sem("ao_done"), 1)

            for u in range(len(units) + 2):
                if u < len(units):
                    probs(u, *units[u])
                if 1 <= u <= len(units):
                    turned(u - 1, *units[u - 1])
                if u >= 2:
                    out(u - 2, *units[u - 2])
            w_in_t = [Tally(sem(f"w_in{s}"), 16 * seen[1][s]) for s in range(4)]
            norm(1)
            act.wait_ge(sem("kvi_out"), 48)
            ffn(1)

        @block.vector
        def _(dve):
            v = nc.vector
            own = Tally(sem("dve_own"))

            def seq(ins):
                ins.then_inc(own.sem, 1)
                dve.wait_ge(own.sem, own.up())

            dve.sem_inc(sem("h_done"), 2)
            dve.sem_inc(sem("r_done"), 2)
            seq(v.memset(qibd[:, :], 0.0))
            seq(v.memset(qbd[:, :], 0.0))
            dve.wait_ge(sem("cst_in"), 16)

            def row(ap, i):
                return ap[:, bass.ds(i, 1), :].rearrange("p a n -> p (a n)")

            wh_done = Tally(sem("wh_done"))

            def weight_low(s, to, n=1024):
                dve.wait_ge(wh_done.sem, wh_done.up())
                v.tensor_tensor(wl[:, to, 0:n], w4[:, s, 0:n], wh[:, to, 0:n].bitcast(F32), ALU.subtract) \
                    .then_inc(sem("wl_done"), 1)

            def x_lows(ready):
                for k in range(KT):
                    dve.wait_ge(ready, k + 1 if ready is sem("xh_done") else KT + k + 1)
                    v.tensor_tensor(xl[:, k, :], x[:, k, :], xh[:, k, :].bitcast(F32), ALU.subtract) \
                        .then_inc(sem("xl_done"), 1)

            def ffn(m):
                weight_low(0, 0)
                x_lows(sem("x_done") if m else sem("xh_done"))
                weight_low(1, 1)
                sd, hd = Tally(sem("s_done"), FT * m), Tally(sem("hh_done"), FT * m)

                def hidden(f, j, down=False):
                    for up in range(2):
                        weight_low(up if down else 2 * (1 - j) + up, up)
                    dve.wait_ge(sd.sem, sd.up())
                    v.tensor_tensor(halves(s_buf[:, j, :]), halves(s_buf[:, j, :]), pair(2 + j), ALU.mult) \
                        .then_inc(sem("h_done"), 1)
                    dve.wait_ge(hd.sem, hd.up())
                    v.tensor_tensor(row(hl, f), s_buf[:, j, :], row(hh, f).bitcast(F32), ALU.subtract) \
                        .then_inc(sem("hl_done"), 1)

                def output(d, j, more=True):
                    for s in range(3):
                        if more or s == 0:
                            nxt = (s + 2) % 3
                            weight_low(nxt, (j + s) % 2, DOWN[nxt])
                    dve.wait_ge(yd.sem, yd.up())
                    v.scalar_tensor_tensor(row(rs[2 * m], d), row(x, d), ALPHA, s_buf[:, j, :],
                                           ALU.mult, ALU.add).then_inc(sem("r_done"), 1)

                with loop(dve, FT // 2 - 1, [(sd, 2), (wh_done, 4), (hd, 2)]) as i:
                    hidden(i * 2, 0)
                    hidden(i * 2 + 1, 1)
                hidden(FT - 2, 0)
                hidden(FT - 1, 1, True)
                yd = Tally(sem("y_done"), KT * m)
                with loop(dve, KT // 2 - 1, [(yd, 2), (wh_done, 6)]) as i:
                    output(i * 2, 0)
                    output(i * 2 + 1, 1)
                output(KT - 2, 0)
                output(KT - 1, 1, False)
                norm(2 * m)

            def norm(n):
                r = rs[n]
                dve.wait_ge(sem("mean_full"), n + 1)
                dve.wait_ge(sem("r_done"), 2 + KT * (n + 1))
                with dve.Fori(0, KT) as i:
                    v.tensor_tensor(halves(row(r, i)), halves(row(r, i)), pair(2), ALU.subtract) \
                        .then_inc(sem("c_done"), 1)
                dve.wait_ge(sem("std_done"), n + 1)
                dve.wait_ge(sem("c_done"), KT * (n + 1))
                seq(v.reciprocal(rstd, rstd))
                with dve.Fori(0, KT) as i:
                    v.tensor_tensor(row(r, i), row(r, i), rstd, ALU.mult).then_inc(sem("n_done"), 1)

            ffn(0)
            dve.wait_ge(sem("z_done"), 4)
            for b2 in range(2):
                for par in range(2):
                    o = qib[64 * b2:64 * b2 + 64, :, 32 * b2:32 * b2 + 32] \
                        .rearrange("p r (a two q) -> p r a two q", two=2, q=NQ)
                    s_ = z[64 * par:64 * par + 64, QI:QI + 4, SMP:TL].rearrange("p a (r two q) -> p r a two q", two=2, q=NQ)
                    for a in range(4):
                        last = v.tensor_copy(o[:, :, a, par, :], s_[:, :, a, b2, :])
            last.then_inc(sem("qib_done"), 1)
            def new_keys(pr):
                for b2 in range(2):
                    lo = 64 * b2
                    c0 = SMP + (2 * pr + b2) * NQ
                    last = v.tensor_copy(kis[pr // 2][lo:lo + 64, pr % 2, PAST:KEYS], kid[lo:lo + 64, c0:c0 + NQ])
                last.then_inc(sem("kin_done"), 1)

            dve.wait_ge(sem("kid_done"), 2)
            for pr in range(4):
                new_keys(pr)
            def pair_queries():
                dve.wait_ge(sem("z_done"), FIRST)
                for h2 in range(2):
                    lo = 64 * h2
                    last = v.tensor_copy(qb[lo:lo + 64, :, :, 4 * h2:4 * h2 + 4],
                                         z[lo:lo + 64, Q:Q + 4, SMP:TL].rearrange("p a (b q) -> p a b q", q=NQ))
                last.then_inc(sem("qb_done"), 1)

            dve.wait_ge(sem("prep_full"), 1)
            for g in range(2):
                last = v.tensor_tensor(ws[:, g, :], ps[:, 7, 0:NS], c("maskg")[:, g * NS:(g + 1) * NS], ALU.mult)
            last.then_inc(sem("wsel_done"), 1)
            dve.wait_ge(sem("wi_done"), 1)
            dve.wait_ge(sem("acc_in"), 16)
            u = 0
            for t in (1, 2, 3, 4):
                n, w = (P, 128 * (t + 1)) if t < 4 else (TAIL, 528)
                for hd in range(AH):
                    dve.wait_ge(sem("rel_done"), u + 1)
                    if hd:
                        dve.wait_ge(sem("acc_done"), u)
                    v.scalar_tensor_tensor(acc_ap(t), rel[0:n, u % 2, 0:w], wi[0:n, t, hd:hd + 1], acc_ap(t),
                                           ALU.mult, ALU.add).then_inc(sem("acc_done"), 1)
                    u += 1
            pair_queries()
            for ch in range(NCH):
                dve.wait_ge(sem("sw_full"), NCH + ch + 1)
                dve.wait_ge(sem("sw_g0"), ch + 1)
                o = sc[0:NS, ch * CH:(ch + 1) * CH]
                v.tensor_tensor(o, o, ps[0:NS, 6 + ch % 2, 0:CH], ALU.add).then_inc(sem("sw_g1"), 1)
            dve.wait_ge(sem("sw_g1"), NCH)
            o = sc[0:NS, PAST:KEYS]
            seq(v.tensor_tensor(o, o, c("tri4")[0:NS, :], ALU.add))
            dve.wait_ge(sem("acc_done"), u)
            with loop(dve, TOPK_P // 8, [(own, 8)]):
                for t in (1, 2, 3, 4):
                    n = P if t < 4 else TAIL
                    v.max(m8[0:n, 8 * (t - 1):8 * t], acc_ap(t)).then_inc(own.sem, 1)
                dve.wait_ge(own.sem, own.up(4))
                dve.sem_inc(sem("rounds"), 1)
                for t in (1, 2, 3, 4):
                    n = P if t < 4 else TAIL
                    v.match_replace(acc_ap(t), m8[0:n, 8 * (t - 1):8 * t], acc_ap(t), TAKEN).then_inc(own.sem, 1)
                dve.wait_ge(own.sem, own.up(4))
                dve.sem_inc(sem("rounds"), 1)
            for t in (1, 2, 3, 4):
                v.tensor_scalar(acc_ap(t), acc_ap(t), TAKEN / 2, NEVER, ALU.is_gt, ALU.mult).then_inc(own.sem, 1)
            dve.wait_ge(own.sem, own.up(4))
            with loop(dve, TOPK_S // 8, [(own, 2)]):
                seq(v.max(m8[0:NS, 0:8], sc[0:NS, :]))
                dve.sem_inc(sem("rounds"), 1)
                seq(v.match_replace(sc[0:NS, :], m8[0:NS, 0:8], sc[0:NS, :], TAKEN))
                dve.sem_inc(sem("rounds"), 1)
            seq(v.tensor_scalar(sc[0:NS, :], sc[0:NS, :], TAKEN / 2, NEVER, ALU.is_gt, ALU.mult))
            v.tensor_tensor(cmp16[0:NS, :].rearrange("p (b j) -> p b j", j=NQ),
                            sc[0:NS, PAST:KEYS].unsqueeze(1).broadcast_to([NS, NB, NQ]),
                            c("own")[0:NS, :].rearrange("p (b j) -> p b j", j=NQ), ALU.add) \
                .then_inc(sem("smask_done"), 1)
            dve.wait_ge(sem("masks_full"), 1)
            seq(v.tensor_copy(mask_t[:, 0:512], ps[:, 4, :]))
            v.tensor_copy(mask_t[0:NS, 512:544], ps[0:NS, 5, 0:NS]).then_inc(sem("masks_read"), 1)
            dve.wait_ge(sem("masks_read"), 1)
            dve.wait_ge(sem("rope_in"), 16)
            for u in range(8):
                dve.wait_ge(sem("rot_full"), u + 1)
                if u:
                    dve.wait_ge(sem("rope_done"), u)
                v.tensor_tensor(halves(zs), pair(u % 2), halves(sin_t), ALU.mult).then_inc(sem("zs_done"), 1)
                dve.wait_ge(sem("zs_done"), u + 1)
                dve.wait_ge(sem("zc_done"), u + 1)
                v.tensor_tensor(z[:, RQ + u, :], zc[:, u % 2, :], zs, ALU.add).then_inc(sem("rope_done"), 1)
            dve.wait_ge(sem("lg_done"), NB + 1)
            dve.wait_ge(sem("p16_done"), 1)
            for b in range(NB):
                o = lgt[:, b, 0:512].rearrange("p (g h q) -> p g h q", g=NPAGE, q=NQ)
                m = mask_t[:, 0:512].rearrange("p (g n) -> p g n", g=NPAGE)[:, :, b * NQ:(b + 1) * NQ]
                v.tensor_tensor(o, o, m.unsqueeze(2).broadcast_to([P, NPAGE, AH, NQ]), ALU.add)
            o = lgt[0:NS, :, 512:544].rearrange("p b (h q) -> p b h q", q=NQ)
            m = mask_t[0:NS, 512:544].rearrange("p (b q) -> p b q", q=NQ)
            v.tensor_tensor(o, o, m.unsqueeze(2).broadcast_to([NS, NB, AH, NQ]), ALU.add).then_inc(sem("mask_used"), 1)
            dve.wait_ge(sem("mask_used"), 1)

            def over_pages(func, b):
                return func(mx[:, b * 32:(b + 1) * 32], lgt[:, b, :].rearrange("p (g n) -> p n g", n=32), axis=AX.X)

            for b in range(NB):
                last = over_pages(v.reduce_max, b)
            last.then_inc(sem("mx_done"), 1)
            dve.wait_ge(sem("mxt_full"), 1)
            seq(v.reduce_max(mx2[:, :], ps[:, 5, 0:256].rearrange("p (g n) -> p g n", g=2), axis=AX.X))
            for g in range(2):
                last = v.tensor_scalar(diag[:, g * P:(g + 1) * P], ident, mx2[:, g:g + 1], None, ALU.mult)
            last.then_inc(sem("diag_done"), 1)
            dve.wait_ge(sem("mxb_full"), 1)
            for b in range(NB):
                o = lgt[:, b, :].rearrange("p (g n) -> p g n", n=32)
                m = ps[:, 4, b * 32:(b + 1) * 32].unsqueeze(1).broadcast_to([P, NPAGE + 1, 32])
                v.tensor_tensor(o, o, m, ALU.subtract).then_inc(sem("sub_done"), 1)
            for b in range(NB):
                dve.wait_ge(sem("sp_done"), b + 1)
                last = over_pages(v.reduce_sum, b)
            last.then_inc(sem("psum_done"), 1)
            dve.wait_ge(sem("sum_full"), 1)
            v.reciprocal(rsum, ps[:, 5, 0:2]).then_inc(sem("rsum_done"), 1)

            def h4(ap, n):
                return ap.rearrange("p (h m) -> p h m", h=RH)[:, :, 0:n]

            def ret_scale(cn, t0, n, dec_, xi_, zeta_):
                dve.wait_ge(sem("inner_full"), cn + 1)
                v.tensor_tensor(h4(it_b[0:n, :], n), h4(ps[0:n, 0, :], n), dec_, ALU.mult).then_inc(sem("it_done"), 1)
                v.tensor_tensor(xi_[0], z[:, RQ:RQ + 4, t0:t0 + n], xi_[1], ALU.mult).then_inc(sem("qx_done"), 1)
                dve.wait_ge(sem("kt_full"), cn + 1)
                v.tensor_tensor(h4(kz_b[0:n, :], P), h4(ps[0:n, 1, :], P), zeta_.unsqueeze(2).broadcast_to([n, RH, P]),
                                ALU.mult).then_inc(sem("kz_done"), 1)

            def group_norm(cn, n, o_ps):
                for hd in range(RH):
                    v.bn_stats(bn[0:n, 6 * hd:6 * hd + 6], o_ps(hd)).then_inc(own.sem, 1)
                dve.wait_ge(own.sem, own.up(4))
                for hd in range(RH):
                    last = v.bn_aggr(bag[0:n, 2 * hd:2 * hd + 2], bn[0:n, 6 * hd:6 * hd + 6])
                last.then_inc(sem("bag_done"), 1)
                dve.wait_ge(sem("bag_done"), cn + 1)
                dve.wait_ge(sem("rsd_done"), cn + 1)
                seq(v.reciprocal(rsd[0:n, :], rsd[0:n, :]))
                for hd in range(RH):
                    last = v.tensor_scalar(rn_b[0:n, hd * P:(hd + 1) * P], o_ps(hd), bag[0:n, 2 * hd:2 * hd + 1],
                                           rsd[0:n, hd:hd + 1], ALU.subtract, ALU.mult)
                last.then_inc(sem("rn_done"), 1)

            def gated(cn, t0, n, bank):
                dve.wait_ge(sem("rt_full"), cn + 1)
                v.tensor_tensor(mix[:, 4:8, t0:t0 + n], h4(ps[:, bank, :], n), z[:, G:G + 4, t0:t0 + n], ALU.mult) \
                    .then_inc(sem("mixr_done"), 1)

            dve.wait_ge(sem("ret_in"), 16)
            dve.wait_ge(sem("sg_done"), 1)
            dve.wait_ge(sem("rope_done"), 8)
            gam = c("gam")
            for cn in range(5):
                t0, n = (128 * cn, P) if cn < 4 else (TL, TAIL)
                ret_scale(cn, t0, n, h4(dec[0:n, :], n), (h4(qx_b, n), h4(xi, n)),
                          c("zeta") if cn < 4 else c("zetat")[0:n, :])
                dve.wait_ge(sem("rst_full"), cn + 1)
                if cn == 0:
                    v.tensor_copy(sr, ps[:, 3, :]).then_inc(sem("sr_done"), 1)
                else:
                    gg = gam[:, 0:4] if cn < 4 else gam[:, 4:8]
                    dve.wait_ge(sem("sr_done"), cn)
                    dve.wait_ge(sem("ro_full"), cn + 1)
                    seq(v.tensor_tensor(h4(sr, P), h4(sr, P), gg.unsqueeze(2).broadcast_to([P, RH, P]), ALU.mult))
                    v.tensor_tensor(sr, sr, ps[:, 3, :], ALU.add).then_inc(sem("sr_done"), 1)
                dve.wait_ge(sem("ro_full"), cn + 1)
                group_norm(cn, n, lambda hd: ps[0:n, 2, hd * P:(hd + 1) * P])
                gated(cn, t0, n, 4)
            qs = qx_b[:, 0:128].rearrange("p (h m) -> p h m", h=RH)
            ret_scale(5, SMP, NS, c("decs")[0:NS, :].rearrange("p (h m) -> p h m", h=RH),
                      (qs, c("xis").rearrange("p (h m) -> p h m", h=RH)), c("zetas")[0:NS, :])
            dve.wait_ge(sem("qx_done"), 6)
            dve.wait_ge(sem("kz_done"), 6)
            blk = c("blkrow").rearrange("p (b m) -> p b m", b=NB)

            def batch_parts(b):
                if b >= 2:
                    dve.wait_ge(sem("cross_full"), b - 1)
                v.tensor_tensor(qx_b[:, 256 + 128 * (b % 2):384 + 128 * (b % 2)].rearrange("p (h m) -> p h m", h=RH), qs,
                                blk[:, b, :].unsqueeze(1).broadcast_to([P, RH, NS]), ALU.mult).then_inc(sem("qxb_done"), 1)
                if b >= 2:
                    dve.wait_ge(sem("dst_full"), b - 1)
                o = rn_b[0:NS, :] if b % 2 else l_b[0:NS, 0, 0:512]
                v.tensor_scalar(o, kz_b[0:NS, :], c("blkcol")[0:NS, b:b + 1], None, ALU.mult).then_inc(sem("kzb_done"), 1)

            batch_parts(0)
            for b in range(NB):
                if b + 1 < NB:
                    batch_parts(b + 1)
                dve.wait_ge(sem("cross_full"), b + 1)
                o = st[:, b % 3, :]
                seq(v.tensor_tensor(h4(o, P), h4(o, P), gam[:, 8:12].unsqueeze(2).broadcast_to([P, RH, P]), ALU.mult))
                dve.wait_ge(sem("dst_full"), b + 1)
                v.tensor_tensor(o, o, ps[:, 2 + b % 2, :], ALU.add).then_inc(sem("st_new"), 1)
            group_norm(5, NS, lambda hd: ps[0:NS, 4 + hd, 0:P])
            gated(5, SMP, NS, 0)

            units = [(hd, t) for hd in range(AH) for t in range(5)]

            def logits(u, hd, t):
                p, n, w = u % 2, (P if t < 4 else TAIL), (128 * (t + 1) if t < 4 else 528)
                dve.wait_ge(sem("as_full"), u + 1)
                if u >= 2:
                    dve.wait_ge(sem("at_full"), u - 1)
                m = c("tri") if t == 0 else acc_ap(t)
                w0 = min(w, 512)
                last = v.scalar_tensor_tensor(l_b[0:n, p, 0:w0], ps[0:n, p, 0:w0], AD ** -0.5, m[:, 0:w0],
                                              ALU.mult, ALU.add)
                if t == 4:
                    last = v.scalar_tensor_tensor(l_b[0:n, p, 512:528], ps[0:n, 2, 0:TAIL], AD ** -0.5,
                                                  m[:, 512:528], ALU.mult, ALU.add)
                last.then_inc(sem("al_done"), 1)
                dve.wait_ge(sem("al_done"), u + 1)
                seq(v.reduce_max(smx[0:n, p:p + 1], l_b[0:n, p, 0:w], axis=AX.X))
                v.tensor_scalar(nmx[0:n, p:p + 1], smx[0:n, p:p + 1], -1.0, None, ALU.mult).then_inc(sem("nmx_done"), 1)

            def scaled(u, hd, t):
                p, n, w = u % 2, (P if t < 4 else TAIL), (128 * (t + 1) if t < 4 else 528)
                dve.wait_ge(sem("ae_done"), u + 1)
                seq(v.reciprocal(rcp[0:n, p:p + 1], ssum[0:n, p:p + 1]))
                v.tensor_scalar(l_b[0:n, p, 0:w], l_b[0:n, p, 0:w], rcp[0:n, p:p + 1], None, ALU.mult) \
                    .then_inc(sem("ap_done"), 1)

            def sample_out(g):
                dve.wait_ge(sem("so_full"), g + 1)
                rows, att = rn_b.rearrange("p (h d) -> p h d", h=AH), kz_b[:, 64 * g:64 * g + 64]
                v.scalar_tensor_tensor(rows, ps[:, 3, :].rearrange("p (h d) -> p h d", h=AH), rsum[:, g:g + 1],
                                       c("hsel").unsqueeze(2).broadcast_to([P, AH, AD]), ALU.mult, ALU.mult) \
                    .then_inc(own.sem, 1)
                dve.wait_ge(own.sem, own.up())
                v.reduce_sum(att, rn_b.rearrange("p (h d) -> p d h", h=AH), axis=AX.X).then_inc(sem("so_att"), 1)
                dve.wait_ge(sem("so_att"), g + 1)
                dve.wait_ge(sem("so_turned"), g + 1)
                t = ps[0:64, 5 if g else 3, 0:P].rearrange("p (b a two q) -> p a b two q", b=4, two=2, q=NQ)
                for h2 in range(2):
                    lo = 64 * h2
                    o = mix[lo:lo + 64, 0:4, SMP + g * 16:SMP + (g + 1) * 16].rearrange("p a (b q) -> p a b q", q=NQ)
                    v.tensor_copy(o, t[:, :, :, h2, :]).then_inc(sem("so_done"), 1)
                dve.wait_ge(sem("so_done"), 2 * (g + 1))
                dve.sem_inc(sem("so_read"), 1)

            dve.wait_ge(sem("rsum_done"), 1)
            for u in range(len(units) + 1):
                if u < len(units):
                    logits(u, *units[u])
                if u >= 1:
                    scaled(u - 1, *units[u - 1])
                if u == len(units) // 2:
                    sample_out(0)
            sample_out(1)
            for d in range(KT):
                dve.wait_ge(sem(f"w_free{d % 4}"), OUT_W[d % 4] + d // 4 + 1)
                v.scalar_tensor_tensor(halves(rs[1][:, d, :]), halves(x[:, d, :]), ALPHA, pair(d % 2), ALU.mult, ALU.add) \
                    .then_inc(sem("r_done"), 1)
            norm(1)
            dve.wait_ge(sem("rp_out"), 16)
            dve.wait_ge(sem("kvi_out"), 48)
            for s in range(3):
                dve.wait_ge(sem(f"st_out{s}"), 16 * ((NB - s + 2) // 3))
            ffn(1)

        @block.gpsimd
        def _(pool):
            pool.wait_ge(sem("pages_in"), 16)
            pool.wait_ge(sem("h_done"), 2 + FT)
            for pr in range(3):
                index_pages(pool, pr)
            pool.wait_ge(sem("sw_g1"), NCH)
            pool.memset(lgt[:, :, 512:544], NEVER).then_inc(sem("lg_init"), 1)
            pool.sem_inc(sem("index_done"), 1)
            pool.wait_ge(sem("w_free2"), FF_W[2])
            for s in range(3):
                pool.dma_start(st[:, s, :], state[s]).then_inc(sem(f"st_in{s}"), 16)
            pool.wait_ge(sem("rope_in"), 16)
            pool.wait_ge(sem("z_done"), ZT)
            for u in range(8):
                if u >= 2:
                    pool.wait_ge(sem("rope_done"), u - 1)
                pool.tensor_tensor(zc[:, u % 2, :], z[:, RQ + u, :], cos_t, ALU.mult).then_inc(sem("zc_done"), 1)
            pool.wait_ge(sem("masks_read"), 1)
            pool.dma_start(sc[:, 0:1024], ret_tab).then_inc(sem("ret_in"), 16)
            pool.wait_ge(sem("sr_done"), 5)
            pool.dma_start(rp_o, sr).then_inc(sem("rp_out"), 16)
            for b in range(NB):
                pool.wait_ge(sem("st_new"), b + 1)
                pool.dma_start(rs_o[b], st[:, b % 3, :]).then_inc(sem(f"st_out{b % 3}"), 16)
                if b + 3 < NB:
                    pool.wait_ge(sem(f"st_out{b % 3}"), 16 * (b // 3 + 1))
                    pool.dma_start(st[:, b % 3, :], state[b + 3]).then_inc(sem(f"st_in{b % 3}"), 16)


OUT_W = [FF_W[0] + 3 + 8, FF_W[1] + 2 + 8, FF_W[2] + 2 + 8, FF_W[3] + 2]


def _tables():
    f = np.float32
    cs = np.zeros((P, CONST_W), f)

    def put(name, a, rows=slice(None)):
        at, w = CONSTS[name]
        cs[rows, at:at + w] = a

    put("ident", np.eye(P))
    put("mean", 1.0 / D)
    put("ones", 1.0)
    rot = np.zeros((P, P), f)
    for m in range(64):
        rot[m + 64, m] = -1.0
        rot[m, m + 64] = 1.0
    put("rot", rot)
    n = np.arange(P)
    put("tri", np.where(n[None, :] <= n[:, None], 0.0, NEVER))
    sel = np.zeros((P, P), f)
    row = np.arange(P)
    sel[64 + (row // NQ) % AH, row] = 1.0
    put("sel", sel)
    mg = np.zeros((P, 2, NS), f)
    for g in range(2):
        mg[row, g, (4 * g + row // 32) * NQ + row % NQ] = AH ** -0.5
    put("maskg", mg.reshape(P, -1))
    own = np.arange(NS) // NQ
    put("blkrow", np.broadcast_to((own[None, :] == np.arange(NB)[:, None]).astype(f)[None], (P, NB, NS)).reshape(P, -1))
    lg = np.log(f(1.0) - f(2.0) ** (f(-5.0) - np.arange(RH, dtype=f))).astype(f).astype(np.float64)
    sc = P ** -0.5
    j = np.arange(NS) % NQ
    dj = j[None, :] - j[:, None]
    same = (own[:, None] == own[None, :]) & (dj >= 0)
    put("decs", np.stack([np.where(same, np.exp(dj * l) * sc, 0) for l in lg], 1).reshape(NS, -1), slice(0, NS))
    put("xis", np.broadcast_to(np.stack([np.exp((j + 1) * l) for l in lg]).reshape(1, -1), (P, RH * NS)))
    put("own", np.where(own[:, None] == own[None, :], 0.0, NEVER), slice(0, NS))
    put("tri4", np.where(np.arange(NQ)[None, :] <= j[:, None], 0.0, NEVER), slice(0, NS))
    put("zeta", np.exp((P - 1 - n)[:, None] * lg[None]) * sc)
    put("zetat", np.exp((TAIL - 1 - np.arange(TAIL))[:, None] * lg[None]) * sc, slice(0, TAIL))
    put("zetas", np.exp((NQ - 1 - j)[:, None] * lg[None]) * sc, slice(0, NS))
    put("gam", np.concatenate([np.exp(L * lg) for L in (P, TAIL, NQ)])[None])
    put("blkcol", (own[:, None] == np.arange(NB)[None]).astype(f), slice(0, NS))
    put("eps", EPS)
    put("hsel", ((row // NQ % AH)[:, None] == np.arange(AH)[None]).astype(f))
    pos = np.concatenate([np.arange(512), PAST + np.arange(NS) % NQ, 512 + np.arange(TAIL)]).astype(f)
    inv = (f(10000.0) ** (-np.arange(64, dtype=f) / f(64))).astype(f)
    ang = (pos[None, :] * inv[:, None]).astype(f)
    ang = np.concatenate([ang, ang])
    rope = np.concatenate([np.cos(ang), np.sin(ang)], 1).astype(f)
    d = n[None, :] - n[:, None]
    dec = np.stack([np.where(d >= 0, np.exp(np.maximum(d, 0) * l) * sc, 0) for l in lg], 1).reshape(P, -1)
    xi = np.broadcast_to(np.stack([np.exp((n + 1) * l) for l in lg]).reshape(1, -1), (P, RH * P))
    ret = np.concatenate([dec, xi], 1).astype(f)
    a0 = np.zeros((P, ACC_W), f)
    for t in (1, 2, 3):
        a0[:, ACC_AT[t] + 128 * t:ACC_AT[t] + 128 * (t + 1)] = np.where(n[None, :] <= n[:, None], 0.0, NEVER)
    a0[0:TAIL, ACC_AT[4] + 512:ACC_AT[4] + 528] = np.where(n[None, :TAIL] <= n[:TAIL, None], 0.0, NEVER)
    return cs, rope, ret, a0


def kernel(**inputs):
    import concourse.bacc as _bacc
    from concourse.bass_utils import run_bass_kernel_spmd as _run

    a = {k: np.asarray(v) for k, v in inputs.items()}

    def cols(xp, xs):
        return np.concatenate([xp[0:512], xs.reshape(NS, -1), xp[512:]], 0)

    def tiled(w):
        kk, nn = w.shape
        return w.reshape(kk // P, P, nn // P, P).transpose(2, 1, 0, 3).reshape(nn // P, P, kk)

    xt = cols(np.concatenate([a["meta_tokens"], a["x_prompt"][0]], 0), a["x_sample"])
    xt = xt.T.reshape(KT, P, T).transpose(1, 0, 2).reshape(P, KT * T)
    w = a["w_in"][0]
    o = np.cumsum([0, 512, 512, 512, 512, 64, 8, 512, 512, 512, 512])
    part = [w[:, o[i]:o[i + 1]] for i in range(10)]
    wp = np.concatenate([part[3], part[4], part[5], np.zeros((D, 56), w.dtype), part[0], part[1], part[2],
                         part[6], part[7], part[8], part[9]], 1)
    pool = a["cache_k"].shape[1]
    cs, rope, ret, a0 = _tables()
    at = CONSTS["ln"][0]
    ln = np.stack([a[f"ln{i}_{s}"][0].reshape(KT, P).T for i in (1, 2, 3) for s in "gb"], 1).reshape(P, 48)
    cs = np.concatenate([cs[:, :at], ln, cs[:, at + 48:]], 1)
    ins = dict(
        x_t=xt, wg1=tiled(a["ffn1_w_gate"][0]), wu1=tiled(a["ffn1_w_up"][0]), wd1=tiled(a["ffn1_w_down"][0]),
        wg2=tiled(a["ffn2_w_gate"][0]), wu2=tiled(a["ffn2_w_up"][0]), wd2=tiled(a["ffn2_w_down"][0]),
        w_in=tiled(wp), w_out=tiled(a["w_out"][0]),
        k_pool=a["cache_k"][0].reshape(pool, PAGE, 4, P).transpose(0, 3, 2, 1).reshape(pool, P, 512),
        v_pool=a["cache_v"][0].reshape(pool, PAGE, 512), i_pool=a["cache_idx_k"][0].transpose(0, 2, 1),
        state=a["state_ret"][0].transpose(0, 2, 1, 3).reshape(NB, P, 512),
        pages=a["page_table"].reshape(1, -1), consts=cs, rope_tab=rope, ret_tab=ret, acc_tab=a0)
    outs = dict(y_o=(KT, P, T), k_o=(P, 4, T), v_o=(P, 4, T), i_o=(64, T), rp_o=(P, 512), rs_o=(NB, P, 512))
    nc = _bacc.Bacc("TRN2", target_bir_lowering=False, num_devices=1)
    arrays, args = {}, {}
    for name, v in ins.items():
        v = np.ascontiguousarray(v)
        arrays["in_" + name] = v
        args[name] = nc.dram_tensor("in_" + name, v.shape, mybir.dt.from_np(v.dtype), kind="ExternalInput").ap()
    for name, shape in outs.items():
        args[name] = nc.dram_tensor("out_" + name, shape, F32, kind="ExternalOutput").ap()
    build(nc, **args)
    r = _run(nc, [arrays], core_ids=[0]).results[0]
    r = {k: r["out_" + k] for k in outs}

    def split(t):
        return np.concatenate([t[0:512], t[TL:T]], 0), t[SMP:TL]

    yp, ys = split(r["y_o"].reshape(D, T).T)
    kp, ks = split(r["k_o"].transpose(1, 0, 2).reshape(512, T).T)
    vp, vs_ = split(r["v_o"].transpose(1, 0, 2).reshape(512, T).T)
    ip, is_ = split(r["i_o"].T)
    L = SEQ + META
    res = (yp[META:].reshape(1, SEQ, D), ys.reshape(NB, NQ, D),
           kp.reshape(1, 1, L, AH, AD), vp.reshape(1, 1, L, AH, AD), ip.reshape(1, 1, L, AD),
           r["rp_o"].reshape(P, RH, P).transpose(1, 0, 2).reshape(1, 1, RH, P, P),
           ks.reshape(1, NB, NQ, AH, AD), vs_.reshape(1, NB, NQ, AH, AD), is_.reshape(1, NB, NQ, AD),
           r["rs_o"].reshape(NB, P, RH, P).transpose(0, 2, 1, 3).reshape(1, NB, RH, P, P))
    return tuple(np.ascontiguousarray(t) for t in res)
```

```python
from contextlib import ExitStack, contextmanager

import numpy as np
import concourse.bass as bass
from concourse import mybir

ALU = mybir.AluOpType
ACT = mybir.ActivationFunctionType
AX = mybir.AxisListType
F32 = mybir.dt.float32
F32R = mybir.dt.float32r
I32 = mybir.dt.int32

P = 128
D, SEQ, META, DFF = 1024, 512, 16, 2816
NB, NQ, PAST, PAGE = 8, 4, 2048, 128
NPAGE = PAST // PAGE
NS = NB * NQ
TAIL = SEQ + META - 512
T = 512 + NS + TAIL
HALF = T // 2
SMP, TL = 512, 512 + NS
KT, FT = D // P, DFF // P
AH, AD, RH = 8, 64, 4
TOPK_P, TOPK_S = 128, 256
ALPHA = 2.0 ** 0.25
EPS = 1e-5
QI, KW, Q, K, V, RQ, RK, RV, G, ZT = 0, 4, 5, 9, 13, 17, 21, 25, 29, 33
FIRST = 9
NEVER, TAKEN = -1e30, -3e38
KEYS = PAST + NQ
CUT = [0, 8, NPAGE]
DOWN = [1024, 1024, 768]
FF_W = [FT // 2 + KT] * 3 + [FT // 2]
FILL = [3, 3, 6]
GROUPS = 4
CH, NCH = KEYS // 6, 6
LGW = (NPAGE + 1) * 32
ACC_AT = [None, 0, 256, 640, 1152]
ACC_W = 1680

CONSTS = {}
_at = 0
for _n, _w in (("ident", 128), ("mean", 128), ("ones", 128), ("rot", 128), ("tri", 128), ("sel", 128),
               ("maskg", 64), ("blkrow", 256), ("decs", 128), ("xis", 128), ("own", 32), ("tri4", 4),
               ("zeta", 4), ("zetat", 4), ("zetas", 4), ("gam", 12), ("blkcol", 8), ("hsel", 8), ("ln", 48), ("eps", 1)):
    CONSTS[_n] = (_at, _w)
    _at += _w
CONST_W = _at


@contextmanager
def loop(eng, count, steps):
    start = [(t, t.n, k) for t, k in steps]
    with eng.Fori(0, count) as i:
        for t, n, k in start:
            t.n = i * k + n
        yield i
    for t, n, k in start:
        t.n = n + count * k


class Tally:

    def __init__(self, sem, n=0):
        self.sem, self.n = sem, n

    def up(self, k=1):
        self.n = self.n + k
        return self.n


def build(nc, x_t, wg1, wu1, wd1, wg2, wu2, wd2, w_in, w_out, k_pool, v_pool, i_pool, state, pages,
          consts, rope_tab, ret_tab, acc_tab, y_o, k_o, v_o, i_o, rp_o, rs_o):
    wgs, wus, wds = [wg1, wg2], [wu1, wu2], [wd1, wd2]
    with ExitStack() as ctx:
        def sb(name, cols, dt=F32):
            return ctx.enter_context(nc.sbuf_tensor(name, [P, cols], dt))

        sems = {}

        def sem(name):
            if name not in sems:
                sems[name] = ctx.enter_context(nc.semaphore(name))
            return sems[name]

        xbuf = sb("xbuf", KT * T)
        rbuf_at = nc.sbuf_base
        rbuf = sb("rbuf", KT * T)
        h_at = nc.sbuf_base
        big, dring, mask_t = sb("big", ZT * T), sb("dring", 5632), sb("mask_t", LGW)
        assert 2 * FT * T <= ZT * T + 5632 + LGW
        wring = sb("wring", 4 * 1024)
        lg_at = nc.sbuf_base
        lg, sc, mxb = sb("lg", NB * LGW), sb("sc", KEYS), sb("mxb", 512)
        assert KT * T + 2048 <= NB * LGW + KEYS + 512
        acc = sb("acc", ACC_W)
        scr_at = nc.sbuf_base
        scr = sb("scr", 4144)
        cst = sb("cst", CONST_W)
        wi_t, wsel, qibd, qbd = sb("wi_t", 40), sb("wsel", 64), sb("qibd", 256), sb("qbd", 256)
        small = sb("small", 160)

        def over(name, cols, offset):
            return nc.alloc_sbuf_tensor_at(name, [P, cols], F32R, offset=offset)

        h_high, h_low = over("h_high", FT * T, h_at), over("h_low", FT * T, h_at + FT * T * 4)
        x_high, x_low = over("x_high", KT * T, rbuf_at), over("x_low", KT * T, lg_at)
        w_high, w_low = over("w_high", 2048, scr_at + 2 * T * 4), over("w_low", 2048, lg_at + KT * T * 4)

        pt = ctx.enter_context(nc.sbuf_tensor("pt", [1, NB * NPAGE], I32))
        ps = ctx.enter_context(nc.psum_tensor("ps", [P, 8, 512], F32))

        def c(name):
            a, w = CONSTS[name]
            return cst[:, a:a + w]

        def tiles(buf, n, at=0):
            return buf[:, at:at + n * T].rearrange("p (k t) -> p k t", t=T)

        x, r0, z = tiles(xbuf, KT), tiles(rbuf, KT), tiles(big, ZT)
        rbig, mix = tiles(big, KT), r0
        rs = [r0, rbig, r0]

        def halves(ap):
            return ap.rearrange("p (a n) -> p a n", a=2)

        def pair(p):
            return ps[:, 2 * p:2 * p + 2, 0:HALF]

        def cols(a):
            return slice(a * HALF, (a + 1) * HALF)

        def squares(n, a, d):
            buf, at = (dring, 0) if n == 1 else (scr, 2 * T)
            at += (4 * a + d % 4) * HALF
            return buf[:, at:at + HALF]

        ident, ones = c("ident"), c("ones")
        lng = c("ln").rearrange("p (n k) -> p n k", n=6)
        xh, xl, hh, hl = tiles(x_high, KT), tiles(x_low, KT), tiles(h_high, FT), tiles(h_low, FT)
        wh, wl = (w[:, :].rearrange("p (s n) -> p s n", s=2) for w in (w_high, w_low))
        w4 = wring[:, :].rearrange("p (s n) -> p s n", s=4)
        kv = dring[:, 0:4096].rearrange("p (s n) -> p s n", s=8)
        gw = dring[:, 0:4096].rearrange("p (s n) -> p s n", s=4)
        st = dring[:, 4096:5632].rearrange("p (s n) -> p s n", s=3)
        s_buf = tiles(scr, 2)
        rstd = rsum_t = scr[:, 6 * T:7 * T]
        kid = scr[:, 0:T]
        rel = scr[:, T:T + 1056].rearrange("p (s n) -> p s n", s=2)
        rl = scr[:, T + 1056:T + 1056 + KEYS]
        kis = [buf[:, 0:2 * KEYS].rearrange("p (s n) -> p s n", s=2) for buf in (lg, rbuf)]
        qib = qibd[:, :].rearrange("p (r n) -> p r n", r=4)
        qb = qbd[:, :].rearrange("p (a b n) -> p a b n", a=4, b=NB)
        wi = wi_t[:, :].rearrange("p (t h) -> p t h", h=8)
        ws = wsel[:, :].rearrange("p (g n) -> p g n", g=2)
        lgt = lg[:, :].rearrange("p (b n) -> p b n", b=NB)
        cos_t, sin_t = scr[:, 0:T], scr[:, T:2 * T]
        zc = tiles(scr, 2, 2 * T)
        zs = scr[:, 4 * T:5 * T]
        diag = scr[:, 5 * T:5 * T + 256]
        it_b, kz_b, qx_b, rn_b = (scr[:, 512 * j:512 * (j + 1)] for j in range(4))
        l_b = [scr[:, at:at + 528] for at in (2048, 2576, 640)]
        pt_b = scr[:, 3104:3104 + 1024].rearrange("p (s n) -> p s n", s=2)
        dec, xi, sr = (sc[:, 512 * j:512 * (j + 1)] for j in range(3))
        vt = big[:, 0:2048].rearrange("p (t n) -> p t n", t=4)
        vr = wring[:, 0:2048].rearrange("p (t n) -> p t n", t=4)
        vrs, vrt, vs, vtl = (wring[:, 2048 + 512 * j:2048 + 512 * (j + 1)] for j in range(4))
        mx, rsum = mxb[:, 0:256], mxb[:, 256:258]
        smx, ssum, nmx, rcp = small[:, 0:2], small[:, 2:4], small[:, 4:6], small[:, 6:8]
        m8, mx2, bn, bag, rsd, cmp16 = (small[:, 8:40], small[:, 40:42], small[:, 42:66], small[:, 66:74],
                                        small[:, 74:78], small[:, 80:112])

        def acc_ap(t):
            w = 128 * (t + 1) if t < 4 else 528
            return acc[0:(P if t < 4 else TAIL), ACC_AT[t]:ACC_AT[t] + w]

        block = ctx.enter_context(nc.Block())

        def page_reg(eng, at):
            return eng.value_load(pt[0:1, bass.ds(at, 1)], min_val=0, max_val=k_pool.shape[0] - 1)

        def index_pages(eng, pr, parts=(0, 1)):
            if pr >= 2:
                eng.wait_ge(sem("x_done1"), KT)
            for b2 in parts:
                with eng.Fori(0, NPAGE // 4) as i:
                    for j in range(4):
                        pg = page_reg(eng, i * 4 + (2 * pr + b2) * NPAGE + j)
                        eng.dma_start(kis[pr // 2][64 * b2:64 * b2 + 64, pr % 2, bass.ds(i * (4 * PAGE) + j * PAGE, PAGE)],
                                      i_pool[bass.ds(pg, 1)].rearrange("a p n -> (a p) n")) \
                            .then_inc(sem(f"ki_in{pr}"), 16)

        @block.sync
        def _(sp):
            free = [Tally(sem(f"w_free{s}")) for s in range(4)]
            sp.dma_start(pt[:, :], pages).then_inc(sem("pages_in"), 16)

            def weight(s, src, first=False):
                if not first:
                    sp.wait_ge(free[s].sem, free[s].up())
                sp.dma_start(w4[:, s, :], src).then_inc(sem(f"w_in{s}"), 16)

            def down_chunk(s, src):
                sp.wait_ge(free[s].sem, free[s].up())
                sp.dma_start(w4[:, s, 0:DOWN[s]], src[:, s * 1024:s * 1024 + DOWN[s]]).then_inc(sem(f"w_in{s}"), 16)

            def ffn_loads(m):
                for s in range(4):
                    f, up = divmod(s, 2)
                    weight(s, (wus if up else wgs)[m][f], first=(m == 0))
                with loop(sp, FT // 2 - 1, [(f, 1) for f in free]) as i:
                    for s in range(4):
                        f, up = divmod(s, 2)
                        weight(s, (wus if up else wgs)[m][bass.ds(i * 2 + 2 + f, 1)].rearrange("a p n -> (a p) n"))
                for s in range(3):
                    down_chunk(s, wds[m][0])
                with loop(sp, KT - 1, [(f, 1) for f in free[:3]]) as i:
                    for s in range(3):
                        down_chunk(s, wds[m][bass.ds(i + 1, 1)].rearrange("a p n -> (a p) n"))

            ffn_loads(0)
            sp.wait_ge(sem("pages_in"), 16)
            for t in range(FIRST):
                weight(t % 4, w_in[t])
                if t in (6, 8):
                    index_pages(sp, 3, ((t - 6) // 2,))
            sp.wait_ge(sem("w_free2"), FF_W[2])
            kvf = [Tally(sem(f"kv_free{s}")) for s in range(8)]

            def kv_page(s, at, pool, first=False):
                if not first:
                    sp.wait_ge(kvf[s].sem, kvf[s].up())
                pg = page_reg(sp, at)
                sp.dma_start(kv[:, s, :], pool[bass.ds(pg, 1)].rearrange("a p n -> (a p) n")) \
                    .then_inc(sem(f"kv_in{s}"), 16)

            for j in range(2):
                weight(j, w_in[FIRST + j])
                for s in range(CUT[j], CUT[j + 1]):
                    kv_page(s % 8, s, k_pool, first=(s < 8))
            with loop(sp, NB - 1, [(f, 1) for f in free[:2]] + [(f, 2) for f in kvf]) as i:
                for j in range(2):
                    weight(j, w_in[bass.ds(i * 2 + FIRST + 2 + j, 1)].rearrange("a p n -> (a p) n"))
                    for s in range(CUT[j], CUT[j + 1]):
                        kv_page(s % 8, i * NPAGE + NPAGE + s, k_pool)
            for j in range(4):
                weight(j, w_in[RV + j])
            for j in range(4):
                for s in (2 * j, 2 * j + 1):
                    sp.wait_ge(sem(f"kv_free{s}"), 2 * NB)
                sp.dma_start(gw[:, j, :], w_in[G + j]).then_inc(sem("gw_in"), 16)
            sp.wait_ge(sem("index_done"), 1)
            sp.dma_start(scr[:, 0:2 * T], rope_tab).then_inc(sem("rope_in"), 16)
            sp.wait_ge(sem("z_done"), RQ)
            sp.dma_start(k_o, z[:, K:K + 4, :]).then_inc(sem("kvi_out"), 16)
            sp.dma_start(v_o, z[:, V:V + 4, :]).then_inc(sem("kvi_out"), 16)
            sp.dma_start(i_o, z[0:64, KW, :]).then_inc(sem("kvi_out"), 16)
            sp.wait_ge(sem("sg_done"), 4)
            with loop(sp, NB * 2, [(f, 1) for f in kvf]) as i:
                for s in range(8):
                    kv_page(s, i * 8 + s, v_pool)
            sp.wait_ge(sem("mix_read"), 1)
            for s in range(4):
                weight(s, w_out[s])
            for s in range(4):
                weight(s, w_out[s + 4])
            ffn_loads(1)
            for a in range(2):
                with sp.Fori(0, KT) as i:
                    sp.wait_ge(sem(f"x_done{a}"), i + 2 * KT + 1)
                    sp.dma_start(y_o[bass.ds(i, 1), :, cols(a)].rearrange("a p n -> (a p) n"),
                                 x[:, bass.ds(i, 1), cols(a)].rearrange("p a n -> p (a n)")).then_inc(sem("y_out"), 16)
            sp.wait_ge(sem("y_out"), 2 * 16 * KT)
            sp.wait_ge(sem("kvi_out"), 48)
            sp.wait_ge(sem("rp_out"), 16)
            for s in range(3):
                sp.wait_ge(sem(f"st_out{s}"), 16 * ((NB - s + 2) // 3))

        @block.tensor
        def _(pe):
            w_in_t = [Tally(sem(f"w_in{s}")) for s in range(4)]
            kv_in_t = [Tally(sem(f"kv_in{s}")) for s in range(8)]
            hdone, rdone = Tally(sem("h_done")), Tally(sem("r_done"))
            zdone = Tally(sem("z_done"))
            for a in range(2):
                pe.sem_inc(sem(f"sq_free{a}"), 4)

            def mm(out, lhs, rhs, start=True, stop=True, **kw):
                return nc.tensor.matmul(out, lhs, rhs, start=start, stop=stop, **kw)

            def tr(out, in_, k0, k1):
                return nc.tensor.transpose(out, in_, ident[k0:k1, k0:k1])

            def wide(p, wt, kn, src):
                for a in range(2):
                    for k in range(kn):
                        last = mm(ps[:, 2 * p + a, 0:HALF], wt[:, k * P:(k + 1) * P],
                                  src[:, k, a * HALF:(a + 1) * HALF], k == 0, k == kn - 1)
                return last

            def weight(s):
                pe.wait_ge(w_in_t[s].sem, w_in_t[s].up(16))

            def wide_split(p, s, high, low, k0=0, kn=KT, total=KT, parts=(0, 1), ready=None):
                for a in parts:
                    for k in range(kn):
                        if ready is not None:
                            pe.wait_ge(sem("xl_done"), ready + k + 1)
                        for j, (w_, x_) in enumerate(((wh, high), (wh, low), (wl, high))):
                            last = mm(ps[:, 2 * p + a, 0:HALF], w_[:, s, k * P:(k + 1) * P],
                                      x_[:, k0 + k, a * HALF:(a + 1) * HALF], k0 + k + j == 0,
                                      k0 + k == total - 1 and j == 2)
                return last

            def ffn(m):
                hdone.n = FT * m
                wl_done = Tally(sem("wl_done"), (2 * FT + 3 * KT) * m)
                for w, n in zip(w_in_t, FF_W):
                    w.up(16 * n)

                def tile(j):
                    pe.wait_ge(sem("h_done"), hdone.up())
                    for up in range(2):
                        pe.wait_ge(sem("wl_done"), wl_done.up())
                        wide_split(2 * up + j, up, xh, xl).then_inc(sem(f"w_free{2 * j + up}"), 1)

                pe.wait_ge(sem("h_done"), hdone.up())
                for a in range(2):
                    for up in range(2):
                        if a == 0:
                            pe.wait_ge(sem("wl_done"), wl_done.up())
                        last = wide_split(2 * up, up, xh, xl, parts=(a,),
                                          ready=None if up or a > m else KT * (m + a))
                        if a:
                            last.then_inc(sem(f"w_free{up}"), 1)
                tile(1)
                with loop(pe, FT // 2 - 1, [(wl_done, 4), (hdone, 2)]):
                    for j in range(2):
                        tile(j)
                pe.wait_ge(sem("h_done"), 1 + FT * (m + 1))
                pe.wait_ge(sem("hl_done"), FT * m + 16)
                rdone.n = 2 * (KT + 1) * m
                with loop(pe, KT // 2, [(wl_done, 6), (rdone, 2)]):
                    for j in range(2):
                        pe.wait_ge(sem("r_done"), rdone.up())
                        for s in range(3):
                            if s == 2:
                                pe.wait_ge(sem("hl_done"), FT * (m + 1))
                            pe.wait_ge(sem("wl_done"), wl_done.up())
                            wide_split(j, (j + s) % 2, hh, hl, 8 * s, DOWN[s] // P, FT).then_inc(sem(f"w_free{s}"), 1)
                norm(2 * m)

            def norm(n):
                if n == 0:
                    pe.wait_ge(sem("cst_in"), 16)
                pe.wait_ge(sem("sum_done"), (KT - 2) * (n + 1))
                for a in range(2):
                    mm(ps[:, 4 + a, 0:HALF], c("mean"), rsum_t[:, cols(a)], True, False)
                    pe.wait_ge(sem("r_done"), 2 + (KT + 1) * n + KT + a)
                    mm(ps[:, 4 + a, 0:HALF], c("mean"), rs[n][:, KT - 1, cols(a)], False, True) \
                        .then_inc(sem(f"mean_full{a}"), 1)
                for a in range(2):
                    for d in range(KT):
                        pe.wait_ge(sem(f"sq_done{a}"), KT * n + d + 1)
                        mm(ps[:, 6 + a, 0:HALF], c("mean"), squares(n, a, d), d == 0, d == KT - 1) \
                            .then_inc(sem(f"sq_free{a}"), 1)

            ffn(0)

            for a in range(2):
                for t in range(4):
                    if a == 0:
                        weight(t)
                    for k in range(KT):
                        if t == 0:
                            pe.wait_ge(sem(f"x_done{a}"), k + 1)
                        last = mm(ps[:, 2 * t + a, 0:HALF], w4[:, t, k * P:(k + 1) * P], x[:, k, cols(a)],
                                  k == 0, k == KT - 1)
                    if a:
                        last.then_inc(sem(f"w_free{t}"), 1)

            def first_tile(t):
                weight(t % 4)
                pe.wait_ge(sem("z_done"), t - 1)
                wide(t % 2, w4[:, t % 4, :], KT, x).then_inc(sem(f"w_free{t % 4}"), 1)

            first_tile(KW)
            pe.wait_ge(sem("z_done"), Q)
            for t in (1, 2, 3):
                tr(ps[:, 6, 64 * t:64 * t + 64], z[64:128, KW, 128 * t:128 * t + 128], 64, 128)
            tr(ps[0:TAIL, 6, 0:64], z[64:128, KW, TL:T], 64, 128)
            mm(ps[:, 7, 0:NS], c("sel")[64:128, :], z[64:128, KW, SMP:TL]).then_inc(sem("prep_full"), 1)
            pe.wait_ge(sem("kid_done"), 2)
            u = 0
            for t in (1, 2, 3, 4):
                first_tile(Q + t - 1)
                if t == 4:
                    pe.wait_ge(sem("wi_done"), 1)
                for hd in range(AH):
                    lo = 64 * (hd % 2)
                    p = u % 2
                    if u >= 2:
                        pe.wait_ge(sem("rel_done"), u - 1)
                    q0, n, nk = (128 * t, P, 128 * (t + 1)) if t < 4 else (TL, TAIL, 512)
                    last = mm(ps[0:n, 4 + p, 0:nk], z[lo:lo + 64, QI + hd // 2, q0:q0 + n], kid[lo:lo + 64, 0:nk])
                    if t == 4:
                        if u >= 1:
                            pe.wait_ge(sem("rel_done"), u)
                        last = mm(ps[0:n, 6, 0:TAIL], z[lo:lo + 64, QI + hd // 2, q0:q0 + n], kid[lo:lo + 64, TL:T])
                    last.then_inc(sem("s_full"), 1)
                    u += 1
            pe.wait_ge(sem("z_done"), FIRST)
            pe.wait_ge(sem("qib_done"), 1)
            pe.wait_ge(sem("rel_done"), u)
            pe.wait_ge(sem("wsel_done"), 1)
            pe.wait_ge(sem("wi_done"), 1)
            for g in range(2):
                for j in range(2):
                    pe.wait_ge(sem(f"ki_in{2 * g + j}"), 16 * 2 * NPAGE)
                    pe.wait_ge(sem("kin_done"), 2 * g + j + 1)
                for ch in range(NCH):
                    if g:
                        pe.wait_ge(sem("rl_done"), ch + 1)
                    for j in range(2):
                        last = mm(ps[64 * j:64 * j + 64, ch, 0:CH], qib[:, 2 * g + j, :],
                                  kis[g][:, j, ch * CH:(ch + 1) * CH])
                    last.then_inc(sem("ss_full"), 1)
                for ch in range(NCH):
                    pe.wait_ge(sem("rl_done"), NCH * g + ch + 1)
                    k = NCH * g + ch
                    if k >= 2:
                        s_, v_ = ("sw_g0", k - 1) if k - 2 < NCH else ("sw_g1", k - 1 - NCH)
                        pe.wait_ge(sem(s_), v_)
                    mm(ps[0:NS, 6 + ch % 2, 0:CH], ws[:, g, :], rl[:, ch * CH:(ch + 1) * CH]) \
                        .then_inc(sem("sw_full"), 1)
            pe.wait_ge(sem("sw_g1"), NCH)
            pe.wait_ge(sem("qb_done"), 1)
            zdone.n = FIRST - 2
            lgd = Tally(sem("lg_done"))
            with loop(pe, NB, [(w, 16) for w in w_in_t[:2]] + [(k_, 32) for k_ in kv_in_t] + [(zdone, 2), (lgd, 1)]) as i:
                for j in range(2):
                    weight(j)
                    pe.wait_ge(sem("z_done"), zdone.up())
                    for g in range(GROUPS):
                        for at in range(g * 2 * KT // GROUPS, (g + 1) * 2 * KT // GROUPS):
                            a, k = divmod(at, KT)
                            last = mm(ps[:, 2 * j + a, 0:HALF], w4[:, j, k * P:(k + 1) * P], x[:, k, cols(a)],
                                      k == 0, k == KT - 1)
                        if g == GROUPS - 1:
                            last.then_inc(sem(f"w_free{j}"), 1)
                        if j == 0 and g == 0:
                            pe.wait_ge(sem("lg_done"), lgd.up())
                        share = NPAGE // 2 // GROUPS
                        for pg in range(CUT[j] + g * share, CUT[j] + (g + 1) * share):
                            s = pg % 8
                            pe.wait_ge(kv_in_t[s].sem, kv_in_t[s].up(16))
                            for hp in range(4):
                                last = mm(ps[:, 6, pg * 32 + hp * 8:pg * 32 + hp * 8 + 8],
                                          kv[:, s, hp * P:(hp + 1) * P],
                                          qb[:, hp, bass.ds(i, 1), :].rearrange("p a n -> p (a n)"))
                            last.then_inc(sem(f"kv_free{s}"), 1)
            for hp in range(4):
                last = mm(ps[0:NS, 7, hp * 64:hp * 64 + 64], z[:, K + hp, SMP:TL],
                          qb[:, hp, :, :].rearrange("p b n -> p (b n)"))
            last.then_inc(sem("p16_full"), 1)
            for j in range(4):
                weight(j)
                pe.wait_ge(sem("z_done"), zdone.up())
                wide(j % 2, w4[:, j, :], KT, x).then_inc(sem(f"w_free{j}"), 1)
            pe.wait_ge(sem("z_done"), G)
            k = 0
            for src in (V, RV):
                for t0, n in [(128 * t, P) for t in range(4)] + [(SMP, NS), (TL, TAIL)]:
                    if k >= 4:
                        pe.wait_ge(sem("tr_done"), k - 3)
                    for j in range(4):
                        last = tr(ps[0:n, k % 4, j * P:(j + 1) * P], z[:, src + j, t0:t0 + n], 0, P)
                    last.then_inc(sem("tr_full"), 1)
                    k += 1
            pe.wait_ge(sem("tr_done"), 12)
            pe.wait_ge(sem("lg_done"), NB + 1)
            pe.wait_ge(sem("smask_done"), 1)
            for pg in range(NPAGE):
                tr(ps[:, 4, pg * NS:(pg + 1) * NS], sc[0:NS, pg * PAGE:(pg + 1) * PAGE], 0, NS)
            tr(ps[0:NS, 5, 0:NS], cmp16[0:NS, :], 0, NS).then_inc(sem("masks_full"), 1)
            for u in range(8):
                if u >= 2:
                    pe.wait_ge(sem("zs_done"), u - 1)
                for a in range(2):
                    last = mm(ps[:, 2 * (u % 2) + a, 0:HALF], c("rot"), z[:, RQ + u, a * HALF:(a + 1) * HALF])
                last.then_inc(sem("rot_full"), 1)

            def gate_tile(j, p):
                wide(p, gw[:, j, :], KT, x).then_inc(sem("g_full"), 1)

            pe.wait_ge(sem("gw_in"), 64)
            pe.wait_ge(sem("p16_done"), 1)
            gate_tile(0, 3)
            pe.wait_ge(sem("zs_done"), 7)
            gate_tile(1, 0)
            pe.wait_ge(sem("sg_done"), 1)
            gate_tile(2, 3)
            pe.wait_ge(sem("mask_used"), 1)
            pe.wait_ge(sem("mx_done"), 1)
            for g in range(2):
                last = tr(ps[:, 5, g * P:(g + 1) * P], mx[:, g * P:(g + 1) * P], 0, P)
            last.then_inc(sem("mxt_full"), 1)
            pe.wait_ge(sem("diag_done"), 1)
            mm(ps[:, 4, 0:256], ones, diag).then_inc(sem("mxb_full"), 1)
            pe.wait_ge(sem("sg_done"), 3)
            gate_tile(3, 3)
            pe.wait_ge(sem("psum_done"), 1)
            for g in range(2):
                last = mm(ps[:, 5, g:g + 1], mx[:, g * P:(g + 1) * P], ones[:, 0:1])
            last.then_inc(sem("sum_full"), 1)
            pe.wait_ge(sem("rsum_done"), 1)
            pe.wait_ge(sem("rope_done"), 8)

            done = [0]

            def value_pages(count):
                for n in range(done[0], done[0] + count):
                    b, pg = divmod(n, NPAGE)
                    if n == 0:
                        pe.wait_ge(sem("sp_done"), NB)
                    s_ = pg % 8
                    o = ps[32 * (b % 4):32 * (b % 4) + 32, 3 if b >= 4 else 5, :]
                    pe.wait_ge(kv_in_t[s_].sem, kv_in_t[s_].up(16))
                    mm(o, lgt[:, b, pg * 32:(pg + 1) * 32], kv[:, s_, :], pg == 0, False) \
                        .then_inc(sem(f"kv_free{s_}"), 1)
                    if pg == NPAGE - 1:
                        last = mm(o, lgt[0:NS, b, 512:544], vs[0:NS, :], False, True)
                        if b % 4 == 3:
                            last.then_inc(sem("so_full"), 1)
                done[0] += count

            def ret_in(cn, t0, n):
                for hd in range(RH):
                    last = mm(ps[0:n, 0, hd * P:hd * P + n], z[:, RK + hd, t0:t0 + n], z[:, RQ + hd, t0:t0 + n])
                last.then_inc(sem("inner_full"), 1)
                for hd in range(RH):
                    last = tr(ps[0:n, 1, hd * P:(hd + 1) * P], z[:, RK + hd, t0:t0 + n], 0, P)
                last.then_inc(sem("kt_full"), 1)

            def ret_out(cn, n):
                pe.wait_ge(sem("rn_done"), cn + 1)
                for hd in range(RH):
                    last = tr(ps[:, 4, hd * P:hd * P + n], rn_b[0:n, hd * P:(hd + 1) * P], 0, n)
                last.then_inc(sem("rt_full"), 1)

            for cn in range(5):
                t0, n = (128 * cn, P) if cn < 4 else (TL, TAIL)
                vv = vr[:, cn, :] if cn < 4 else vrt
                ret_in(cn, t0, n)
                value_pages(FILL[0])
                pe.wait_ge(sem("it_done"), cn + 1)
                pe.wait_ge(sem("qx_done"), cn + 1)
                if cn:
                    pe.wait_ge(sem("sr_done"), cn)
                for hd in range(RH):
                    o = ps[0:n, 2, hd * P:(hd + 1) * P]
                    last = mm(o, it_b[0:n, hd * P:hd * P + n], vv[0:n, hd * P:(hd + 1) * P], True, cn == 0)
                    if cn:
                        last = mm(o, qx_b[:, hd * P:hd * P + n], sr[:, hd * P:(hd + 1) * P], False, True)
                last.then_inc(sem("ro_full"), 1)
                pe.wait_ge(sem("kz_done"), cn + 1)
                for hd in range(RH):
                    last = mm(ps[:, 3, hd * P:(hd + 1) * P], kz_b[0:n, hd * P:(hd + 1) * P],
                              vv[0:n, hd * P:(hd + 1) * P])
                last.then_inc(sem("rst_full"), 1)
                value_pages(min(FILL[1], NPAGE * 4 - done[0]))
                ret_out(cn, n)
                value_pages(min(FILL[2], NPAGE * 4 - done[0]))
                pe.wait_ge(sem("mixr_done"), cn + 1)
            ret_in(5, SMP, NS)
            value_pages(NPAGE * 4 - done[0])
            pe.wait_ge(sem("so_out"), 1)
            pe.wait_ge(sem("sr_done"), 5)
            pe.wait_ge(sem("it_done"), 6)
            for hd in range(RH):
                mm(ps[0:NS, 4 + hd, 0:P], it_b[0:NS, hd * P:hd * P + NS], vrs[0:NS, hd * P:(hd + 1) * P], True, False)
            for b in range(NB):
                pe.wait_ge(sem("qxb_done"), b + 1)
                pe.wait_ge(sem(f"st_in{b % 3}"), 16 * (b // 3 + 1))
                for hd in range(RH):
                    last = mm(ps[0:NS, 4 + hd, 0:P], qx_b[:, 128 * (b % 2) + hd * NS + 256:128 * (b % 2) + (hd + 1) * NS + 256],
                              st[:, b % 3, hd * P:(hd + 1) * P], False, b == NB - 1)
                last.then_inc(sem("cross_full"), 1)
                pe.wait_ge(sem("kzb_done"), b + 1)
                if b >= 2:
                    pe.wait_ge(sem("st_new"), b - 1)
                for hd in range(RH):
                    last = mm(ps[:, 2 - b % 2, hd * P:(hd + 1) * P],
                              rn_b[0:NS, hd * P:(hd + 1) * P] if b % 2 else l_b[0][0:NS, hd * P:(hd + 1) * P],
                              vrs[0:NS, hd * P:(hd + 1) * P])
                last.then_inc(sem("dst_full"), 1)
            pe.wait_ge(sem("rn_done"), 6)
            for hd in range(RH):
                last = tr(ps[:, 0, hd * P:hd * P + NS], rn_b[0:NS, hd * P:(hd + 1) * P], 0, NS)
            last.then_inc(sem("rt_full"), 1)
            pe.wait_ge(sem("mixr_done"), 6)
            pe.wait_ge(sem("st_new"), NB)

            units = [(hd, t) for hd in range(AH) for t in range(5)]

            def scores(u, hd, t):
                lo, p = 64 * (hd % 2), u % 2
                q0, n, nk = (128 * t, P, 128 * (t + 1)) if t < 4 else (TL, TAIL, 512)
                if u >= 2:
                    pe.wait_ge(sem("al_done"), u - 1)
                last = mm(ps[0:n, p, 0:nk], z[lo:lo + 64, Q + hd // 2, q0:q0 + n], z[lo:lo + 64, K + hd // 2, 0:nk])
                if t == 4:
                    if u > len(units) // 2:
                        pe.wait_ge(sem("so_done"), 2)
                    last = mm(ps[0:n, 2, 0:TAIL], z[lo:lo + 64, Q + hd // 2, q0:q0 + n],
                              z[lo:lo + 64, K + hd // 2, TL:T])
                last.then_inc(sem("as_full"), 1)

            def turn(u, hd, t):
                p, n = u % 2, (P if t < 4 else TAIL)
                pe.wait_ge(sem("ap_done"), u + 1)
                if u >= 2:
                    pe.wait_ge(sem("apt_done"), u - 1)
                for j in range(t + 1 if t < 4 else 4):
                    last = tr(ps[:, 4 + p, j * n:(j + 1) * n], l_b[u % 3][0:n, j * P:(j + 1) * P], 0, n)
                if t == 4:
                    last = tr(ps[0:TAIL, 4 + p, 4 * n:5 * n], l_b[u % 3][0:n, 512:512 + TAIL], 0, n)
                last.then_inc(sem("at_full"), 1)

            def values(u, hd, t):
                p, n, lo = u % 2, (P if t < 4 else TAIL), 64 * (hd % 2)
                pe.wait_ge(sem("apt_done"), u + 1)
                if u >= 2:
                    pe.wait_ge(sem("ao_done"), u - 1)
                nj = t + 1 if t < 4 else 5
                for j in range(nj):
                    lhs = vt[:, j, hd * AD:(hd + 1) * AD] if j < 4 else vtl[0:TAIL, hd * AD:(hd + 1) * AD]
                    rhs = pt_b[:, p, j * n:(j + 1) * n] if j < 4 else pt_b[0:TAIL, p, 4 * n:5 * n]
                    last = mm(ps[lo:lo + 64, 6 + p, 0:n], lhs, rhs, j == 0, j == nj - 1)
                last.then_inc(sem("ao_full"), 1)

            def sample_turn(g):
                pe.wait_ge(sem("so_att"), g + 1)
                if g == 0:
                    pe.wait_ge(sem("al_done"), len(units) // 2)
                tr(ps[0:64, 5 if g else 2, 0:P], kz_b[:, 64 * g:64 * g + 64], 0, P) \
                    .then_inc(sem("so_turned"), 1)

            first, rest = done[0], NPAGE * NB - done[0]
            scores(0, *units[0])
            for u in range(len(units) + 2):
                if u + 1 < len(units):
                    scores(u + 1, *units[u + 1])
                if u >= 2:
                    values(u - 2, *units[u - 2])
                if u < len(units):
                    value_pages(first + (u + 1) * rest // len(units) - done[0])
                if 1 <= u <= len(units):
                    turn(u - 1, *units[u - 1])
                if u == len(units) // 2:
                    sample_turn(0)
            sample_turn(1)
            pe.wait_ge(sem("ao_done"), len(units))
            pe.wait_ge(sem("so_done"), 4)
            pe.sem_inc(sem("mix_read"), 1)

            for d in range(KT):
                weight(d % 4)
                pe.wait_ge(sem("r_done"), KT + 1 + d + 1)
                wide(d % 2, w4[:, d % 4, :], KT, mix).then_inc(sem(f"w_free{d % 4}"), 1)
            norm(1)
            ffn(1)

        @block.scalar
        def _(act):
            act.sem_inc(sem("lg_done"), 1)
            for q in range(4):
                act.dma_start(x[:, 2 * q:2 * q + 2, :], x_t[:, 2 * q * T:(2 * q + 2) * T]
                              .rearrange("p (k t) -> p k t", k=2)).then_inc(sem(f"x_in{q}"), 16)
            act.dma_start(cst[:, :], consts).then_inc(sem("cst_in"), 16)
            act.dma_start(acc[:, :], acc_tab).then_inc(sem("acc_in"), 16)

            def ev(out, in_, func=ACT.Copy, **kw):
                return nc.scalar.activation(out, in_, func, **kw)

            def weight_high(s, to, n=1024):
                act.wait_ge(w_in_t[s].sem, w_in_t[s].up(16))
                ev(wh[:, to, 0:n], w4[:, s, 0:n]).then_inc(sem("wh_done"), 1)

            def ffn(m):
                frees = [Tally(sem(f"w_free{s}"), seen[m][s]) for s in range(4)]

                def hidden(f, j, down=False):
                    for up in range(2):
                        w = frees[2 * j + up]
                        act.wait_ge(w.sem, w.up())
                        weight_high(up if down else 2 * (1 - j) + up, up)
                    ev(halves(s_buf[:, j, :]), pair(j), ACT.Silu).then_inc(sem("s_done"), 1)
                    act.wait_ge(hdone.sem, hdone.up())
                    ev(hh[:, bass.ds(f, 1), :].rearrange("p a n -> p (a n)"), s_buf[:, j, :]).then_inc(sem("hh_done"), 1)

                def output(j, more=True):
                    for s in range(3):
                        w = frees[s]
                        act.wait_ge(w.sem, w.up())
                        if more or s == 0:
                            nxt = (s + 2) % 3
                            weight_high(nxt, (j + s) % 2, DOWN[nxt])
                    if more:
                        ev(halves(s_buf[:, j, :]), pair(j), scale=0.5).then_inc(sem("y_done"), 1)
                    else:
                        for a in range(2):
                            ev(s_buf[:, j, cols(a)], ps[:, 2 * j + a, 0:HALF], scale=0.5).then_inc(sem("y_done"), 1)

                hdone = Tally(sem("h_done"), 2 + FT * m)
                with loop(act, FT // 2 - 1, [(w, 1) for w in frees] + [(w, 16) for w in w_in_t] + [(hdone, 2)]) as i:
                    hidden(i * 2, 0)
                    hidden(i * 2 + 1, 1)
                hidden(FT - 2, 0)
                hidden(FT - 1, 1, True)
                with loop(act, KT // 2 - 1, [(w, 2) for w in frees[:3]] + [(w, 32) for w in w_in_t[:3]]):
                    output(0)
                    output(1)
                output(0)
                output(1, False)
                norm(2 * m)

            def norm(n):
                r = rs[n]
                if n == 0:
                    act.wait_ge(sem("cst_in"), 16)
                for d in range(KT):
                    act.wait_ge(sem("c_done0"), KT * n + d + 1)
                    act.wait_ge(sem("sq_free0"), KT * n + d + 1)
                    ev(squares(n, 0, d), r[:, d, cols(0)], ACT.Square).then_inc(sem("sq_done0"), 1)
                if n == 1:
                    weight_high(0, 0)
                    weight_high(1, 1)
                for a in range(2):
                    act.wait_ge(sem(f"sq_free{a}"), 4 + KT * (n + 1))
                    ev(rstd[:, cols(a)], ps[:, 6 + a, 0:HALF], ACT.Sqrt, bias=c("eps")).then_inc(sem(f"std_done{a}"), 1)
                    for d in range(KT):
                        act.wait_ge(sem(f"n_done{a}"), KT * n + d + 1)
                        gain = dict(scale=lng[:, 2 * n, d:d + 1], bias=lng[:, 2 * n + 1, d:d + 1])
                        if n == 1:
                            ev(xh[:, d, cols(a)], r[:, d, cols(a)], ACT.Identity, **gain)
                        ev(x[:, d, cols(a)], r[:, d, cols(a)], ACT.Identity, **gain).then_inc(sem(f"x_done{a}"), 1)

            seen = [[0] * 4, [OUT_W[s] + 2 for s in range(4)]]
            w_in_t = [Tally(sem(f"w_in{s}")) for s in range(4)]
            weight_high(0, 0)
            for k in range(KT):
                act.wait_ge(sem(f"x_in{k // 2}"), 16)
                ev(xh[:, k, :], x[:, k, :]).then_inc(sem("xh_done"), 1)
            weight_high(1, 1)
            ffn(0)
            def first_tile(t):
                act.wait_ge(sem(f"w_free{t % 4}"), FF_W[t % 4] + t // 4 + 1)
                if t == KW:
                    for lo in (0, 64):
                        ev(halves(kid[lo:lo + 64, :]), ps[0:64, 2 * (t % 2):2 * (t % 2) + 2, 0:HALF]) \
                            .then_inc(sem("kid_done"), 1)
                ev(halves(z[:, t, :]), pair(t if t < 4 else t % 2)).then_inc(sem("z_done"), 1)

            for t in range(Q):
                first_tile(t)
            act.wait_ge(sem("prep_full"), 1)
            for t in (1, 2, 3):
                ev(wi[:, t, :], ps[:, 6, 64 * t:64 * t + 8], scale=AH ** -0.5)
            ev(wi[0:TAIL, 4, :], ps[0:TAIL, 6, 0:8], scale=AH ** -0.5).then_inc(sem("wi_done"), 1)
            u = 0
            for t in (1, 2, 3, 4):
                first_tile(Q + t - 1)
                for hd in range(AH):
                    n, nk = (P, 128 * (t + 1)) if t < 4 else (TAIL, 512)
                    act.wait_ge(sem("s_full"), u + 1)
                    if u >= 2:
                        act.wait_ge(sem("acc_done"), u - 1)
                    last = ev(rel[0:n, u % 2, 0:nk], ps[0:n, 4 + u % 2, 0:nk], ACT.Relu, scale=AD ** -0.5)
                    if t == 4:
                        last = ev(rel[0:n, u % 2, 512:512 + TAIL], ps[0:n, 6, 0:TAIL], ACT.Relu, scale=AD ** -0.5)
                    last.then_inc(sem("rel_done"), 1)
                    u += 1
            for g in range(2):
                for ch in range(NCH):
                    act.wait_ge(sem("ss_full"), NCH * g + ch + 1)
                    if g:
                        act.wait_ge(sem("sw_full"), ch + 1)
                    ev(rl[:, ch * CH:(ch + 1) * CH], ps[:, ch, 0:CH], ACT.Relu, scale=AD ** -0.5) \
                        .then_inc(sem("rl_done"), 1)
                if g == 0:
                    for ch in range(NCH):
                        act.wait_ge(sem("sw_full"), ch + 1)
                        ev(sc[0:NS, ch * CH:(ch + 1) * CH], ps[0:NS, 6 + ch % 2, 0:CH]).then_inc(sem("sw_g0"), 1)
            wf = [Tally(sem(f"w_free{s}"), FF_W[s] + (3 if s == 0 else 2)) for s in range(4)]
            kf = Tally(sem("kv_free7"))
            with loop(act, NB, [(w, 1) for w in wf[:2]] + [(kf, 2)]) as i:
                for j in range(2):
                    act.wait_ge(wf[j].sem, wf[j].up())
                    ev(halves(z[:, bass.ds(i * 2 + FIRST + j, 1), :].rearrange("p a n -> p (a n)")), pair(j)) \
                        .then_inc(sem("z_done"), 1)
                act.wait_ge(kf.sem, kf.up(2))
                ev(lgt[:, bass.ds(i, 1), 0:512].rearrange("p a n -> p (a n)"), ps[:, 6, :], scale=AD ** -0.5) \
                    .then_inc(sem("lg_done"), 1)
            act.wait_ge(sem("p16_full"), 1)
            act.wait_ge(sem("lg_init"), 1)
            for hp in range(4):
                last = ev(lgt[0:NS, :, 512 + hp * 8:512 + hp * 8 + 8],
                          ps[0:NS, 7, hp * 64:hp * 64 + 64].rearrange("p (b n) -> p b n", b=NB), scale=AD ** -0.5)
            last.then_inc(sem("p16_done"), 1)
            for j in range(4):
                act.wait_ge(wf[j].sem, wf[j].up())
                ev(halves(z[:, RV + j, :]), pair(j % 2)).then_inc(sem("z_done"), 1)
            k = 0
            for src in (V, RV):
                for t in range(6):
                    n = P if t < 4 else (NS, TAIL)[t - 4]
                    dst = ((vt, vs, vtl) if src == V else (vr, vrs, vrt))
                    o = dst[0][:, t, :] if t < 4 else dst[t - 3][0:n, :]
                    act.wait_ge(sem("tr_full"), k + 1)
                    ev(o, ps[0:n, k % 4, :]).then_inc(sem("tr_done"), 1)
                    k += 1

            def gate(j, p):
                act.wait_ge(sem("g_full"), j + 1)
                ev(halves(z[:, G + j, :]), pair(p), ACT.Silu).then_inc(sem("sg_done"), 1)

            gate(0, 3)
            gate(1, 0)
            gate(2, 3)
            for b in range(NB):
                act.wait_ge(sem("sub_done"), b + 1)
                ev(lgt[:, b, :], lgt[:, b, :], ACT.Exp).then_inc(sem("sp_done"), 1)
            gate(3, 3)
            for cn in range(6):
                n = P if cn < 4 else (TAIL, NS)[cn - 4]
                act.wait_ge(sem("bag_done"), cn + 1)
                ev(rsd[0:n, :], bag[0:n, 1::2], ACT.Sqrt, bias=c("eps")[0:n, :]).then_inc(sem("rsd_done"), 1)
                if cn == 4:
                    act.wait_ge(sem("so_full"), 1)
                    ev(lg[:, 0:512], ps[:, 5, :]).then_inc(sem("so_out"), 1)
            units = [(hd, t) for hd in range(AH) for t in range(5)]

            def probs(u, hd, t):
                p, n, w = u % 2, (P if t < 4 else TAIL), (128 * (t + 1) if t < 4 else 528)
                act.wait_ge(sem("nmx_done"), u + 1)
                ev(l_b[u % 3][0:n, 0:w], l_b[u % 3][0:n, 0:w], ACT.Exp, bias=nmx[0:n, p:p + 1],
                   accum_out=ssum[0:n, p:p + 1]).then_inc(sem("ae_done"), 1)

            def turned(u, hd, t):
                p, n = u % 2, (P if t < 4 else TAIL)
                act.wait_ge(sem("at_full"), u + 1)
                if u >= 2:
                    act.wait_ge(sem("ao_full"), u - 1)
                w = (t + 1 if t < 4 else 4) * n
                last = ev(pt_b[:, p, 0:w], ps[:, 4 + p, 0:w])
                if t == 4:
                    last = ev(pt_b[0:TAIL, p, 4 * n:5 * n], ps[0:TAIL, 4 + p, 4 * n:5 * n])
                last.then_inc(sem("apt_done"), 1)

            def out(u, hd, t):
                p, n, lo, q0 = u % 2, (P if t < 4 else TAIL), 64 * (hd % 2), (128 * t if t < 4 else TL)
                act.wait_ge(sem("ao_full"), u + 1)
                ev(mix[lo:lo + 64, hd // 2, q0:q0 + n], ps[lo:lo + 64, 6 + p, 0:n]).then_inc(sem("ao_done"), 1)

            for u in range(len(units) + 2):
                if u < len(units):
                    probs(u, *units[u])
                if 1 <= u <= len(units):
                    turned(u - 1, *units[u - 1])
                if u >= 2:
                    out(u - 2, *units[u - 2])
            w_in_t = [Tally(sem(f"w_in{s}"), 16 * seen[1][s]) for s in range(4)]
            norm(1)
            act.wait_ge(sem("kvi_out"), 48)
            ffn(1)

        @block.vector
        def _(dve):
            v = nc.vector
            own = Tally(sem("dve_own"))

            def seq(ins):
                ins.then_inc(own.sem, 1)
                dve.wait_ge(own.sem, own.up())

            dve.sem_inc(sem("h_done"), 2)
            dve.sem_inc(sem("r_done"), 2)
            seq(v.memset(qibd[:, :], 0.0))
            seq(v.memset(qbd[:, :], 0.0))

            def row(ap, i):
                return ap[:, bass.ds(i, 1), :].rearrange("p a n -> p (a n)")

            wh_done = Tally(sem("wh_done"))

            def weight_low(s, to, n=1024):
                dve.wait_ge(wh_done.sem, wh_done.up())
                v.tensor_tensor(wl[:, to, 0:n], w4[:, s, 0:n], wh[:, to, 0:n].bitcast(F32), ALU.subtract) \
                    .then_inc(sem("wl_done"), 1)

            def x_lows():
                for k in range(KT):
                    dve.wait_ge(sem("xh_done"), k + 1)
                    v.tensor_tensor(xl[:, k, :], x[:, k, :], xh[:, k, :].bitcast(F32), ALU.subtract) \
                        .then_inc(sem("xl_done"), 1)

            def ffn(m):
                if m == 0:
                    weight_low(0, 0)
                    x_lows()
                    weight_low(1, 1)
                sd, hd = Tally(sem("s_done"), FT * m), Tally(sem("hh_done"), FT * m)

                def hidden(f, j, down=False):
                    for up in range(2):
                        weight_low(up if down else 2 * (1 - j) + up, up)
                    dve.wait_ge(sd.sem, sd.up())
                    v.tensor_tensor(halves(s_buf[:, j, :]), halves(s_buf[:, j, :]), pair(2 + j), ALU.mult) \
                        .then_inc(sem("h_done"), 1)
                    dve.wait_ge(hd.sem, hd.up())
                    v.tensor_tensor(row(hl, f), s_buf[:, j, :], row(hh, f).bitcast(F32), ALU.subtract) \
                        .then_inc(sem("hl_done"), 1)

                def output(d, j, more=True):
                    for s in range(3):
                        if more or s == 0:
                            nxt = (s + 2) % 3
                            weight_low(nxt, (j + s) % 2, DOWN[nxt])
                    if more:
                        dve.wait_ge(yd.sem, yd.up())
                        v.scalar_tensor_tensor(row(rs[2 * m], d), row(x, d), ALPHA, s_buf[:, j, :],
                                               ALU.mult, ALU.add).then_inc(sem("r_done"), 1)
                    else:
                        for a in range(2):
                            dve.wait_ge(yd.sem, yd.up())
                            v.scalar_tensor_tensor(rs[2 * m][:, d, cols(a)], x[:, d, cols(a)], ALPHA,
                                                   s_buf[:, j, cols(a)], ALU.mult, ALU.add).then_inc(sem("r_done"), 1)

                with loop(dve, FT // 2 - 1, [(sd, 2), (wh_done, 4), (hd, 2)]) as i:
                    hidden(i * 2, 0)
                    hidden(i * 2 + 1, 1)
                hidden(FT - 2, 0)
                hidden(FT - 1, 1, True)
                yd = Tally(sem("y_done"), (KT + 1) * m)
                with loop(dve, KT // 2 - 1, [(yd, 2), (wh_done, 6)]) as i:
                    output(i * 2, 0)
                    output(i * 2 + 1, 1)
                output(KT - 2, 0)
                output(KT - 1, 1, False)
                norm(2 * m)

            def norm(n):
                r = rs[n]
                if n == 0:
                    dve.wait_ge(sem("cst_in"), 16)
                for a in range(2):
                    dve.wait_ge(sem(f"mean_full{a}"), n + 1)
                    for d in range(KT):
                        v.tensor_tensor(r[:, d, cols(a)], r[:, d, cols(a)], ps[:, 4 + a, 0:HALF], ALU.subtract) \
                            .then_inc(sem(f"c_done{a}"), 1)
                if n == 1:
                    dve.wait_ge(sem("rp_out"), 16)
                    weight_low(0, 0)
                    weight_low(1, 1)
                for a in range(2):
                    dve.wait_ge(sem(f"std_done{a}"), n + 1)
                    dve.wait_ge(sem(f"c_done{a}"), KT * (n + 1))
                    seq(v.reciprocal(rstd[:, cols(a)], rstd[:, cols(a)]))
                    for d in range(KT):
                        v.tensor_tensor(r[:, d, cols(a)], r[:, d, cols(a)], rstd[:, cols(a)], ALU.mult) \
                            .then_inc(sem(f"n_done{a}"), 1)

            ffn(0)
            dve.wait_ge(sem("z_done"), 4)
            for b2 in range(2):
                for par in range(2):
                    o = qib[64 * b2:64 * b2 + 64, :, 32 * b2:32 * b2 + 32] \
                        .rearrange("p r (a two q) -> p r a two q", two=2, q=NQ)
                    s_ = z[64 * par:64 * par + 64, QI:QI + 4, SMP:TL].rearrange("p a (r two q) -> p r a two q", two=2, q=NQ)
                    for a in range(4):
                        last = v.tensor_copy(o[:, :, a, par, :], s_[:, :, a, b2, :])
            last.then_inc(sem("qib_done"), 1)
            def new_keys(pr):
                for b2 in range(2):
                    lo = 64 * b2
                    c0 = SMP + (2 * pr + b2) * NQ
                    last = v.tensor_copy(kis[pr // 2][lo:lo + 64, pr % 2, PAST:KEYS], kid[lo:lo + 64, c0:c0 + NQ])
                last.then_inc(sem("kin_done"), 1)

            dve.wait_ge(sem("kid_done"), 2)
            for pr in range(4):
                new_keys(pr)
            def pair_queries():
                dve.wait_ge(sem("z_done"), FIRST)
                for h2 in range(2):
                    lo = 64 * h2
                    last = v.tensor_copy(qb[lo:lo + 64, :, :, 4 * h2:4 * h2 + 4],
                                         z[lo:lo + 64, Q:Q + 4, SMP:TL].rearrange("p a (b q) -> p a b q", q=NQ))
                last.then_inc(sem("qb_done"), 1)

            dve.wait_ge(sem("prep_full"), 1)
            for g in range(2):
                last = v.tensor_tensor(ws[:, g, :], ps[:, 7, 0:NS], c("maskg")[:, g * NS:(g + 1) * NS], ALU.mult)
            last.then_inc(sem("wsel_done"), 1)
            dve.wait_ge(sem("wi_done"), 1)
            dve.wait_ge(sem("acc_in"), 16)
            u = 0
            for t in (1, 2, 3, 4):
                n, w = (P, 128 * (t + 1)) if t < 4 else (TAIL, 528)
                for hd in range(AH):
                    dve.wait_ge(sem("rel_done"), u + 1)
                    if hd:
                        dve.wait_ge(sem("acc_done"), u)
                    v.scalar_tensor_tensor(acc_ap(t), rel[0:n, u % 2, 0:w], wi[0:n, t, hd:hd + 1], acc_ap(t),
                                           ALU.mult, ALU.add).then_inc(sem("acc_done"), 1)
                    u += 1
            pair_queries()
            for ch in range(NCH):
                dve.wait_ge(sem("sw_full"), NCH + ch + 1)
                dve.wait_ge(sem("sw_g0"), ch + 1)
                o = sc[0:NS, ch * CH:(ch + 1) * CH]
                v.tensor_tensor(o, o, ps[0:NS, 6 + ch % 2, 0:CH], ALU.add).then_inc(sem("sw_g1"), 1)
            dve.wait_ge(sem("sw_g1"), NCH)
            o = sc[0:NS, PAST:KEYS]
            seq(v.tensor_tensor(o, o, c("tri4")[0:NS, :], ALU.add))
            dve.wait_ge(sem("acc_done"), u)
            with loop(dve, TOPK_P // 8, [(own, 8)]):
                for t in (1, 2, 3, 4):
                    n = P if t < 4 else TAIL
                    v.max(m8[0:n, 8 * (t - 1):8 * t], acc_ap(t)).then_inc(own.sem, 1)
                dve.wait_ge(own.sem, own.up(4))
                dve.sem_inc(sem("rounds"), 1)
                for t in (1, 2, 3, 4):
                    n = P if t < 4 else TAIL
                    v.match_replace(acc_ap(t), m8[0:n, 8 * (t - 1):8 * t], acc_ap(t), TAKEN).then_inc(own.sem, 1)
                dve.wait_ge(own.sem, own.up(4))
                dve.sem_inc(sem("rounds"), 1)
            for t in (1, 2, 3, 4):
                v.tensor_scalar(acc_ap(t), acc_ap(t), TAKEN / 2, NEVER, ALU.is_gt, ALU.mult).then_inc(own.sem, 1)
            dve.wait_ge(own.sem, own.up(4))
            with loop(dve, TOPK_S // 8, [(own, 2)]):
                seq(v.max(m8[0:NS, 0:8], sc[0:NS, :]))
                dve.sem_inc(sem("rounds"), 1)
                seq(v.match_replace(sc[0:NS, :], m8[0:NS, 0:8], sc[0:NS, :], TAKEN))
                dve.sem_inc(sem("rounds"), 1)
            seq(v.tensor_scalar(sc[0:NS, :], sc[0:NS, :], TAKEN / 2, NEVER, ALU.is_gt, ALU.mult))
            v.tensor_tensor(cmp16[0:NS, :].rearrange("p (b j) -> p b j", j=NQ),
                            sc[0:NS, PAST:KEYS].unsqueeze(1).broadcast_to([NS, NB, NQ]),
                            c("own")[0:NS, :].rearrange("p (b j) -> p b j", j=NQ), ALU.add) \
                .then_inc(sem("smask_done"), 1)
            dve.wait_ge(sem("masks_full"), 1)
            seq(v.tensor_copy(mask_t[:, 0:512], ps[:, 4, :]))
            v.tensor_copy(mask_t[0:NS, 512:544], ps[0:NS, 5, 0:NS]).then_inc(sem("masks_read"), 1)
            dve.wait_ge(sem("masks_read"), 1)
            dve.wait_ge(sem("rope_in"), 16)
            for u in range(8):
                dve.wait_ge(sem("rot_full"), u + 1)
                if u:
                    dve.wait_ge(sem("rope_done"), u)
                v.tensor_tensor(halves(zs), pair(u % 2), halves(sin_t), ALU.mult).then_inc(sem("zs_done"), 1)
                dve.wait_ge(sem("zs_done"), u + 1)
                dve.wait_ge(sem("zc_done"), u + 1)
                v.tensor_tensor(z[:, RQ + u, :], zc[:, u % 2, :], zs, ALU.add).then_inc(sem("rope_done"), 1)
            dve.wait_ge(sem("lg_done"), NB + 1)
            dve.wait_ge(sem("p16_done"), 1)
            for b in range(NB):
                o = lgt[:, b, 0:512].rearrange("p (g h q) -> p g h q", g=NPAGE, q=NQ)
                m = mask_t[:, 0:512].rearrange("p (g n) -> p g n", g=NPAGE)[:, :, b * NQ:(b + 1) * NQ]
                v.tensor_tensor(o, o, m.unsqueeze(2).broadcast_to([P, NPAGE, AH, NQ]), ALU.add)
            o = lgt[0:NS, :, 512:544].rearrange("p b (h q) -> p b h q", q=NQ)
            m = mask_t[0:NS, 512:544].rearrange("p (b q) -> p b q", q=NQ)
            v.tensor_tensor(o, o, m.unsqueeze(2).broadcast_to([NS, NB, AH, NQ]), ALU.add).then_inc(sem("mask_used"), 1)
            dve.wait_ge(sem("mask_used"), 1)

            def over_pages(func, b):
                return func(mx[:, b * 32:(b + 1) * 32], lgt[:, b, :].rearrange("p (g n) -> p n g", n=32), axis=AX.X)

            for b in range(NB):
                last = over_pages(v.reduce_max, b)
            last.then_inc(sem("mx_done"), 1)
            dve.wait_ge(sem("mxt_full"), 1)
            seq(v.reduce_max(mx2[:, :], ps[:, 5, 0:256].rearrange("p (g n) -> p g n", g=2), axis=AX.X))
            for g in range(2):
                last = v.tensor_scalar(diag[:, g * P:(g + 1) * P], ident, mx2[:, g:g + 1], None, ALU.mult)
            last.then_inc(sem("diag_done"), 1)
            dve.wait_ge(sem("mxb_full"), 1)
            for b in range(NB):
                o = lgt[:, b, :].rearrange("p (g n) -> p g n", n=32)
                m = ps[:, 4, b * 32:(b + 1) * 32].unsqueeze(1).broadcast_to([P, NPAGE + 1, 32])
                v.tensor_tensor(o, o, m, ALU.subtract).then_inc(sem("sub_done"), 1)
            for b in range(NB):
                dve.wait_ge(sem("sp_done"), b + 1)
                last = over_pages(v.reduce_sum, b)
            last.then_inc(sem("psum_done"), 1)
            dve.wait_ge(sem("sum_full"), 1)
            v.reciprocal(rsum, ps[:, 5, 0:2]).then_inc(sem("rsum_done"), 1)

            def h4(ap, n):
                return ap.rearrange("p (h m) -> p h m", h=RH)[:, :, 0:n]

            def ret_scale(cn, t0, n, dec_, xi_, zeta_):
                dve.wait_ge(sem("inner_full"), cn + 1)
                v.tensor_tensor(h4(it_b[0:n, :], n), h4(ps[0:n, 0, :], n), dec_, ALU.mult).then_inc(sem("it_done"), 1)
                v.tensor_tensor(xi_[0], z[:, RQ:RQ + 4, t0:t0 + n], xi_[1], ALU.mult).then_inc(sem("qx_done"), 1)
                dve.wait_ge(sem("kt_full"), cn + 1)
                v.tensor_tensor(h4(kz_b[0:n, :], P), h4(ps[0:n, 1, :], P), zeta_.unsqueeze(2).broadcast_to([n, RH, P]),
                                ALU.mult).then_inc(sem("kz_done"), 1)

            def group_norm(cn, n, o_ps):
                for hd in range(RH):
                    v.bn_stats(bn[0:n, 6 * hd:6 * hd + 6], o_ps(hd)).then_inc(own.sem, 1)
                dve.wait_ge(own.sem, own.up(4))
                for hd in range(RH):
                    last = v.bn_aggr(bag[0:n, 2 * hd:2 * hd + 2], bn[0:n, 6 * hd:6 * hd + 6])
                last.then_inc(sem("bag_done"), 1)
                dve.wait_ge(sem("bag_done"), cn + 1)
                dve.wait_ge(sem("rsd_done"), cn + 1)
                seq(v.reciprocal(rsd[0:n, :], rsd[0:n, :]))
                for hd in range(RH):
                    last = v.tensor_scalar(rn_b[0:n, hd * P:(hd + 1) * P], o_ps(hd), bag[0:n, 2 * hd:2 * hd + 1],
                                           rsd[0:n, hd:hd + 1], ALU.subtract, ALU.mult)
                last.then_inc(sem("rn_done"), 1)

            def gated(cn, t0, n, bank):
                dve.wait_ge(sem("rt_full"), cn + 1)
                v.tensor_tensor(mix[:, 4:8, t0:t0 + n], h4(ps[:, bank, :], n), z[:, G:G + 4, t0:t0 + n], ALU.mult) \
                    .then_inc(sem("mixr_done"), 1)

            dve.wait_ge(sem("ret_in"), 16)
            dve.wait_ge(sem("sg_done"), 4)
            dve.wait_ge(sem("rope_done"), 8)
            gam = c("gam")
            for cn in range(5):
                t0, n = (128 * cn, P) if cn < 4 else (TL, TAIL)
                ret_scale(cn, t0, n, h4(dec[0:n, :], n), (h4(qx_b, n), h4(xi, n)),
                          c("zeta") if cn < 4 else c("zetat")[0:n, :])
                dve.wait_ge(sem("rst_full"), cn + 1)
                if cn == 0:
                    v.tensor_copy(sr, ps[:, 3, :]).then_inc(sem("sr_done"), 1)
                else:
                    gg = gam[:, 0:4] if cn < 4 else gam[:, 4:8]
                    dve.wait_ge(sem("sr_done"), cn)
                    dve.wait_ge(sem("ro_full"), cn + 1)
                    seq(v.tensor_tensor(h4(sr, P), h4(sr, P), gg.unsqueeze(2).broadcast_to([P, RH, P]), ALU.mult))
                    v.tensor_tensor(sr, sr, ps[:, 3, :], ALU.add).then_inc(sem("sr_done"), 1)
                dve.wait_ge(sem("ro_full"), cn + 1)
                group_norm(cn, n, lambda hd: ps[0:n, 2, hd * P:(hd + 1) * P])
                gated(cn, t0, n, 4)
            qs = qx_b[:, 0:128].rearrange("p (h m) -> p h m", h=RH)
            ret_scale(5, SMP, NS, c("decs")[0:NS, :].rearrange("p (h m) -> p h m", h=RH),
                      (qs, c("xis").rearrange("p (h m) -> p h m", h=RH)), c("zetas")[0:NS, :])
            dve.wait_ge(sem("qx_done"), 6)
            dve.wait_ge(sem("kz_done"), 6)
            blk = c("blkrow").rearrange("p (b m) -> p b m", b=NB)

            def batch_parts(b):
                if b >= 2:
                    dve.wait_ge(sem("cross_full"), b - 1)
                v.tensor_tensor(qx_b[:, 256 + 128 * (b % 2):384 + 128 * (b % 2)].rearrange("p (h m) -> p h m", h=RH), qs,
                                blk[:, b, :].unsqueeze(1).broadcast_to([P, RH, NS]), ALU.mult).then_inc(sem("qxb_done"), 1)
                if b >= 2:
                    dve.wait_ge(sem("dst_full"), b - 1)
                o = rn_b[0:NS, :] if b % 2 else l_b[0][0:NS, 0:512]
                v.tensor_scalar(o, kz_b[0:NS, :], c("blkcol")[0:NS, b:b + 1], None, ALU.mult).then_inc(sem("kzb_done"), 1)

            batch_parts(0)
            for b in range(NB):
                if b + 1 < NB:
                    batch_parts(b + 1)
                dve.wait_ge(sem("cross_full"), b + 1)
                o = st[:, b % 3, :]
                seq(v.tensor_tensor(h4(o, P), h4(o, P), gam[:, 8:12].unsqueeze(2).broadcast_to([P, RH, P]), ALU.mult))
                dve.wait_ge(sem("dst_full"), b + 1)
                v.tensor_tensor(o, o, ps[:, 2 - b % 2, :], ALU.add).then_inc(sem("st_new"), 1)
            group_norm(5, NS, lambda hd: ps[0:NS, 4 + hd, 0:P])
            gated(5, SMP, NS, 0)

            units = [(hd, t) for hd in range(AH) for t in range(5)]

            def logits(u, hd, t):
                p, n, w = u % 2, (P if t < 4 else TAIL), (128 * (t + 1) if t < 4 else 528)
                dve.wait_ge(sem("as_full"), u + 1)
                if u >= 3:
                    dve.wait_ge(sem("at_full"), u - 2)
                m = c("tri") if t == 0 else acc_ap(t)
                w0 = min(w, 512)
                last = v.scalar_tensor_tensor(l_b[u % 3][0:n, 0:w0], ps[0:n, p, 0:w0], AD ** -0.5, m[:, 0:w0],
                                              ALU.mult, ALU.add)
                if t == 4:
                    last = v.scalar_tensor_tensor(l_b[u % 3][0:n, 512:528], ps[0:n, 2, 0:TAIL], AD ** -0.5,
                                                  m[:, 512:528], ALU.mult, ALU.add)
                last.then_inc(sem("al_done"), 1)
                dve.wait_ge(sem("al_done"), u + 1)
                seq(v.reduce_max(smx[0:n, p:p + 1], l_b[u % 3][0:n, 0:w], axis=AX.X))
                v.tensor_scalar(nmx[0:n, p:p + 1], smx[0:n, p:p + 1], -1.0, None, ALU.mult).then_inc(sem("nmx_done"), 1)

            def scaled(u, hd, t):
                p, n, w = u % 2, (P if t < 4 else TAIL), (128 * (t + 1) if t < 4 else 528)
                dve.wait_ge(sem("ae_done"), u + 1)
                seq(v.reciprocal(rcp[0:n, p:p + 1], ssum[0:n, p:p + 1]))
                v.tensor_scalar(l_b[u % 3][0:n, 0:w], l_b[u % 3][0:n, 0:w], rcp[0:n, p:p + 1], None, ALU.mult) \
                    .then_inc(sem("ap_done"), 1)

            def sample_out(g):
                dve.wait_ge(sem("so_full" if g else "so_out"), g + 1)
                rows, att = rn_b.rearrange("p (h d) -> p h d", h=AH), kz_b[:, 64 * g:64 * g + 64]
                v.scalar_tensor_tensor(rows, (ps[:, 3, :] if g else lg[:, 0:512]).rearrange("p (h d) -> p h d", h=AH), rsum[:, g:g + 1],
                                       c("hsel").unsqueeze(2).broadcast_to([P, AH, AD]), ALU.mult, ALU.mult) \
                    .then_inc(own.sem, 1)
                dve.wait_ge(own.sem, own.up())
                v.reduce_sum(att, rn_b.rearrange("p (h d) -> p d h", h=AH), axis=AX.X).then_inc(sem("so_att"), 1)
                dve.wait_ge(sem("so_att"), g + 1)
                dve.wait_ge(sem("so_turned"), g + 1)
                t = ps[0:64, 5 if g else 2, 0:P].rearrange("p (b a two q) -> p a b two q", b=4, two=2, q=NQ)
                for h2 in range(2):
                    lo = 64 * h2
                    o = mix[lo:lo + 64, 0:4, SMP + g * 16:SMP + (g + 1) * 16].rearrange("p a (b q) -> p a b q", q=NQ)
                    v.tensor_copy(o, t[:, :, :, h2, :]).then_inc(sem("so_done"), 1)

            dve.wait_ge(sem("rsum_done"), 1)
            for u in range(len(units) + 1):
                if u < len(units):
                    logits(u, *units[u])
                if u >= 1:
                    scaled(u - 1, *units[u - 1])
                if u == len(units) // 2:
                    sample_out(0)
            sample_out(1)
            for d in range(KT):
                dve.wait_ge(sem(f"w_free{d % 4}"), OUT_W[d % 4] + d // 4 + 1)
                if d < KT - 1:
                    v.scalar_tensor_tensor(halves(rs[1][:, d, :]), halves(x[:, d, :]), ALPHA, pair(d % 2),
                                           ALU.mult, ALU.add).then_inc(sem("r_done"), 1)
                else:
                    for a in range(2):
                        v.scalar_tensor_tensor(rs[1][:, d, cols(a)], x[:, d, cols(a)], ALPHA,
                                               ps[:, 2 * (d % 2) + a, 0:HALF], ALU.mult, ALU.add) \
                            .then_inc(sem("r_done"), 1)
            norm(1)
            dve.wait_ge(sem("kvi_out"), 48)
            for s in range(3):
                dve.wait_ge(sem(f"st_out{s}"), 16 * ((NB - s + 2) // 3))
            ffn(1)

        @block.gpsimd
        def _(pool):
            sums = Tally(sem("sum_done"))

            def norm(n):
                r = rs[n]
                for d in range(1, KT - 1):
                    pool.wait_ge(sem("r_done"), 2 + (KT + 1) * n + d + 1)
                    if d > 1:
                        pool.wait_ge(sums.sem, sums.n)
                    pool.tensor_tensor(rsum_t, r[:, 0, :] if d == 1 else rsum_t, r[:, d, :], ALU.add) \
                        .then_inc(sums.sem, 1)
                    sums.up()
                for d in range(KT):
                    pool.wait_ge(sem("c_done1"), KT * n + d + 1)
                    pool.wait_ge(sem("sq_free1"), KT * n + d + 1)
                    pool.tensor_tensor(squares(n, 1, d), r[:, d, cols(1)], r[:, d, cols(1)], ALU.mult) \
                        .then_inc(sem("sq_done1"), 1)

            pool.wait_ge(sem("pages_in"), 16)
            pool.wait_ge(sem("h_done"), 2 + FT)
            index_pages(pool, 0)
            index_pages(pool, 1)
            norm(0)
            index_pages(pool, 2)
            pool.wait_ge(sem("sw_g1"), NCH)
            pool.memset(lgt[:, :, 512:544], NEVER).then_inc(sem("lg_init"), 1)
            pool.sem_inc(sem("index_done"), 1)
            pool.wait_ge(sem("w_free2"), FF_W[2])
            for s in range(3):
                pool.dma_start(st[:, s, :], state[s]).then_inc(sem(f"st_in{s}"), 16)
            pool.wait_ge(sem("rope_in"), 16)
            pool.wait_ge(sem("z_done"), RV)
            for u in range(8):
                if u >= 2:
                    pool.wait_ge(sem("rope_done"), u - 1)
                pool.tensor_tensor(zc[:, u % 2, :], z[:, RQ + u, :], cos_t, ALU.mult).then_inc(sem("zc_done"), 1)
            pool.wait_ge(sem("masks_read"), 1)
            pool.dma_start(sc[:, 0:1024], ret_tab).then_inc(sem("ret_in"), 16)
            pool.wait_ge(sem("sr_done"), 5)
            pool.dma_start(rp_o, sr).then_inc(sem("rp_out"), 16)
            for b in range(NB):
                pool.wait_ge(sem("st_new"), b + 1)
                pool.dma_start(rs_o[b], st[:, b % 3, :]).then_inc(sem(f"st_out{b % 3}"), 16)
                if b + 3 < NB:
                    pool.wait_ge(sem(f"st_out{b % 3}"), 16 * (b // 3 + 1))
                    pool.dma_start(st[:, b % 3, :], state[b + 3]).then_inc(sem(f"st_in{b % 3}"), 16)
            norm(1)
            for a in range(2):
                for k in range(KT):
                    pool.wait_ge(sem(f"x_done{a}"), KT + k + 1)
                    pool.tensor_tensor(xl[:, k, cols(a)], x[:, k, cols(a)], xh[:, k, cols(a)].bitcast(F32), ALU.subtract) \
                        .then_inc(sem("xl_done"), 1)
            norm(2)


OUT_W = [FF_W[0] + 3 + NB + 1, FF_W[1] + 2 + NB + 1, FF_W[2] + 2 + 1, FF_W[3] + 2 + 1]


def _tables():
    f = np.float32
    cs = np.zeros((P, CONST_W), f)

    def put(name, a, rows=slice(None)):
        at, w = CONSTS[name]
        cs[rows, at:at + w] = a

    put("ident", np.eye(P))
    put("mean", 1.0 / D)
    put("ones", 1.0)
    rot = np.zeros((P, P), f)
    for m in range(64):
        rot[m + 64, m] = -1.0
        rot[m, m + 64] = 1.0
    put("rot", rot)
    n = np.arange(P)
    put("tri", np.where(n[None, :] <= n[:, None], 0.0, NEVER))
    sel = np.zeros((P, P), f)
    row = np.arange(P)
    sel[64 + (row // NQ) % AH, row] = 1.0
    put("sel", sel)
    mg = np.zeros((P, 2, NS), f)
    for g in range(2):
        mg[row, g, (4 * g + row // 32) * NQ + row % NQ] = AH ** -0.5
    put("maskg", mg.reshape(P, -1))
    own = np.arange(NS) // NQ
    put("blkrow", np.broadcast_to((own[None, :] == np.arange(NB)[:, None]).astype(f)[None], (P, NB, NS)).reshape(P, -1))
    lg = np.log(f(1.0) - f(2.0) ** (f(-5.0) - np.arange(RH, dtype=f))).astype(f).astype(np.float64)
    sc = P ** -0.5
    j = np.arange(NS) % NQ
    dj = j[None, :] - j[:, None]
    same = (own[:, None] == own[None, :]) & (dj >= 0)
    put("decs", np.stack([np.where(same, np.exp(dj * l) * sc, 0) for l in lg], 1).reshape(NS, -1), slice(0, NS))
    put("xis", np.broadcast_to(np.stack([np.exp((j + 1) * l) for l in lg]).reshape(1, -1), (P, RH * NS)))
    put("own", np.where(own[:, None] == own[None, :], 0.0, NEVER), slice(0, NS))
    put("tri4", np.where(np.arange(NQ)[None, :] <= j[:, None], 0.0, NEVER), slice(0, NS))
    put("zeta", np.exp((P - 1 - n)[:, None] * lg[None]) * sc)
    put("zetat", np.exp((TAIL - 1 - np.arange(TAIL))[:, None] * lg[None]) * sc, slice(0, TAIL))
    put("zetas", np.exp((NQ - 1 - j)[:, None] * lg[None]) * sc, slice(0, NS))
    put("gam", np.concatenate([np.exp(L * lg) for L in (P, TAIL, NQ)])[None])
    put("blkcol", (own[:, None] == np.arange(NB)[None]).astype(f), slice(0, NS))
    put("eps", EPS)
    put("hsel", ((row // NQ % AH)[:, None] == np.arange(AH)[None]).astype(f))
    pos = np.concatenate([np.arange(512), PAST + np.arange(NS) % NQ, 512 + np.arange(TAIL)]).astype(f)
    inv = (f(10000.0) ** (-np.arange(64, dtype=f) / f(64))).astype(f)
    ang = (pos[None, :] * inv[:, None]).astype(f)
    ang = np.concatenate([ang, ang])
    rope = np.concatenate([np.cos(ang), np.sin(ang)], 1).astype(f)
    d = n[None, :] - n[:, None]
    dec = np.stack([np.where(d >= 0, np.exp(np.maximum(d, 0) * l) * sc, 0) for l in lg], 1).reshape(P, -1)
    xi = np.broadcast_to(np.stack([np.exp((n + 1) * l) for l in lg]).reshape(1, -1), (P, RH * P))
    ret = np.concatenate([dec, xi], 1).astype(f)
    a0 = np.zeros((P, ACC_W), f)
    for t in (1, 2, 3):
        a0[:, ACC_AT[t] + 128 * t:ACC_AT[t] + 128 * (t + 1)] = np.where(n[None, :] <= n[:, None], 0.0, NEVER)
    a0[0:TAIL, ACC_AT[4] + 512:ACC_AT[4] + 528] = np.where(n[None, :TAIL] <= n[:TAIL, None], 0.0, NEVER)
    return cs, rope, ret, a0


def kernel(**inputs):
    import concourse.bacc as _bacc
    from concourse.bass_utils import run_bass_kernel_spmd as _run

    a = {k: np.asarray(v) for k, v in inputs.items()}

    def cols(xp, xs):
        return np.concatenate([xp[0:512], xs.reshape(NS, -1), xp[512:]], 0)

    def tiled(w):
        kk, nn = w.shape
        return w.reshape(kk // P, P, nn // P, P).transpose(2, 1, 0, 3).reshape(nn // P, P, kk)

    xt = cols(np.concatenate([a["meta_tokens"], a["x_prompt"][0]], 0), a["x_sample"])
    xt = xt.T.reshape(KT, P, T).transpose(1, 0, 2).reshape(P, KT * T)
    w = a["w_in"][0]
    o = np.cumsum([0, 512, 512, 512, 512, 64, 8, 512, 512, 512, 512])
    part = [w[:, o[i]:o[i + 1]] for i in range(10)]
    wp = np.concatenate([part[3], part[4], part[5], np.zeros((D, 56), w.dtype), part[0], part[1], part[2],
                         part[6], part[7], part[8], part[9]], 1)
    pool = a["cache_k"].shape[1]
    cs, rope, ret, a0 = _tables()
    at = CONSTS["ln"][0]
    ln = np.stack([a[f"ln{i}_{s}"][0].reshape(KT, P).T for i in (1, 2, 3) for s in "gb"], 1).reshape(P, 48)
    cs = np.concatenate([cs[:, :at], ln, cs[:, at + 48:]], 1)
    ins = dict(
        x_t=xt, wg1=tiled(a["ffn1_w_gate"][0]), wu1=tiled(a["ffn1_w_up"][0]), wd1=tiled(a["ffn1_w_down"][0]),
        wg2=tiled(a["ffn2_w_gate"][0]), wu2=tiled(a["ffn2_w_up"][0]), wd2=tiled(a["ffn2_w_down"][0]),
        w_in=tiled(wp), w_out=tiled(a["w_out"][0]),
        k_pool=a["cache_k"][0].reshape(pool, PAGE, 4, P).transpose(0, 3, 2, 1).reshape(pool, P, 512),
        v_pool=a["cache_v"][0].reshape(pool, PAGE, 512), i_pool=a["cache_idx_k"][0].transpose(0, 2, 1),
        state=a["state_ret"][0].transpose(0, 2, 1, 3).reshape(NB, P, 512),
        pages=a["page_table"].reshape(1, -1), consts=cs, rope_tab=rope, ret_tab=ret, acc_tab=a0)
    outs = dict(y_o=(KT, P, T), k_o=(P, 4, T), v_o=(P, 4, T), i_o=(64, T), rp_o=(P, 512), rs_o=(NB, P, 512))
    nc = _bacc.Bacc("TRN2", target_bir_lowering=False, num_devices=1)
    arrays, args = {}, {}
    for name, v in ins.items():
        v = np.ascontiguousarray(v)
        arrays["in_" + name] = v
        args[name] = nc.dram_tensor("in_" + name, v.shape, mybir.dt.from_np(v.dtype), kind="ExternalInput").ap()
    for name, shape in outs.items():
        args[name] = nc.dram_tensor("out_" + name, shape, F32, kind="ExternalOutput").ap()
    build(nc, **args)
    r = _run(nc, [arrays], core_ids=[0]).results[0]
    r = {k: r["out_" + k] for k in outs}

    def split(t):
        return np.concatenate([t[0:512], t[TL:T]], 0), t[SMP:TL]

    yp, ys = split(r["y_o"].reshape(D, T).T)
    kp, ks = split(r["k_o"].transpose(1, 0, 2).reshape(512, T).T)
    vp, vs_ = split(r["v_o"].transpose(1, 0, 2).reshape(512, T).T)
    ip, is_ = split(r["i_o"].T)
    L = SEQ + META
    res = (yp[META:].reshape(1, SEQ, D), ys.reshape(NB, NQ, D),
           kp.reshape(1, 1, L, AH, AD), vp.reshape(1, 1, L, AH, AD), ip.reshape(1, 1, L, AD),
           r["rp_o"].reshape(P, RH, P).transpose(1, 0, 2).reshape(1, 1, RH, P, P),
           ks.reshape(1, NB, NQ, AH, AD), vs_.reshape(1, NB, NQ, AH, AD), is_.reshape(1, NB, NQ, AD),
           r["rs_o"].reshape(NB, P, RH, P).transpose(0, 2, 1, 3).reshape(1, NB, RH, P, P))
    return tuple(np.ascontiguousarray(t) for t in res)
```
